# Optimizing a Trainium2 kernel written in Bass

```python
import math
import jax, jax.numpy as jnp
from jax import lax
import numpy as np

D_MODEL = 1024
BATCH = 1
SEQ = 256
DEPTH = 2

NORM_EPS = 1e-6
GLA_HEADS = 4
GLA_DV = D_MODEL // 8
GLA_DK = GLA_DV // 2
GLA_LOWRANK = 16
GLA_TAU = 16.0
GLA_CHUNK = 64
NSA_HEADS = 8
NSA_KV_GROUPS = 2
NSA_HEAD_DIM = D_MODEL // 16
CMP_BLOCK = 32
CMP_STRIDE = 16
CMP_HIDDEN = 4 * NSA_HEAD_DIM
SEL_BLOCK = 64
N_SELECT = 8
WINDOW = 512
Q_BLOCK = 128
D_INNER = 2 * D_MODEL
SSM_HEAD_DIM = 64
SSM_HEADS = D_INNER // SSM_HEAD_DIM
SSM_GROUPS = 4
SSM_STATE = 128
CONV_K = 4
SSM_CHUNK = 64
CONV_CH = D_INNER + 2 * SSM_GROUPS * SSM_STATE
FFN_DENSE = ((8 * D_MODEL // 3 + 127) // 128) * 128
N_EXPERTS = 8
TOP_K = 2
FFN_EXPERT = 7 * D_MODEL // 2
N_EVEN = (DEPTH + 1) // 2
N_ODD = DEPTH // 2
HYB_SPLITS = (GLA_HEADS * GLA_DK, GLA_HEADS * GLA_DK, GLA_HEADS * GLA_DV, GLA_LOWRANK, GLA_HEADS * GLA_DV,
              NSA_HEADS * NSA_HEAD_DIM, 6 * NSA_KV_GROUPS * NSA_HEAD_DIM, 3 * NSA_HEADS)
HYB_IN = sum(HYB_SPLITS)
HYB_MIX = GLA_HEADS * GLA_DV + NSA_HEADS * NSA_HEAD_DIM
SSM_SPLITS = (D_INNER, CONV_CH, SSM_HEADS)
SSM_IN = sum(SSM_SPLITS)


def rmsnorm(x, w):
    xf = x.astype(jnp.float32)
    y = xf * lax.rsqrt(jnp.mean(xf * xf, axis=-1, keepdims=True) + NORM_EPS)
    return (y * w.astype(jnp.float32)).astype(x.dtype)

def split_cols(a, sizes):
    return jnp.split(a, [int(s) for s in np.cumsum(sizes)[:-1]], axis=-1)

def adaln(c, w, b):
    mod = jax.nn.silu(c) @ w + b
    shift, scale, gate = jnp.split(mod[:, None, :], 3, axis=-1)
    return shift, scale, gate

def modulate(x, norm_w, shift, scale):
    return rmsnorm(x, norm_w) * (1 + scale) + shift

def masked_softmax(s, mask):
    s = jnp.where(mask, s.astype(jnp.float32), -jnp.inf)
    m = jnp.max(s, axis=-1, keepdims=True)
    m = jnp.where(jnp.isfinite(m), m, 0.0)
    p = jnp.where(mask, jnp.exp(s - m), 0.0)
    return p / jnp.maximum(jnp.sum(p, axis=-1, keepdims=True), 1e-20)

def alibi_slopes(n):
    return 2.0 ** (-8.0 * jnp.arange(1, n + 1, dtype=jnp.float32) / n)

def swiglu(h, w_gu, w_down):
    g, u = jnp.split(h @ w_gu, 2, axis=-1)
    return (jax.nn.silu(g) * u) @ w_down

def gla_mixer(q, k, v, lowrank, r, gk_up, gk_bias, out_norm):
    B, T, _ = q.shape
    H, DK, DV, C = GLA_HEADS, GLA_DK, GLA_DV, GLA_CHUNK
    NC = T // C

    def chunks(a, d):
        return a.astype(jnp.float32).reshape(B, NC, C, H, d).transpose(0, 3, 1, 2, 4)

    log_alpha = jax.nn.log_sigmoid((lowrank @ gk_up + gk_bias).astype(jnp.float32)) / GLA_TAU
    b = jnp.cumsum(chunks(log_alpha, DK), axis=3)
    qc = chunks(q, DK) * DK ** -0.5
    kc = chunks(k, DK)
    vc = chunks(v, DV)
    q_dec = qc * jnp.exp(b)
    k_dec = kc * jnp.exp(-b)
    causal = jnp.tril(jnp.ones((C, C), dtype=bool))
    att = jnp.where(causal, jnp.einsum('bhncd,bhnsd->bhncs', q_dec, k_dec), 0.0)
    o_intra = jnp.einsum('bhncs,bhnsv->bhncv', att, vc)
    b_end = b[:, :, :, -1]
    k_to_end = kc * jnp.exp(b_end[:, :, :, None] - b)

    def step(S, inp):
        qd, kd, vv, decay = inp
        o = jnp.einsum('bhcd,bhdv->bhcv', qd, S)
        S = jnp.exp(decay)[..., None] * S + jnp.einsum('bhcd,bhcv->bhdv', kd, vv)
        return S, o

    S0 = jnp.zeros((B, H, DK, DV), jnp.float32)
    xs = tuple(jnp.moveaxis(a, 2, 0) for a in (q_dec, k_to_end, vc, b_end))
    _, o_inter = lax.scan(step, S0, xs)
    o = o_intra + jnp.moveaxis(o_inter, 0, 2)
    o = o.transpose(0, 2, 3, 1, 4).reshape(B, T, H, DV)
    o = rmsnorm(o, out_norm) * jax.nn.silu(r.astype(jnp.float32).reshape(B, T, H, DV))
    return o.reshape(B, T, H * DV)

def nsa_mixer(q, kv, gate_logits, cmp_pe, cmp_w1, cmp_w2):
    B, T, _ = q.shape
    G, Dh = NSA_KV_GROUPS, NSA_HEAD_DIM
    R = NSA_HEADS // G
    qh = q.astype(jnp.float32).reshape(B, T, G, R, Dh).transpose(0, 2, 3, 1, 4) * Dh ** -0.5
    kvh = kv.astype(jnp.float32).reshape(B, T, 6, G, Dh).transpose(2, 0, 3, 1, 4)
    k_cmp, v_cmp, k_slc, v_slc, k_win, v_win = (kvh[j] for j in range(6))
    gates = jax.nn.sigmoid(gate_logits.astype(jnp.float32)).reshape(B, T, G, R, 3).transpose(0, 2, 3, 1, 4)

    n_cmp = (T - CMP_BLOCK) // CMP_STRIDE + 1
    blk_idx = np.arange(n_cmp)[:, None] * CMP_STRIDE + np.arange(CMP_BLOCK)[None, :]

    def compress(a, j):
        blocks = a[:, :, blk_idx] + cmp_pe[j]
        h = jax.nn.gelu(blocks.reshape(B, G, n_cmp, CMP_BLOCK * Dh) @ cmp_w1[j])
        return h @ cmp_w2[j]

    kc = compress(k_cmp, 0)
    vc = compress(v_cmp, 1)
    cmp_end = jnp.asarray(blk_idx[:, -1], jnp.int32)
    cmp_center = jnp.asarray(blk_idx.mean(axis=-1), jnp.float32)

    n_sel = T // SEL_BLOCK
    n_top = min(N_SELECT, n_sel)
    sel_start_np = np.arange(n_sel) * SEL_BLOCK
    overlap = jnp.asarray((blk_idx[:, :1] < sel_start_np[None, :] + SEL_BLOCK)
                          & (blk_idx[:, -1:] >= sel_start_np[None, :]), jnp.float32)
    sel_start = jnp.asarray(sel_start_np, jnp.int32)
    kb = k_slc.reshape(B, G, n_sel, SEL_BLOCK, Dh)
    vb = v_slc.reshape(B, G, n_sel, SEL_BLOCK, Dh)
    bi = jnp.arange(B)[:, None, None, None]
    gi = jnp.arange(G)[None, :, None, None]

    k_wp = jnp.pad(k_win, ((0, 0), (0, 0), (WINDOW, 0), (0, 0)))
    v_wp = jnp.pad(v_win, ((0, 0), (0, 0), (WINDOW, 0), (0, 0)))
    slopes = alibi_slopes(NSA_HEADS).reshape(G, R, 1, 1)

    def block_fn(i):
        q0 = i * Q_BLOCK
        qb = lax.dynamic_slice_in_dim(qh, q0, Q_BLOCK, axis=3)
        gb = lax.dynamic_slice_in_dim(gates, q0, Q_BLOCK, axis=3)
        t = q0 + jnp.arange(Q_BLOCK, dtype=jnp.int32)
        tf = t.astype(jnp.float32)
        s = jnp.einsum('bgrqd,bgkd->bgrqk', qb, kc) - slopes * (tf[:, None] - cmp_center[None, :])
        p_cmp = masked_softmax(s, cmp_end[None, :] <= t[:, None])
        o_cmp = jnp.einsum('bgrqk,bgkd->bgrqd', p_cmp, vc)
        imp = jnp.einsum('bgqk,ks->bgqs', jnp.sum(p_cmp, axis=2), overlap)
        blk_t = t // SEL_BLOCK
        ids = jnp.arange(n_sel)[None, :]
        forced = (ids == 0) | (ids == blk_t[:, None]) | (ids == blk_t[:, None] - 1)
        future = sel_start[None, :] > t[:, None]
        imp = jnp.where(forced, jnp.inf, jnp.where(future, -jnp.inf, imp))
        _, idx = lax.top_k(imp, n_top)
        ks_ = kb[bi, gi, idx].reshape(B, G, Q_BLOCK, n_top * SEL_BLOCK, Dh)
        vs_ = vb[bi, gi, idx].reshape(B, G, Q_BLOCK, n_top * SEL_BLOCK, Dh)
        pos = (idx[..., None] * SEL_BLOCK + jnp.arange(SEL_BLOCK)).reshape(B, G, Q_BLOCK, n_top * SEL_BLOCK)
        dist = (t[None, None, :, None] - pos)[:, :, None]
        s = jnp.einsum('bgrqd,bgqkd->bgrqk', qb, ks_) - slopes * dist.astype(jnp.float32)
        p_slc = masked_softmax(s, dist >= 0)
        o_slc = jnp.einsum('bgrqk,bgqkd->bgrqd', p_slc, vs_)
        kw = lax.dynamic_slice_in_dim(k_wp, q0, WINDOW + Q_BLOCK, axis=2)
        vw = lax.dynamic_slice_in_dim(v_wp, q0, WINDOW + Q_BLOCK, axis=2)
        s_pos = q0 - WINDOW + jnp.arange(WINDOW + Q_BLOCK, dtype=jnp.int32)
        d = t[:, None] - s_pos[None, :]
        s = jnp.einsum('bgrqd,bgkd->bgrqk', qb, kw) - slopes * d.astype(jnp.float32)
        p_win = masked_softmax(s, (d >= 0) & (d < WINDOW) & (s_pos[None, :] >= 0))
        o_win = jnp.einsum('bgrqk,bgkd->bgrqd', p_win, vw)
        o = gb[..., 0:1] * o_cmp + gb[..., 1:2] * o_slc + gb[..., 2:3] * o_win
        return o.transpose(0, 3, 1, 2, 4).reshape(B, Q_BLOCK, NSA_HEADS * Dh)

    out = lax.map(block_fn, jnp.arange(T // Q_BLOCK))
    return out.transpose(1, 0, 2, 3).reshape(B, T, NSA_HEADS * Dh)

def hybrid_mixer(h, w_in, gk_up, gk_bias, gla_norm, cmp_pe, cmp_w1, cmp_w2, w_out):
    q_a, k_a, v_a, lr_a, r_a, q_b, kv_b, g_b = split_cols(h @ w_in, HYB_SPLITS)
    o_a = gla_mixer(q_a, k_a, v_a, lr_a, r_a, gk_up, gk_bias, gla_norm)
    o_b = nsa_mixer(q_b, kv_b, g_b, cmp_pe, cmp_w1, cmp_w2)
    return jnp.concatenate([o_a, o_b], axis=-1).astype(h.dtype) @ w_out

def mamba2_mixer(h, w_in, conv_w, conv_b, dt_bias, a_log, d_skip, norm_w, w_out):
    B, T, _ = h.shape
    H, P, G, N, Q = SSM_HEADS, SSM_HEAD_DIM, SSM_GROUPS, SSM_STATE, SSM_CHUNK
    R = H // G
    NC = T // Q
    z, xbc, dt = split_cols(h @ w_in, SSM_SPLITS)
    xbc = lax.conv_general_dilated(xbc, conv_w[:, None, :].astype(xbc.dtype), window_strides=(1,),
                                   padding=((CONV_K - 1, 0),), dimension_numbers=('NWC', 'WIO', 'NWC'),
                                   feature_group_count=CONV_CH) + conv_b
    xbc = jax.nn.silu(xbc.astype(jnp.float32))
    xs_, Bm, Cm = split_cols(xbc, (D_INNER, G * N, G * N))
    dt = jax.nn.softplus(dt.astype(jnp.float32) + dt_bias)
    A = -jnp.exp(a_log.astype(jnp.float32))
    x = xs_.reshape(B, T, H, P)
    xdt = (x * dt[..., None]).reshape(B, NC, Q, G, R, P)
    Bc = Bm.reshape(B, NC, Q, G, N)
    Cc = Cm.reshape(B, NC, Q, G, N)
    a = (dt * A).reshape(B, NC, Q, G, R).transpose(0, 3, 4, 1, 2)
    cum = jnp.cumsum(a, axis=-1)
    seg = cum[..., :, None] - cum[..., None, :]
    causal = jnp.tril(jnp.ones((Q, Q), dtype=bool))
    L = jnp.exp(jnp.where(causal, seg, -jnp.inf))
    cb = jnp.einsum('bclgn,bcsgn->bgcls', Cc, Bc)
    y_diag = jnp.einsum('bgcls,bgrcls,bcsgrp->bclgrp', cb, L, xdt)
    decay_to_end = jnp.exp(cum[..., -1:] - cum)
    decay_from_start = jnp.exp(cum)
    chunk_decay = jnp.exp(cum[..., -1])

    def step(S, inp):
        Bn, Cn, xn, dte, dfs, cd = inp
        y = jnp.einsum('blgn,bgrpn,bgrl->blgrp', Cn, S, dfs)
        S = cd[..., None, None] * S + jnp.einsum('bsgn,bgrs,bsgrp->bgrpn', Bn, dte, xn)
        return S, y

    S0 = jnp.zeros((B, G, R, P, N), jnp.float32)
    xs = (jnp.moveaxis(Bc, 1, 0), jnp.moveaxis(Cc, 1, 0), jnp.moveaxis(xdt, 1, 0),
          jnp.moveaxis(decay_to_end, 3, 0), jnp.moveaxis(decay_from_start, 3, 0), jnp.moveaxis(chunk_decay, 3, 0))
    _, y_off = lax.scan(step, S0, xs)
    y = (y_diag + jnp.moveaxis(y_off, 0, 1)).reshape(B, T, H, P) + d_skip[:, None] * x
    y = y.reshape(B, T, D_INNER) * jax.nn.silu(z.astype(jnp.float32))
    y = rmsnorm(y.reshape(B, T, G, D_INNER // G), norm_w.reshape(G, D_INNER // G)).reshape(B, T, D_INNER)
    return y.astype(h.dtype) @ w_out

def moe_ffn(h, router, w_gu, w_down):
    logits = (h @ router).astype(jnp.float32)
    top_val, top_idx = lax.top_k(logits, TOP_K)
    weights = jax.nn.softmax(top_val, axis=-1)
    gate = jnp.sum(jax.nn.one_hot(top_idx, N_EXPERTS, dtype=jnp.float32) * weights[..., None], axis=-2)
    out = jnp.zeros(h.shape, jnp.float32)
    for e in range(N_EXPERTS):
        out = out + gate[..., e:e + 1] * swiglu(h, w_gu[e], w_down[e])
    return out

def first_inputs(seed: int = 0) -> dict:
    key = jax.random.key(seed)
    ks = jax.random.split(key, 40)
    f32 = jnp.float32

    def nrm(i, shape, scale):
        return scale * jax.random.normal(ks[i], shape, f32)

    def gain(i, shape):
        return 1.0 + 0.1 * jax.random.normal(ks[i], shape, f32)

    dt = jnp.exp(jax.random.uniform(ks[30], (N_ODD, SSM_HEADS), f32,
                                    math.log(0.001), math.log(0.1)))
    return {
        'x': nrm(0, (BATCH, SEQ, D_MODEL), 1.0),
        'c': nrm(1, (BATCH, D_MODEL), 1.0),
        'hyb_norm': gain(2, (N_EVEN, D_MODEL)),
        'hyb_mod_w': nrm(3, (N_EVEN, D_MODEL, 3 * D_MODEL), 0.5 * D_MODEL ** -0.5),
        'hyb_mod_b': nrm(4, (N_EVEN, 3 * D_MODEL), 0.02),
        'hyb_w_in': nrm(5, (N_EVEN, D_MODEL, HYB_IN), D_MODEL ** -0.5),
        'gla_gk_up': nrm(6, (N_EVEN, GLA_LOWRANK, GLA_HEADS * GLA_DK), GLA_LOWRANK ** -0.5),
        'gla_gk_bias': nrm(7, (N_EVEN, GLA_HEADS * GLA_DK), 0.1),
        'gla_out_norm': gain(8, (N_EVEN, GLA_DV)),
        'nsa_cmp_pe': nrm(9, (N_EVEN, 2, CMP_BLOCK, NSA_HEAD_DIM), 0.1),
        'nsa_cmp_w1': nrm(10, (N_EVEN, 2, CMP_BLOCK * NSA_HEAD_DIM, CMP_HIDDEN), (CMP_BLOCK * NSA_HEAD_DIM) ** -0.5),
        'nsa_cmp_w2': nrm(11, (N_EVEN, 2, CMP_HIDDEN, NSA_HEAD_DIM), CMP_HIDDEN ** -0.5),
        'hyb_w_out': nrm(12, (N_EVEN, HYB_MIX, D_MODEL), HYB_MIX ** -0.5),
        'dense_norm': gain(13, (N_EVEN, D_MODEL)),
        'dense_mod_w': nrm(14, (N_EVEN, D_MODEL, 3 * D_MODEL), 0.5 * D_MODEL ** -0.5),
        'dense_mod_b': nrm(15, (N_EVEN, 3 * D_MODEL), 0.02),
        'dense_w_gu': nrm(16, (N_EVEN, D_MODEL, 2 * FFN_DENSE), D_MODEL ** -0.5),
        'dense_w_down': nrm(17, (N_EVEN, FFN_DENSE, D_MODEL), FFN_DENSE ** -0.5),
        'ssm_norm': gain(18, (N_ODD, D_MODEL)),
        'ssm_mod_w': nrm(19, (N_ODD, D_MODEL, 3 * D_MODEL), 0.5 * D_MODEL ** -0.5),
        'ssm_mod_b': nrm(20, (N_ODD, 3 * D_MODEL), 0.02),
        'ssm_w_in': nrm(21, (N_ODD, D_MODEL, SSM_IN), D_MODEL ** -0.5),
        'ssm_conv_w': nrm(22, (N_ODD, CONV_K, CONV_CH), CONV_K ** -0.5),
        'ssm_conv_b': nrm(23, (N_ODD, CONV_CH), 0.02),
        'ssm_dt_bias': dt + jnp.log(-jnp.expm1(-dt)),
        'ssm_a_log': jnp.log(jax.random.uniform(ks[24], (N_ODD, SSM_HEADS), f32, 1.0, 16.0)),
        'ssm_d': gain(25, (N_ODD, SSM_HEADS)),
        'ssm_gate_norm': gain(26, (N_ODD, D_INNER)),
        'ssm_w_out': nrm(27, (N_ODD, D_INNER, D_MODEL), D_INNER ** -0.5),
        'moe_norm': gain(28, (N_ODD, D_MODEL)),
        'moe_mod_w': nrm(29, (N_ODD, D_MODEL, 3 * D_MODEL), 0.5 * D_MODEL ** -0.5),
        'moe_mod_b': nrm(31, (N_ODD, 3 * D_MODEL), 0.02),
        'moe_router': nrm(32, (N_ODD, D_MODEL, N_EXPERTS), D_MODEL ** -0.5),
        'moe_w_gu': nrm(33, (N_ODD, N_EXPERTS, D_MODEL, 2 * FFN_EXPERT), D_MODEL ** -0.5),
        'moe_w_down': nrm(34, (N_ODD, N_EXPERTS, FFN_EXPERT, D_MODEL), FFN_EXPERT ** -0.5),
        'final_norm': gain(35, (D_MODEL,)),
    }

def first_block(x, c, hyb_norm, hyb_mod_w, hyb_mod_b, hyb_w_in, gla_gk_up, gla_gk_bias, gla_out_norm,
              nsa_cmp_pe, nsa_cmp_w1, nsa_cmp_w2, hyb_w_out, dense_norm, dense_mod_w, dense_mod_b,
              dense_w_gu, dense_w_down, ssm_norm, ssm_mod_w, ssm_mod_b, ssm_w_in, ssm_conv_w, ssm_conv_b,
              ssm_dt_bias, ssm_a_log, ssm_d, ssm_gate_norm, ssm_w_out, moe_norm, moe_mod_w, moe_mod_b,
              moe_router, moe_w_gu, moe_w_down, final_norm):
    for layer in range(DEPTH):
        i = layer // 2
        if layer % 2 == 0:
            shift, scale, gate = adaln(c, hyb_mod_w[i], hyb_mod_b[i])
            mix = hybrid_mixer(modulate(x, hyb_norm[i], shift, scale), hyb_w_in[i], gla_gk_up[i], gla_gk_bias[i],
                               gla_out_norm[i], nsa_cmp_pe[i], nsa_cmp_w1[i], nsa_cmp_w2[i], hyb_w_out[i])
            x = x + (gate * mix).astype(x.dtype)
            shift, scale, gate = adaln(c, dense_mod_w[i], dense_mod_b[i])
            ffn = swiglu(modulate(x, dense_norm[i], shift, scale), dense_w_gu[i], dense_w_down[i])
            x = x + (gate * ffn).astype(x.dtype)
        else:
            shift, scale, gate = adaln(c, ssm_mod_w[i], ssm_mod_b[i])
            mix = mamba2_mixer(modulate(x, ssm_norm[i], shift, scale), ssm_w_in[i], ssm_conv_w[i], ssm_conv_b[i],
                               ssm_dt_bias[i], ssm_a_log[i], ssm_d[i], ssm_gate_norm[i], ssm_w_out[i])
            x = x + (gate * mix).astype(x.dtype)
            shift, scale, gate = adaln(c, moe_mod_w[i], moe_mod_b[i])
            ffn = moe_ffn(modulate(x, moe_norm[i], shift, scale), moe_router[i], moe_w_gu[i], moe_w_down[i])
            x = x + (gate * ffn).astype(x.dtype)
    return rmsnorm(x, final_norm)


GDN_HEADS = D_MODEL // 256
GDN_DK = 128
GDN_DV = 128
GDN_CONV = 4
GDN_CHUNK = 64
MOBA_HEADS = D_MODEL // 128
MOBA_DH = 64
MOBA_BLOCK = 256
MOBA_TOPK = 3
MOBA_QCHUNK = 32
ROPE_DIMS = MOBA_DH // 4
ROPE_THETA = 500000.0
GDN_QK_W = GDN_HEADS * GDN_DK
GDN_V_W = GDN_HEADS * GDN_DV
MOBA_W = MOBA_HEADS * MOBA_DH
D_MIX = GDN_V_W + MOBA_W
IN_SPLITS = (GDN_QK_W, GDN_QK_W, GDN_V_W, GDN_HEADS, GDN_HEADS, GDN_V_W, MOBA_W, MOBA_W, MOBA_W)
N_IN = sum(IN_SPLITS)
D_FF = 256 * ((8 * D_MODEL // 3 + 255) // 256)
FFN_CONV = 3
DEEPNORM_ALPHA = (2 * DEPTH) ** 0.25
DEEPNORM_BETA = (8 * DEPTH) ** -0.25
LN_EPS = 1e-5


def layer_norm(x, g, b):
    xf = x.astype(jnp.float32)
    mu = xf.mean(-1, keepdims=True)
    var = jnp.square(xf - mu).mean(-1, keepdims=True)
    return ((xf - mu) * lax.rsqrt(var + LN_EPS) * g + b).astype(x.dtype)

def causal_dwconv(x, w):
    k_w = w.shape[0]
    s = x.shape[1]
    xp = jnp.pad(x, ((0, 0), (k_w - 1, 0), (0, 0)))
    return sum(xp[:, j:j + s, :] * w[j] for j in range(k_w))

def l2norm(x):
    return x * lax.rsqrt(jnp.sum(x * x, -1, keepdims=True) + NORM_EPS)

def split_heads(t, n_heads):
    b, s, _ = t.shape
    return t.reshape(b, s, n_heads, -1).transpose(0, 2, 1, 3)

def partial_rotary(x, pos):
    half = ROPE_DIMS // 2
    inv = ROPE_THETA ** (-jnp.arange(half, dtype=jnp.float32) / half)
    ang = pos.astype(jnp.float32)[:, None] * inv[None, :]
    cos = jnp.cos(ang).astype(x.dtype)
    sin = jnp.sin(ang).astype(x.dtype)
    x1, x2, rest = x[..., :half], x[..., half:ROPE_DIMS], x[..., ROPE_DIMS:]
    return jnp.concatenate([x1 * cos - x2 * sin, x2 * cos + x1 * sin, rest], -1)

def gated_delta_rule(q, k, v, g, beta):
    b_, h, s, dk = q.shape
    dv = v.shape[-1]
    c = GDN_CHUNK
    n = s // c
    q = q * dk ** -0.5
    resh = lambda t: t.reshape(b_, h, n, c, *t.shape[3:])
    q, k, v, g, beta = map(resh, (q, k, v, g, beta))
    g = jnp.cumsum(g, axis=-1)
    idx = jnp.arange(c)
    lower_incl = idx[:, None] >= idx[None, :]
    decay = jnp.exp(jnp.where(lower_incl, g[..., :, None] - g[..., None, :], -jnp.inf))
    k_beta = k * beta[..., None]
    a_strict = jnp.where(idx[:, None] > idx[None, :],
                         jnp.einsum('bhncd,bhnmd->bhncm', k_beta, k) * decay, 0.0)
    t_mat = a_strict + jnp.eye(c, dtype=q.dtype)
    rhs = jnp.concatenate([v * beta[..., None], k_beta * jnp.exp(g)[..., None]], -1)
    sol = lax.linalg.triangular_solve(t_mat, rhs, left_side=True, lower=True, unit_diagonal=True)
    u, w = sol[..., :dv], sol[..., dv:]
    attn_intra = jnp.einsum('bhncd,bhnmd->bhncm', q, k) * decay
    q_dec = q * jnp.exp(g)[..., None]
    g_last = g[..., -1]
    k_dec = k * jnp.exp(g_last[..., None] - g)[..., None]

    def step(state, xs):
        q_c, k_c, u_c, w_c, a_c, gl = xs
        v_new = u_c - jnp.einsum('bhcd,bhde->bhce', w_c, state)
        o = jnp.einsum('bhcd,bhde->bhce', q_c, state) + jnp.einsum('bhcm,bhme->bhce', a_c, v_new)
        state = state * jnp.exp(gl)[..., None, None] + jnp.einsum('bhcd,bhce->bhde', k_c, v_new)
        return state, o

    xs = tuple(jnp.moveaxis(t, 2, 0) for t in (q_dec, k_dec, u, w, attn_intra, g_last))
    s0 = jnp.zeros((b_, h, dk, dv), q.dtype)
    _, o = lax.scan(step, s0, xs)
    return jnp.moveaxis(o, 0, 2).reshape(b_, h, s, dv)

def gdn_mixer(q, k, v, a_logit, b_logit, z, conv_w, a_log, dt_bias, norm_g):
    b_, s, _ = q.shape
    qkv = jax.nn.silu(causal_dwconv(jnp.concatenate([q, k, v], -1), conv_w))
    q, k, v = jnp.split(qkv, [GDN_QK_W, 2 * GDN_QK_W], -1)
    f32 = jnp.float32
    qh = l2norm(split_heads(q, GDN_HEADS).astype(f32))
    kh = l2norm(split_heads(k, GDN_HEADS).astype(f32))
    vh = split_heads(v, GDN_HEADS).astype(f32)
    beta = jax.nn.sigmoid(b_logit.astype(f32)).transpose(0, 2, 1)
    g = (-jnp.exp(a_log.astype(f32)) * jax.nn.softplus(a_logit.astype(f32) + dt_bias.astype(f32))).transpose(0, 2, 1)
    o = gated_delta_rule(qh, kh, vh, g, beta).transpose(0, 2, 1, 3)
    o = o * lax.rsqrt(jnp.mean(o * o, -1, keepdims=True) + NORM_EPS) * norm_g.astype(f32)
    o = o * jax.nn.silu(z.reshape(b_, s, GDN_HEADS, GDN_DV).astype(f32))
    return o.reshape(b_, s, GDN_V_W).astype(q.dtype)

def moba_mixer(q, k, v, pos):
    b_, s, _ = q.shape
    h, dh, blk, qc_len = MOBA_HEADS, MOBA_DH, MOBA_BLOCK, MOBA_QCHUNK
    qh = partial_rotary(split_heads(q, h), pos)
    kh = partial_rotary(split_heads(k, h), pos)
    vh = split_heads(v, h)
    nb = -(-s // blk)
    pad = nb * blk - s
    n_sel = min(MOBA_TOPK, nb)
    kb = jnp.pad(kh, ((0, 0), (0, 0), (0, pad), (0, 0))).reshape(b_, h, nb, blk, dh)
    vb = jnp.pad(vh, ((0, 0), (0, 0), (0, pad), (0, 0))).reshape(b_, h, nb, blk, dh)
    k_mean = kb.mean(axis=3)
    nq = s // qc_len
    q_chunks = jnp.moveaxis(qh.reshape(b_, h, nq, qc_len, dh), 2, 0)
    scale = dh ** -0.5
    bi = jnp.arange(b_)[:, None, None, None]
    hi = jnp.arange(h)[None, :, None, None]
    blk_ids = jnp.arange(nb)
    sel_rank = jnp.arange(n_sel)

    def attend(args):
        q_c, ci = args
        t = ci * qc_len + jnp.arange(qc_len)
        own = (ci * qc_len) // blk
        gate = jnp.einsum('bhqd,bhnd->bhqn', q_c, k_mean).astype(jnp.float32)
        gate = jnp.where(blk_ids < own, gate, -jnp.inf)
        _, sel = lax.top_k(gate, n_sel)
        sel_valid = sel_rank < own
        k_sel = kb[bi, hi, sel]
        v_sel = vb[bi, hi, sel]
        s_sel = jnp.einsum('bhqd,bhqjkd->bhqjk', q_c, k_sel).astype(jnp.float32) * scale
        s_sel = jnp.where(sel_valid[:, None], s_sel, -jnp.inf).reshape(b_, h, qc_len, n_sel * blk)
        k_own = lax.dynamic_index_in_dim(kb, own, axis=2, keepdims=False)
        v_own = lax.dynamic_index_in_dim(vb, own, axis=2, keepdims=False)
        s_own = jnp.einsum('bhqd,bhkd->bhqk', q_c, k_own).astype(jnp.float32) * scale
        key_pos = own * blk + jnp.arange(blk)
        s_own = jnp.where(key_pos[None, :] <= t[:, None], s_own, -jnp.inf)
        p = jax.nn.softmax(jnp.concatenate([s_own, s_sel], -1), axis=-1).astype(v_sel.dtype)
        p_own = p[..., :blk]
        p_sel = p[..., blk:].reshape(b_, h, qc_len, n_sel, blk)
        return (jnp.einsum('bhqk,bhkd->bhqd', p_own, v_own)
                + jnp.einsum('bhqjk,bhqjkd->bhqd', p_sel, v_sel))

    o = lax.map(attend, (q_chunks, jnp.arange(nq)))
    o = jnp.moveaxis(o, 0, 2).reshape(b_, h, s, dh)
    return o.transpose(0, 2, 1, 3).reshape(b_, s, MOBA_W)

def hybrid_layer(x, w_in, gdn_conv_w, gdn_a_log, gdn_dt_bias, gdn_norm_g, w_out,
                 ln1_g, ln1_b, w_up, ffn_conv_w, ffn_conv_b, w_down, ln2_g, ln2_b, pos):
    proj = x @ w_in
    offs = np.cumsum(IN_SPLITS)[:-1].tolist()
    q_a, k_a, v_a, a_logit, b_logit, z, q_b, k_b, v_b = jnp.split(proj, offs, -1)
    o_a = gdn_mixer(q_a, k_a, v_a, a_logit, b_logit, z, gdn_conv_w, gdn_a_log, gdn_dt_bias, gdn_norm_g)
    o_b = moba_mixer(q_b, k_b, v_b, pos)
    mix = jnp.concatenate([o_a, o_b], -1) @ w_out
    x = layer_norm(DEEPNORM_ALPHA * x + mix, ln1_g, ln1_b)
    hid = causal_dwconv(x @ w_up, ffn_conv_w) + ffn_conv_b
    gate, val = jnp.split(hid, 2, -1)
    ffn = (jax.nn.silu(gate) * val) @ w_down
    return layer_norm(DEEPNORM_ALPHA * x + ffn, ln2_g, ln2_b)

def second_inputs(seed: int = 0) -> dict:
    key = jax.random.key(seed)
    ks = jax.random.split(key, 16)
    f = jnp.float32
    nrm = lambda k, shape, scale: jax.random.normal(k, shape, f) * scale
    x = jax.random.normal(ks[0], (BATCH, SEQ, D_MODEL), f)
    w_in = nrm(ks[1], (DEPTH, D_MODEL, N_IN), D_MODEL ** -0.5)
    gdn_conv_w = nrm(ks[2], (DEPTH, GDN_CONV, 2 * GDN_QK_W + GDN_V_W), GDN_CONV ** -0.5)
    gdn_a_log = jnp.log(jax.random.uniform(ks[3], (DEPTH, GDN_HEADS), f, 1.0, 16.0))
    dt = jnp.exp(jax.random.uniform(ks[4], (DEPTH, GDN_HEADS), f, float(np.log(1e-3)), float(np.log(1e-1))))
    gdn_dt_bias = dt + jnp.log(-jnp.expm1(-dt))
    gdn_norm_g = 1.0 + nrm(ks[5], (DEPTH, GDN_DV), 0.02)
    w_out = nrm(ks[6], (DEPTH, D_MIX, D_MODEL), DEEPNORM_BETA * D_MIX ** -0.5)
    ln1_g = 1.0 + nrm(ks[7], (DEPTH, D_MODEL), 0.02)
    ln1_b = nrm(ks[8], (DEPTH, D_MODEL), 0.02)
    w_up = nrm(ks[9], (DEPTH, D_MODEL, 2 * D_FF), D_MODEL ** -0.5)
    ffn_conv_w = nrm(ks[10], (DEPTH, FFN_CONV, 2 * D_FF), FFN_CONV ** -0.5)
    ffn_conv_b = nrm(ks[11], (DEPTH, 2 * D_FF), 0.01)
    w_down = nrm(ks[12], (DEPTH, D_FF, D_MODEL), DEEPNORM_BETA * D_FF ** -0.5)
    ln2_g = 1.0 + nrm(ks[13], (DEPTH, D_MODEL), 0.02)
    ln2_b = nrm(ks[14], (DEPTH, D_MODEL), 0.02)
    return {'x': x, 'w_in': w_in, 'gdn_conv_w': gdn_conv_w, 'gdn_a_log': gdn_a_log,
            'gdn_dt_bias': gdn_dt_bias, 'gdn_norm_g': gdn_norm_g, 'w_out': w_out,
            'ln1_g': ln1_g, 'ln1_b': ln1_b, 'w_up': w_up, 'ffn_conv_w': ffn_conv_w,
            'ffn_conv_b': ffn_conv_b, 'w_down': w_down, 'ln2_g': ln2_g, 'ln2_b': ln2_b}

def second_block(x, w_in, gdn_conv_w, gdn_a_log, gdn_dt_bias, gdn_norm_g, w_out,
              ln1_g, ln1_b, w_up, ffn_conv_w, ffn_conv_b, w_down, ln2_g, ln2_b):
    pos = jnp.arange(x.shape[1], dtype=jnp.int32)
    for l in range(DEPTH):
        x = hybrid_layer(x, w_in[l], gdn_conv_w[l], gdn_a_log[l], gdn_dt_bias[l], gdn_norm_g[l],
                         w_out[l], ln1_g[l], ln1_b[l], w_up[l], ffn_conv_w[l], ffn_conv_b[l],
                         w_down[l], ln2_g[l], ln2_b[l], pos)
    return x


def setup_inputs(seed=0):
    out = dict(first_inputs(seed))
    for name, value in second_inputs(seed + 1).items():
        if name != "x":
            out[name + "_2"] = value
    return out


def reference(
    x, c, hyb_norm, hyb_mod_w, hyb_mod_b, hyb_w_in, gla_gk_up, gla_gk_bias, gla_out_norm,
    nsa_cmp_pe, nsa_cmp_w1, nsa_cmp_w2, hyb_w_out, dense_norm, dense_mod_w, dense_mod_b,
    dense_w_gu, dense_w_down, ssm_norm, ssm_mod_w, ssm_mod_b, ssm_w_in, ssm_conv_w, ssm_conv_b,
    ssm_dt_bias, ssm_a_log, ssm_d, ssm_gate_norm, ssm_w_out, moe_norm, moe_mod_w, moe_mod_b,
    moe_router, moe_w_gu, moe_w_down, final_norm, w_in_2, gdn_conv_w_2, gdn_a_log_2,
    gdn_dt_bias_2, gdn_norm_g_2, w_out_2, ln1_g_2, ln1_b_2, w_up_2, ffn_conv_w_2, ffn_conv_b_2,
    w_down_2, ln2_g_2, ln2_b_2,
):
    x = first_block(
        x, c, hyb_norm, hyb_mod_w, hyb_mod_b, hyb_w_in, gla_gk_up, gla_gk_bias, gla_out_norm,
        nsa_cmp_pe, nsa_cmp_w1, nsa_cmp_w2, hyb_w_out, dense_norm, dense_mod_w, dense_mod_b,
        dense_w_gu, dense_w_down, ssm_norm, ssm_mod_w, ssm_mod_b, ssm_w_in, ssm_conv_w,
        ssm_conv_b, ssm_dt_bias, ssm_a_log, ssm_d, ssm_gate_norm, ssm_w_out, moe_norm,
        moe_mod_w, moe_mod_b, moe_router, moe_w_gu, moe_w_down, final_norm,
    )
    return second_block(
        x, w_in_2, gdn_conv_w_2, gdn_a_log_2, gdn_dt_bias_2, gdn_norm_g_2, w_out_2, ln1_g_2,
        ln1_b_2, w_up_2, ffn_conv_w_2, ffn_conv_b_2, w_down_2, ln2_g_2, ln2_b_2,
    )


_drawn_inputs = setup_inputs


def setup_inputs(seed=0):
    import zlib

    import numpy as np

    out = dict(_drawn_inputs(seed))
    spreads = {}
    factors = {'gla_gk_bias': 5.545,
     'nsa_cmp_pe': 5.256,
     'dense_mod_b': 2.887,
     'ssm_conv_b': 4.995,
     'ssm_d': 3.194,
     'moe_mod_b': 2.681,
     'gdn_norm_g_2': 8.0,
     'ffn_conv_b_2': 8.0}
    for name, (base, spread) in spreads.items():
        noise = np.random.default_rng([zlib.crc32(name.encode()), seed]).standard_normal(out[name].shape)
        drawn = base * np.exp(spread * noise) if base else spread * noise
        out[name] = __import__('jax').numpy.asarray(drawn.astype(out[name].dtype))
    for name, factor in factors.items():
        out[name] = (out[name] * factor).astype(out[name].dtype)
    return out
```

```python
import numpy as np
import concourse.bass as bass
from concourse import mybir
from concourse.alu_op_type import AluOpType as ALU
from contextlib import ExitStack

F32 = mybir.dt.float32
AF = mybir.ActivationFunctionType
AX = mybir.AxisListType

ENGINES = ("sync", "tensor", "vector", "scalar", "gpsimd")


class Op:

    def __init__(self, eng, fn, waits, dma):
        self.eng, self.fn, self.waits, self.dma = eng, fn, waits, dma
        self.needed, self.sem, self.val = False, None, 0


class Program:

    def __init__(self):
        self.q = {e: [] for e in ENGINES}
        self.hold = {e: [] for e in ENGINES}
        self.dma_count = {}

    def add(self, eng, fn, waits=(), dma=None):
        flat = []

        def walk(w):
            if w is None:
                return
            if isinstance(w, (list, tuple)):
                for x in w:
                    walk(x)
            else:
                flat.append(w)

        walk(list(waits) if isinstance(waits, (list, tuple)) else [waits])
        flat += self.hold[eng]
        self.hold[eng] = []
        for w in flat:
            w.needed = True
        op = Op(eng, fn, flat, dma)
        if dma is not None:
            self.dma_count[dma] = self.dma_count.get(dma, 0) + 16
            op.sem, op.val = dma, self.dma_count[dma]
        self.q[eng].append(op)
        return op

    def last(self):
        return [next(o for o in reversed(self.q[e]) if o.dma is None)
                for e in ("tensor", "vector", "scalar", "gpsimd")
                if any(o.dma is None for o in self.q[e])]

    def barrier(self):
        ends = self.last()
        for e in ("tensor", "vector", "scalar", "gpsimd"):
            self.hold[e] = self.hold[e] + ends
        return ends

    def number(self, sems):
        for e in ENGINES:
            n = 0
            for op in self.q[e]:
                if op.dma is None and op.needed:
                    n += 1
                    op.sem, op.val = sems[e], n

    def write(self, name, eng):
        seen = {}
        for op in self.q[name]:
            need = {}
            for w in op.waits:
                need[w.sem] = max(need.get(w.sem, 0), w.val)
            for s, v in need.items():
                if seen.get(s, 0) < v:
                    eng.wait_ge(s, v)
                    seen[s] = v
            ins = op.fn(eng)
            if op.dma is not None:
                ins.then_inc(op.dma, 16)
            elif op.needed:
                ins.then_inc(op.sem, 1)

D = 1024
T = 256
KC = 8
SLOT = 528 * 8
NSLOT = 4
EPS = 1e-6
LN_EPS = 1e-5
ALPHA = 4.0 ** 0.25
FF = 2816
FE = 3584
NE = 8
BIG = 1e30


def constants():
    p = np.arange(128)
    c = {}
    c["ident"] = np.eye(128)
    c["causal"] = p[:, None] <= p[None, :]
    c["glamask"] = (p[:, None] <= p[None, :]) & (p[:, None] // 64 == p[None, :] // 64)
    lev = np.zeros((128, 7, 128))
    for n in range(7):
        b = p >> n
        lev[:, n, :] = (b[None, :] % 2 == 1) & (b[:, None] == b[None, :] - 1)
    c["levels"] = lev.reshape(128, -1)
    dist = np.zeros((128, 256))
    dist[:, :128] = 128 + p[:, None] - p[None, :]
    dist[:, 128:] = np.where(p[:, None] >= p[None, :], p[:, None] - p[None, :], BIG)
    c["dist"] = dist
    dc = np.full((128, 2, 16), BIG)
    for h in range(2):
        t = h * 128 + p
        for n in range(15):
            dc[:, h, n] = np.where(n * 16 + 31 <= t, t - (n * 16 + 15.5), BIG)
    c["distc"] = dc.reshape(128, -1)
    c["blockdiag"] = (p[:, None] // 16 == np.arange(8)[None, :])
    c["cmask"] = np.where(p[:, None] >= p[None, :], 0.0, -BIG)
    half = 8
    inv = np.float32(500000.0) ** (-np.arange(half, dtype=np.float32) / np.float32(half))
    ang = np.arange(T, dtype=np.float32)[None, :] * inv.astype(np.float32)[:, None]
    cos, sin = np.ones((128, T)), np.zeros((128, T))
    perm = np.zeros((128, 128))
    for b in (0, 64):
        cos[b:b + 8] = cos[b + 8:b + 16] = np.cos(ang.astype(np.float32))
        sin[b:b + 8] = -np.sin(ang.astype(np.float32))
        sin[b + 8:b + 16] = np.sin(ang.astype(np.float32))
        for i in range(8):
            perm[b + 8 + i, b + i] = 1
            perm[b + i, b + 8 + i] = 1
    c["cos"], c["sin"], c["perm"] = cos, sin, perm
    e = np.arange(8)
    c["tie"] = np.broadcast_to((e[None, :] < e[:, None]).reshape(1, 64), (128, 64))
    c["reset64"] = np.broadcast_to((np.arange(T) % 64 != 0)[None], (128, T))
    c["reset128"] = np.broadcast_to((np.arange(T) % 128 != 0)[None], (128, T))
    return {k: np.ascontiguousarray(v, dtype=np.float32) for k, v in c.items()}



def program(nc, io, cn, out):
    prog = Program()
    ctx = ExitStack()

    def sb(name, shape, stack=ctx):
        return stack.enter_context(nc.sbuf_tensor(name, list(shape), F32))

    psum = [ctx.enter_context(nc.psum_tensor(f"ps{i}", [128, 512], F32)) for i in range(8)]
    sems = {e: ctx.enter_context(nc.semaphore(f"s_{e}")) for e in ENGINES}

    def dsem(name):
        return ctx.enter_context(nc.semaphore(name))

    def mm(o, lhsT, rhs, start=True, stop=True, w=(), skip=False):
        return prog.add("tensor", lambda e: e.matmul(o, lhsT, rhs, start=start, stop=stop, skip_group_check=skip), w)

    def chain(o, pairs, w=()):
        for i, (a, b) in enumerate(pairs):
            t = mm(o, a, b, i == 0, i == len(pairs) - 1, w if i == 0 else ())
        return t

    def tp(o, i, w=()):
        n = i.shape[0]
        return prog.add("tensor", lambda e: e.transpose(o, i, K["ident"][0:n, 0:n]), w)

    def act(o, i, f, w=(), **kw):
        return prog.add("scalar", lambda e: e.activation(o, i, f, **kw), w)

    def tt(o, a, b, op, w=(), eng="vector"):
        return prog.add(eng, lambda e: e.tensor_tensor(o, a, b, op), w)

    def ts(o, a, s1, op0, s2=None, op1=None, w=(), eng="vector"):
        if op1 is None:
            return prog.add(eng, lambda e: e.tensor_scalar(o, a, s1, None, op0), w)
        return prog.add(eng, lambda e: e.tensor_scalar(o, a, s1, s2, op0, op1), w)

    def stt(o, a, s, b, op0, op1, w=()):
        return prog.add("vector", lambda e: e.scalar_tensor_tensor(o, a, s, b, op0, op1), w)

    def cp(o, i, w=(), eng="vector"):
        if eng == "scalar":
            return act(o, i, AF.Copy, w)
        return prog.add(eng, lambda e: e.tensor_copy(o, i), w)

    def red(o, i, op, w=(), negate=False):
        return prog.add("vector", lambda e: e.tensor_reduce(o, i, AX.X, op, negate=negate), w)

    def recip(o, i, w=()):
        return prog.add("vector", lambda e: e.reciprocal(o, i), w)

    def scan(o, a, b, w=()):
        return prog.add("vector", lambda e: e.tensor_tensor_scan(o, a, b, 0.0, ALU.mult, ALU.add), w)

    def fill(o, v, w=(), eng="gpsimd"):
        return prog.add(eng, lambda e: e.memset(o, v), w)

    def dma(o, i, sem, w=(), eng="sync"):
        return prog.add(eng, lambda e: e.dma_start(o, i), w, dma=sem)

    def lnexp(w=()):
        return prog.add("scalar", lambda e: e.preload_act_table_set("natural_log_exp_and_others"), w)

    def bc(ap, axis, n):
        a = ap.unsqueeze(axis)
        s = list(a.shape)
        s[axis] = n
        return a.to_broadcast(s)

    class Bank:
        def __init__(self, t):
            self.t, self.w = t, []

    class Banks:
        def __init__(self, ts_):
            self.b, self.i = ts_, 0

        def take(self):
            b = self.b[self.i]
            self.i = (self.i + 1) % len(self.b)
            return b

    allbanks = [Bank(t) for t in psum]
    banks = Banks(allbanks)

    slots = sb("slots", [128, NSLOT, SLOT])
    slot_sem = [dsem(f"s_w{i}") for i in range(NSLOT)]
    slot_free = [[] for _ in range(NSLOT)]
    nload = [0]

    class Piece:
        def __init__(self, i, ap, tok):
            self.i, self.ap, self.tok = i, ap, tok

        def done(self, *toks):
            slot_free[self.i] = list(toks)

    def load(src, shape):
        i = nload[0] % NSLOT
        nload[0] += 1
        a, b = shape
        assert slot_free[i] is not None
        v = slots[:, i, 0:a * b].rearrange("p (a b) -> p a b", b=b)
        t = dma(v, src, slot_sem[i], slot_free[i])
        slot_free[i] = None
        return Piece(i, v, t)

    def wcols(w, c0, n):
        return load(w[:, c0:c0 + n].rearrange("(k p) n -> p k n", p=128), (KC, n))

    def wheads(w, c0):
        i = nload[0] % NSLOT
        nload[0] += 1
        v = slots[:, i, 0:KC * 512].rearrange("p (a b) -> p a b", b=512)
        for g in range(2):
            for k in range(KC):
                t = dma(v[:, k, :].rearrange("p (r g d) -> p g r d", g=2, d=64)[:, g, :, :],
                        w[k * 128:(k + 1) * 128, c0 + g * 256:c0 + (g + 1) * 256].rearrange("p (r d) -> p r d", d=64), slot_sem[i], slot_free[i])
        slot_free[i] = None
        return Piece(i, v, t)

    def wrows(w, r0, n):
        return load(w[r0:r0 + n * 128, :].rearrange("(f p) n -> p f n", p=128), (n, D))

    K, Ksh = {}, {}
    s_const = dsem("s_const")
    X = sb("X", [128, 2, D])
    s_x = dsem("s_x")
    t_x = dma(X[:, :, :], io["x"][0].rearrange("(h p) d -> p h d", p=128), s_x)
    rows = sb("rows", [128, 128])

    def const(n, shape=None):
        K[n] = sb("k_" + n, [128, cn[n].shape[1]])
        return dma(K[n][:, :], cn[n], s_const)

    for n in ("ident", "causal", "glamask", "levels", "dist", "distc", "blockdiag", "cmask", "cos", "sin", "perm", "tie", "reset64", "reset128"):
        t_const = const(n)
    ones = sb("ones", [128, 128])
    t_ones = fill(ones[:, :], 1.0)

    vec = {}
    vec_tok = {}
    rows_free = []
    s_rows = dsem("s_rows")

    def vectors(block, parts):
        nonlocal rows_free
        n = sum(s.shape[0] for _, s in parts)
        z = fill(rows[:, :], 0.0, rows_free)
        at = 0
        first = [z]
        for _, s in parts:
            t = dma(rows[at:at + s.shape[0], :], s, s_rows, first, eng="gpsimd")
            at += s.shape[0]
        b = banks.take()
        m = tp(b.t[:, 0:128], rows[:, :], [t, t_const, b.w])
        v = sb("v_" + block, [128, n])
        c = cp(v[:, :], b.t[:, 0:n], [m])
        b.w = [c]
        rows_free = [m]
        at = 0
        for name, s in parts:
            vec[name] = v[:, at:at + s.shape[0]]
            vec_tok[name] = c
            at += s.shape[0]

    def r128(v):
        return v.rearrange("(r p) -> r p", p=128)

    vectors("a", [("c", r128(io["c"][0])), ("hyb_norm", r128(io["hyb_norm"][0])), ("dense_norm", r128(io["dense_norm"][0])),
                  ("ssm_norm", r128(io["ssm_norm"][0])), ("moe_norm", r128(io["moe_norm"][0])),
                  ("gate_norm", r128(io["ssm_gate_norm"][0])), ("conv_b", r128(io["ssm_conv_b"][0])),
                  ("gk_bias", r128(io["gla_gk_bias"][0]))])
    vectors("b", [("conv_w", io["ssm_conv_w"][0].rearrange("j (r p) -> (j r) p", p=128))])
    for l in range(2):
        vectors(f"g{l}", [(f"gconv{l}", io["gdn_conv_w_2"][l].rearrange("j (r p) -> (j r) p", p=128))])
        vectors(f"f{l}", [(f"fconv{l}", io["ffn_conv_w_2"][l][0:2].rearrange("j (r p) -> (j r) p", p=128))])
        vectors(f"h{l}", [(f"fconv2{l}", io["ffn_conv_w_2"][l][2:3].rearrange("j (r p) -> (j r) p", p=128)),
                          (f"fconvb{l}", r128(io["ffn_conv_b_2"][l]))])

    sc = sb("sc", [128, KC])
    with_e = sb("sc_e", [128, KC])
    e0 = lnexp()
    e1 = act(with_e[:, :], vec["c"], AF.Exp, [vec_tok["c"], e0], scale=-1.0)
    a1 = ts(with_e[:, :], with_e[:, :], 1.0, ALU.add, w=[e1])
    a2 = recip(with_e[:, :], with_e[:, :], [a1])
    t_sc = tt(sc[:, :], with_e[:, :], vec["c"], ALU.mult, [a2])

    HT = sb("HT", [128, KC, T])
    xn = sb("xn", [128, 2, D])
    ssq = sb("ssq", [128, 2])
    rst = sb("rst", [128, 2])
    pfirst = ExitStack()
    macc = sb("macc", [128, 3 * D], pfirst)
    macc_free = []
    s_macc = dsem("s_macc")
    mod = {}
    gates = [sb(f"gate{i}", [128, D], pfirst) for i in range(3)]
    gate_free = [[], [], []]
    side = []

    def step(n=1):
        for _ in range(n):
            while side:
                try:
                    next(side[0])
                    break
                except StopIteration:
                    side.pop(0)

    def finish_side():
        while side:
            step()

    s12 = {n: (sb(f"s1_{n}", [128, KC], pfirst), sb(f"s2_{n}", [128, KC], pfirst)) for n in ("hyb", "dense", "ssm", "moe")}

    def adaln(name, slot):
        nonlocal macc_free
        w_, b_ = io[name + "_mod_w"][0], io[name + "_mod_b"]
        z = fill(macc[:, :], 0.0, macc_free)
        t = dma(macc[0:1, :], b_, s_macc, [z], eng="gpsimd")
        for k in range(KC):
            pc = load(w_[k * 128:(k + 1) * 128, :].rearrange("p (a n) -> p a n", a=1), (1, 3 * D))
            t = stt(macc[:, :], pc.ap[:, 0, :], sc[:, k:k + 1], macc[:, :], ALU.mult, ALU.add, [t, pc.tok, t_sc])
            pc.done(t)
            yield
        b = banks.take()
        for i in range(16):
            m = mm(b.t[:, i:i + 1], macc[:, i * 128:(i + 1) * 128], ones[:, 0:1], w=[t, t_ones, b.w])
        s1, s2 = s12[name]
        c2 = cp(s2[:, :], b.t[:, 0:8], [m])
        c1 = stt(s1[:, :], b.t[:, 8:16], 1.0, vec[name + "_norm"], ALU.add, ALU.mult, [m, vec_tok[name + "_norm"]])
        b.w = [c1]
        toks = [c1, c2]
        g = gates[slot]
        for i in range(2):
            b = banks.take()
            m = mm(b.t[:, :], ones[:, :], macc[:, 2 * D + i * 512:2 * D + (i + 1) * 512], w=[b.w])
            b.w = [cp(g[:, i * 512:(i + 1) * 512], b.t[:, :], [m, gate_free[slot]])]
            toks += b.w
        macc_free = [m]
        mod[name] = (s1, s2, g, slot, toks)

    HT_free = []
    xn_free = []
    t_X = [t_x, t_x]

    def rms(dst):
        out_ = []
        for h in range(2):
            q = act(dst[:, h, :], X[:, h, :], AF.Square, [t_X[h], xn_free], accum_out=ssq[:, h:h + 1])
            out_.append(q)
        t = ts(ssq[:, :], ssq[:, :], 1.0 / D, ALU.mult, EPS, ALU.add, w=out_)
        t = act(rst[:, :], ssq[:, :], AF.Ln, [t])
        t = act(rst[:, :], rst[:, :], AF.Exp, [t], scale=-0.5)
        return [ts(dst[:, h, :], X[:, h, :], rst[:, h:h + 1], ALU.mult, w=[t]) for h in range(2)]

    def to_HT(src, toks, s1=None, s2=None, w=()):
        nonlocal HT_free
        res = []
        for k in range(KC):
            b = banks.take()
            for h in range(2):
                m = tp(b.t[:, h * 128:(h + 1) * 128], src[:, h, k * 128:(k + 1) * 128], [toks[h], b.w, t_const])
            if s1 is None:
                c = cp(HT[:, k, :], b.t[:, 0:256], [m, HT_free], eng="scalar" if k % 2 else "vector")
            elif k % 2:
                c = act(HT[:, k, :], b.t[:, 0:256], AF.Identity, [m, HT_free, w], scale=s1[:, k:k + 1], bias=s2[:, k:k + 1])
            else:
                c = ts(HT[:, k, :], b.t[:, 0:256], s1[:, k:k + 1], ALU.mult, s2[:, k:k + 1], ALU.add, w=[m, HT_free, w])
            b.w = [c]
            res.append(c)
        HT_free = []
        return res, m

    def modulated(name):
        nonlocal xn_free
        s1, s2, g, slot, toks = mod[name]
        x2 = rms(xn)
        res, m = to_HT(xn, x2, s1, s2, toks)
        xn_free = [m]
        return res

    def gated_add(bk, name, m):
        s1, s2, g, slot, toks = mod[name]
        last = None
        for h in range(2):
            for i in range(2):
                o = xn[:, h, i * 512:(i + 1) * 512]
                c = tt(o, bk[h][i].t[:, :], g[:, i * 512:(i + 1) * 512], ALU.mult, [m[h][i], toks, xn_free])
                bk[h][i].w = [c]
                last = tt(X[:, h, i * 512:(i + 1) * 512], X[:, h, i * 512:(i + 1) * 512], o, ALU.add, [c])
            t_X[h] = last
        gate_free[slot] = [last]

    def A(o, pc, c0, n, w, rhs=None, lhs=None):
        return chain(o, [(pc.ap[:, k, c0:c0 + n], HT[:, k, :]) for k in range(KC)], [w, pc.tok])

    def Bm(o, pc, c0, n, h, w):
        return chain(o, [(HT[:, k, h * 128:(h + 1) * 128], pc.ap[:, k, c0:c0 + n]) for k in range(KC)], [w, pc.tok])

    def silu_of(o, i, w):
        return act(o, i, AF.Silu, w)

    def project(src, ntile, wmat, toks, w=()):
        bk = [[banks.take() for _ in range(2)] for _ in range(2)]
        m = [[None] * 2 for _ in range(2)]
        for r in range(0, ntile, 4):
            n = min(4, ntile - r)
            pc = wrows(wmat, r * 128, n)
            for f in range(n):
                for h in range(2):
                    for i in range(2):
                        first, lst = r + f == 0, r + f == ntile - 1
                        m[h][i] = mm(bk[h][i].t[:, :], src[:, r + f, h * 128:(h + 1) * 128],
                                     pc.ap[:, f, i * 512:(i + 1) * 512], first, lst,
                                     [pc.tok, toks[r + f]] + (bk[h][i].w if first else []))
            pc.done(m[1][1])
        return bk, m

    def transposed(src, ntile, dst, toks, scale=None, w=()):
        res = []
        for k in range(ntile):
            b = banks.take()
            for h in range(2):
                m = tp(b.t[:, h * 128:(h + 1) * 128], src[:, h, k * 128:(k + 1) * 128], [toks[h], b.w, t_const])
            if scale is None:
                c = cp(dst[:, k, :], b.t[:, 0:256], [m, w], eng="scalar" if k % 2 else "vector")
            elif k % 2:
                c = act(dst[:, k, :], b.t[:, 0:256], AF.Copy, [m, w], scale=scale[:, k:k + 1])
            else:
                c = ts(dst[:, k, :], b.t[:, 0:256], scale[:, k:k + 1], ALU.mult, w=[m, w])
            b.w = [c]
            res.append(c)
        return res

    side.append(adaln("hyb", 0))
    finish_side()
    side.append(adaln("dense", 1))
    ph = ExitStack()
    h = modulated("hyb")
    W = io["hyb_w_in"][0]
    mix = sb("mix", [128, 2, D], ph)
    pn = ph
    ph = ExitStack()
    q2 = sb("q2", [128, 2, T], ph)
    k2 = sb("k2", [128, 2, T], ph)
    va = sb("va", [128, 2, 512], ph)
    rs = sb("rs", [128, 2, 512], ph)
    lrT = sb("lrT", [16, T], ph)
    gku = sb("gku", [16, T], ph)
    s_g = dsem("s_gla")
    t_gku = dma(gku[:, :], io["gla_gk_up"][0], s_g, eng="gpsimd")
    onr = sb("onr", [128, 128], ph)
    t_onr = dma(onr[:, :], io["gla_out_norm"][0].partition_broadcast(128), s_g, eng="gpsimd")
    t_gku = t_onr

    pc = wcols(W, 0, 512)
    tq, tk = [], []
    for f in range(4):
        b = banks.take()
        m = A(b.t[:, 0:256], pc, f * 128, 128, [h, b.w])
        if f < 2:
            c = act(q2[:, f, :], b.t[:, 0:256], AF.Copy, [m], scale=0.125)
            tq.append(c)
        else:
            c = cp(k2[:, f - 2, :], b.t[:, 0:256], [m])
            tk.append(c)
        b.w = [c]
    pc.done(m)
    step()
    pc = wcols(W, 512, 512)
    tv = []
    for hf in range(2):
        b = banks.take()
        m = Bm(b.t[:, :], pc, 0, 512, hf, [h, b.w])
        b.w = [cp(va[:, hf, :], b.t[:, :], [m])]
        tv += b.w
    pc.done(m)
    step()
    pc = wcols(W, 1024, 528)
    b = banks.take()
    m = A(b.t[0:16, 0:256], pc, 0, 16, [h, b.w])
    t_lr = cp(lrT[:, :], b.t[0:16, 0:256], [m])
    b.w = [t_lr]
    tr = []
    for hf in range(2):
        b = banks.take()
        m = Bm(b.t[:, :], pc, 16, 512, hf, [h, b.w])
        b.w = [silu_of(rs[:, hf, :], b.t[:, :], [m])]
        tr += b.w
    pc.done(m)
    step()

    zb = sb("zb", [128, 2, T], ph)
    za = sb("za", [128, 2, T], ph)
    cum = sb("cum", [128, 2, T], ph)
    Eq, Ek, Ee = zb, za, sb("Ee", [128, 2, T], ph)
    be = sb("be", [128, 2, 4], ph)
    dec = sb("dec", [128, 2, 4], ph)
    lnexp()
    bz = banks.take()
    tz = []
    for f in range(2):
        m = mm(bz.t[:, f * 256:(f + 1) * 256], gku[:, f * 128:(f + 1) * 128], lrT[:, :], w=[t_lr, t_gku, bz.w])
    for f in range(2):
        tz.append(ts(zb[:, f, :], bz.t[:, f * 256:(f + 1) * 256], vec["gk_bias"][:, f:f + 1], ALU.add, w=[m, vec_tok["gk_bias"]]))
    bz.w = tz
    t = act(za[:, :, :], zb[:, :, :], AF.Abs, tz)
    t = act(za[:, :, :], za[:, :, :], AF.Exp, [t], scale=-1.0)
    t = act(za[:, :, :], za[:, :, :], AF.Ln, [t], bias=1.0)
    t = stt(zb[:, :, :], zb[:, :, :], 0.0, za[:, :, :], ALU.min, ALU.subtract, [t])
    tcum = [scan(cum[:, f, :], K["reset64"][:, :], zb[:, f, :], [t, t_const]) for f in range(2)]
    ce = cum[:, :, :].rearrange("p f (n c) -> p f n c", c=64)[:, :, :, 63]
    tbe = ts(be[:, :, :], ce, 1.0 / 16, ALU.mult, w=tcum)
    tde = act(dec[:, :, :], be[:, :, :], AF.Exp, [tbe])
    t1 = act(Eq[:, :, :], cum[:, :, :], AF.Exp, tcum, scale=1.0 / 16)
    t2 = act(Ek[:, :, :], cum[:, :, :], AF.Exp, tcum, scale=-1.0 / 16)
    for f in range(2):
        for n in range(4):
            t3 = act(Ee[:, f, n * 64:(n + 1) * 64], cum[:, f, n * 64:(n + 1) * 64], AF.Exp, [tbe], scale=-1.0 / 16, bias=be[:, f, n:n + 1])
    tqd = tt(q2[:, :, :], q2[:, :, :], Eq[:, :, :], ALU.mult, [tq, t1])
    tke = tt(Ee[:, :, :], k2[:, :, :], Ee[:, :, :], ALU.mult, [tk, t3])
    tkd = tt(k2[:, :, :], k2[:, :, :], Ek[:, :, :], ALU.mult, [tke, t2])
    ke = sb("ke", [128, 2, T], ph)
    b = banks.take()
    for hf in range(2):
        for f in range(2):
            m = tp(b.t[:, hf * 256 + f * 128:hf * 256 + (f + 1) * 128], Ee[:, f, hf * 128:(hf + 1) * 128], [tke, b.w])
    tket = cp(ke[:, :, :].rearrange("p a b -> p (a b)"), b.t[:, :], [m])
    b.w = [tket]
    St = sb("St", [128, 3, 2, 128], ph)
    ts_ = None
    tst = []
    for n in range(3):
        hf, r = n // 2, (n % 2) * 64
        b = banks.take()
        for f in range(2):
            for g in range(2):
                hd = f * 2 + g
                m = mm(b.t[g * 64:g * 64 + 64, f * 128:(f + 1) * 128], ke[r:r + 64, hf, f * 128 + g * 64:f * 128 + g * 64 + 64],
                       va[r:r + 64, hf, hd * 128:(hd + 1) * 128], w=[tket, tv, b.w])
        if n == 0:
            ts_ = cp(St[:, 0, :, :], b.t[:, 0:256].rearrange("p (f v) -> p f v", v=128), [m])
        else:
            for f in range(2):
                ts_ = stt(St[:, n, f, :], St[:, n - 1, f, :], dec[:, f, n:n + 1], b.t[:, f * 128:(f + 1) * 128], ALU.mult, ALU.add, [m, tde, ts_])
        b.w = [ts_]
        tst.append(ts_)
    AT = sb("AT", [128, 2, 4, 128], ph)
    tat = []
    for g in range(2):
        b = banks.take()
        for f in range(2):
            for hf in range(2):
                m = mm(b.t[:, (f * 2 + hf) * 128:(f * 2 + hf + 1) * 128], k2[g * 64:g * 64 + 64, f, hf * 128:(hf + 1) * 128],
                       q2[g * 64:g * 64 + 64, f, hf * 128:(hf + 1) * 128], w=[tqd, tkd, b.w])
        c = tt(AT[:, g, :, :], b.t[:, :].rearrange("p (a c) -> p a c", c=128), bc(K["glamask"][:, :], 1, 4), ALU.mult, [m])
        b.w = [c]
        tat.append(c)
    Og = sb("Og", [128, 2, 4, 128], ph)
    to_ = []
    for hf in range(2):
        for g in range(2):
            b = banks.take()
            for f in range(2):
                hd = f * 2 + g
                o = b.t[:, f * 128:(f + 1) * 128]
                m = mm(o, AT[:, g, f * 2 + hf, :], va[:, hf, hd * 128:(hd + 1) * 128], w=[tat, tv, b.w])
                for n in (2 * hf, 2 * hf + 1):
                    if n:
                        r = (n % 2) * 64
                        m = mm(o[r:r + 64, :], q2[g * 64:g * 64 + 64, f, n * 64:(n + 1) * 64], St[g * 64:g * 64 + 64, n - 1, f, :], False, True, [tst], skip=True)
            c = cp(Og[:, hf, :, :].rearrange("p (f g) v -> p g f v", g=2)[:, g, :, :], b.t[:, 0:256].rearrange("p (f v) -> p f v", v=128), [m])
            b.w = [c]
            to_.append(c)
    og3 = Og[:, :, :, :].rearrange("p h a v -> p (h a) v")
    sq = AT[:, :, :, :].rearrange("p g a v -> p (g a) v")
    vs = sb("vs", [128, 8], ph)
    t = tt(sq, og3, og3, ALU.mult, to_)
    t = red(vs[:, :], sq, ALU.add, [t])
    t = ts(vs[:, :], vs[:, :], 1.0 / 128, ALU.mult, EPS, ALU.add, w=[t])
    t = act(vs[:, :], vs[:, :], AF.Ln, [t])
    t = act(vs[:, :], vs[:, :], AF.Exp, [t], scale=-0.5)
    t = tt(og3, og3, bc(vs[:, :], 2, 128), ALU.mult, [t])
    t = tt(og3, og3, bc(onr[:, :], 1, 8), ALU.mult, [t, t_onr])
    t_gla = tt(mix[:, :, 0:512], Og[:, :, :, :].rearrange("p h a v -> p h (a v)"), rs[:, :, :], ALU.mult, [t, tr])

    prog.barrier()
    ph.close()
    ph = pn
    qT = sb("nq", [128, 4, T], ph)
    pc = wheads(W, 1552)
    tnq = []
    for j in range(4):
        b = banks.take()
        m = A(b.t[:, 0:256], pc, j * 128, 128, [h, b.w])
        c = act(qT[:, j, :], b.t[:, 0:256], AF.Copy, [m], scale=0.125)
        b.w = [c]
        tnq.append(c)
    pc.done(m)
    step()
    KCm = [sb(f"kc{j}", [128, 3, T], ph) for j in range(2)]
    kb = [sb(f"kb{j}", [128, T], ph) for j in range(2)]
    vb = [sb(f"vb{j}", [128, 2, 128], ph) for j in range(2)]
    gt = sb("gt", [128, 2, 24], ph)
    pe_sb = sb("pe_sb", [32, 2, 64], ph)
    s_nsa = dsem("s_nsa")
    t_pe = dma(pe_sb[:, :, :], io["nsa_cmp_pe"][0].rearrange("j b d -> b j d"), s_nsa, eng="gpsimd")
    w2 = sb("w2", [128, 2, 2, 64], ph)
    for j in range(2):
        t_w2 = dma(w2[:, j, :, :], io["nsa_cmp_w2"][0][j].rearrange("(c p) d -> p c d", p=128), s_nsa, eng="gpsimd")
    t_pe = t_w2
    pc = wcols(W, 2064, 512)
    tkc = []
    for j in range(2):
        b = banks.take()
        m = A(b.t[:, 0:256], pc, j * 128, 128, [h, b.w])
        z = fill(KCm[j][:, 2, :], 0.0)
        for g in range(2):
            s_ = b.t[g * 64:g * 64 + 64, :]
            c = cp(KCm[j][0:64, g, 0:256], s_[:, 0:256], [m])
            c = cp(KCm[j][64:128, g, 0:255], s_[:, 1:256], [m])
        b.w = [c]
        b2 = banks.take()
        m2 = tp(b2.t[0:64, 0:32], pe_sb[:, j, :], [t_pe, t_w2, t_const, b2.w])
        pv = b2.t[0:64, 0:32].rearrange("p (i two) -> p two i", two=2)
        kv = KCm[j][:, 2, 0:32].rearrange("p (i two) -> p two i", two=2)
        c = cp(kv[0:64, 0, :], pv[:, 0, :], [m2, z])
        c = cp(kv[64:128, 0, :], pv[:, 1, :], [m2, z])
        b2.w = [c]
        tkc.append(c)
    b = banks.take()
    m = A(b.t[:, 0:256], pc, 256, 128, [h, b.w])
    tkb = [cp(kb[0][:, :], b.t[:, 0:256], [m])]
    b.w = [tkb[0]]
    tvb = [[], []]
    for hf in range(2):
        b = banks.take()
        m = Bm(b.t[:, 0:128], pc, 384, 128, hf, [h, b.w])
        b.w = [cp(vb[0][:, hf, :], b.t[:, 0:128], [m])]
        tvb[0] += b.w
    pc.done(m)
    step()
    pc = wcols(W, 2576, 280)
    b = banks.take()
    m = A(b.t[:, 0:256], pc, 0, 128, [h, b.w])
    tkb.append(cp(kb[1][:, :], b.t[:, 0:256], [m]))
    b.w = [tkb[1]]
    tg = []
    for hf in range(2):
        b = banks.take()
        m = Bm(b.t[:, 0:152], pc, 128, 152, hf, [h, b.w])
        c = cp(vb[1][:, hf, :], b.t[:, 0:128], [m])
        tvb[1].append(c)
        c = act(gt[:, hf, :], b.t[:, 128:152], AF.Exp, [c], scale=-1.0)
        b.w = [c]
        tg.append(c)
    pc.done(m)
    step()
    t = ts(gt[:, :, :], gt[:, :, :], 1.0, ALU.add, w=tg)
    t_gt = recip(gt[:, :, :], gt[:, :, :], [t])

    hid = sb("hid", [128, 2, 2, 2, 16], ph)
    hx = sb("hx", [128, 3, 15], ph)
    hb = sb("hb", [128, 1], ph)
    hy = sb("hy", [128, 2, 15], ph)
    hz = sb("hz", [128, 2, 15], ph)
    z = fill(hid[:, :, :, :, :].rearrange("p a b c d -> p (a b c d)"), 0.0)
    thid = []
    tfree = []
    for j in range(2):
        pc = load(io["nsa_cmp_w1"][0][j].rearrange("(i p) n -> p i n", p=128), (16, 256))
        for c_ in range(2):
            b = banks.take()
            rv = KCm[j][:, :, 0:240].rearrange("p g (n s) -> p g n s", s=16)
            pairs = []
            for i in range(16):
                r = KCm[j][:, :, 2 * i:2 * i + 225 - 1]
                ap = list(r.ap)
                r2 = bass.AP(tensor=r.tensor, offset=r.offset, ap=[ap[0], ap[1], [16, 15]])
                pairs.append((pc.ap[:, i, c_ * 128:(c_ + 1) * 128], r2))
            m = chain(b.t[:, 0:45], pairs, [pc.tok, tkc[j], tfree, b.w])
            t = cp(hb[:, :], b.t[:, 30:31], [m, tfree])
            x_ = hx[:, 0:2, :]
            t = ts(x_, b.t[:, 0:30].rearrange("p (g n) -> p g n", n=15), hb[:, 0:1], ALU.add, w=[t, tfree])
            b.w = [t]
            t2 = tt(hy[:, :, :], x_, x_, ALU.mult, [t, tfree])
            t2 = ts(hy[:, :, :], hy[:, :, :], 0.044715, ALU.mult, 1.0, ALU.add, w=[t2])
            t2 = tt(hy[:, :, :], hy[:, :, :], x_, ALU.mult, [t2])
            t2 = act(hz[:, :, :], hy[:, :, :], AF.Exp, [t2, tfree], scale=-2.0 * 0.7978845608028654)
            t2 = ts(hz[:, :, :], hz[:, :, :], 1.0, ALU.add, w=[t2])
            t2 = recip(hz[:, :, :], hz[:, :, :], [t2])
            t2 = tt(hid[:, j, c_, :, 0:15], x_, hz[:, :, :], ALU.mult, [t2, z])
            tfree = [t2]
            thid.append(t2)
        pc.done(m)
        step()
    kcT = sb("kcT", [128, 16], ph)
    b = banks.take()
    for g in range(2):
        m = chain(b.t[g * 64:g * 64 + 64, 0:16], [(w2[:, 0, c_, :], hid[:, 0, c_, g, :]) for c_ in range(2)], [thid, t_w2, b.w])
    t_kcT = cp(kcT[:, :], b.t[:, 0:16], [m])
    b.w = [t_kcT]
    vbd = sb("vbd", [128, 8, 64], ph)
    b = banks.take()
    hrep = sb("hrep", [128, 2, 8, 16], ph)
    for c_ in range(2):
        t = cp(hrep[:, c_, :, :].rearrange("p (g r) n -> p g r n", r=4), bc(hid[:, 1, c_, :, :], 2, 4), [thid])
    m = chain(b.t[:, 0:64], [(hrep[:, c_, :, :].rearrange("p a n -> p (a n)"), w2[:, 1, c_, :]) for c_ in range(2)], [t, t_w2, b.w])
    vct = sb("vct", [128, 64], ph)
    t = cp(vct[:, :], b.t[:, 0:64], [m])
    b.w = [t]
    t_vbd = tt(vbd[:, :, :], bc(vct[:, :], 1, 8), bc(K["blockdiag"][:, :], 2, 64), ALU.mult, [t, t_const])

    nb = sb("nb", [128, 2, 512], ph)
    S = sb("S", [128, 8, 256], ph)
    PT = sb("PT", [128, 8, 2, 128], ph)
    mx = sb("mx", [128, 8], ph)
    sm = sb("sm", [128, 8], ph)
    fac = sb("fac", [128, 8], ph)
    tmp = sb("tmp", [128, 8, 64], ph)
    slope = [2.0 ** -(i + 1) for i in range(8)]
    free_S, free_PT, free_sm, free_tmp = [], [], [], []
    t_nb = [None, None]
    for hf in range(2):
        q_ = slice(hf * 128, hf * 128 + 128)
        Sc = S[:, 0:8, 0:16]
        t = free_S
        bks = []
        for g in range(2):
            b = banks.take()
            for j in range(4):
                m = mm(b.t[:, j * 16:(j + 1) * 16], qT[g * 64:g * 64 + 64, j, q_], kcT[g * 64:g * 64 + 64, :], w=[tnq, t_kcT, b.w])
            for j in range(4):
                hd = g * 4 + j
                c = stt(S[:, hd, 0:16], K["distc"][:, hf * 16:(hf + 1) * 16], -slope[hd], b.t[:, j * 16:(j + 1) * 16], ALU.mult, ALU.add, [m, t])
            b.w = [c]
        t = red(mx[:, :], Sc, ALU.max, [c, free_sm], negate=True)
        t = ts(mx[:, :], mx[:, :], 1e20, ALU.min, w=[t])
        t = tt(Sc, Sc, bc(mx[:, :], 2, 16), ALU.add, [t])
        t = act(Sc, Sc, AF.Exp, [t])
        t2 = red(sm[:, :], Sc, ALU.add, [t])
        t2 = ts(sm[:, :], sm[:, :], 1e-20, ALU.max, w=[t2])
        t2 = recip(sm[:, :], sm[:, :], [t2])
        t_fac = tt(fac[:, :], sm[:, :], gt[:, hf, :].rearrange("p (a c) -> p c a", c=3)[:, 0, :], ALU.mult, [t2, t_gt])
        pcm = sb(f"pcm{hf}", [128, 128], ph)
        t = cp(pcm[:, :].rearrange("p (a n) -> p a n", n=16), Sc, [t])
        free_S = [t]
        b = banks.take()
        m = tp(b.t[:, 0:128], pcm[:, :], [t, b.w])
        t = cp(PT[:, 0, 0, :], b.t[:, 0:128], [m, free_PT])
        b.w = [t]
        b = banks.take()
        m = mm(b.t[:, :], PT[:, 0, 0, :], vbd[:, :, :].rearrange("p a d -> p (a d)"), w=[t, t_vbd, b.w])
        free_PT = [m]
        t = tt(nb[:, hf, :].rearrange("p (a d) -> p a d", d=64), b.t[:, :].rearrange("p (a d) -> p a d", d=64), bc(fac[:, :], 2, 64), ALU.mult, [m, t_fac])
        b.w = [t]
        t_nb[hf] = t
        free_sm = [t]
        nk = (hf + 1) * 128
        for br in range(2):
            per = 512 // nk
            t_p = [None] * 8
            for g in range(2):
                for j0 in range(0, 4, per):
                    b = banks.take()
                    for j in range(j0, j0 + per):
                        m = mm(b.t[:, (j - j0) * nk:(j - j0 + 1) * nk], qT[g * 64:g * 64 + 64, j, q_], kb[br][g * 64:g * 64 + 64, 0:nk], w=[tnq, tkb[br], b.w])
                    for j in range(j0, j0 + per):
                        hd = g * 4 + j
                        c = stt(S[:, hd, 0:nk], K["dist"][:, 256 - nk:256], -slope[hd], b.t[:, (j - j0) * nk:(j - j0 + 1) * nk], ALU.mult, ALU.add, [m, free_S])
                    b.w = [c]
                t = red(mx[:, g * 4:g * 4 + 4], S[:, g * 4:g * 4 + 4, 0:nk], ALU.max, [c, free_sm], negate=True)
                for hd in range(g * 4, g * 4 + 4):
                    t_p[hd] = act(S[:, hd, 0:nk], S[:, hd, 0:nk], AF.Exp, [t, free_sm], bias=mx[:, hd:hd + 1], accum_out=sm[:, hd:hd + 1])
            t2 = recip(sm[:, :], sm[:, :], t_p)
            t_fac = tt(fac[:, :], sm[:, :], gt[:, hf, :].rearrange("p (a c) -> p c a", c=3)[:, br + 1, :], ALU.mult, [t2, t_gt, free_sm])
            t_pt = []
            for hd in range(0, 8, 2):
                b = banks.take()
                for a in range(2):
                    for k in range(hf + 1):
                        m = tp(b.t[:, (a * (hf + 1) + k) * 128:(a * (hf + 1) + k + 1) * 128], S[:, hd + a, k * 128:(k + 1) * 128], [t_p, b.w])
                c = cp(PT[:, hd:hd + 2, 0:hf + 1, :], b.t[:, 0:2 * nk].rearrange("p (a k q) -> p a k q", a=2, q=128), [m, free_PT], eng="scalar" if hd % 4 else "vector")
                b.w = [c]
                t_pt.append(c)
            free_S = [m]
            b = banks.take()
            for hd in range(8):
                g = hd // 4
                m = chain(b.t[:, hd * 64:(hd + 1) * 64], [(PT[:, hd, k, :], vb[br][:, k, g * 64:g * 64 + 64]) for k in range(hf + 1)], [t_pt, tvb[br], b.w])
            free_PT = [m]
            t = tt(tmp[:, :, :], b.t[:, :].rearrange("p (a d) -> p a d", d=64), bc(fac[:, :], 2, 64), ALU.mult, [m, t_fac, free_tmp])
            b.w = [t]
            free_sm = [t]
            dst = nb[:, hf, :] if br == 0 else mix[:, hf, 512:1024]
            t_nb[hf] = tt(dst.rearrange("p (a d) -> p a d", d=64), nb[:, hf, :].rearrange("p (a d) -> p a d", d=64), tmp[:, :, :], ALU.add, [t, t_nb[hf]])
            free_tmp = [t_nb[hf]]
    mixT = sb("mixT", [128, 8, T], ph)
    tm = transposed(mix, 8, mixT, [[t_nb[0], t_gla], [t_nb[1], t_gla]])
    bk, m = project(mixT, 8, io["hyb_w_out"][0], tm)
    gated_add(bk, "hyb", m)
    finish_side()
    prog.barrier()
    ph.close()

    def up(Wg, hT, toks_h, free, nf):
        res = []
        half = nf * 128
        for c0 in range(0, half, 512):
            n = min(512, half - c0)
            pg, pu = wcols(Wg, c0, n), wcols(Wg, half + c0, n)
            for f in range(0, n, 128):
                i = (c0 + f) // 128
                bg, bu = banks.take(), banks.take()
                m1 = A(bg.t[:, 0:256], pg, f, 128, [toks_h, bg.w])
                m2 = A(bu.t[:, 0:256], pu, f, 128, [bu.w])
                s_ = sg[i % 3]
                a = silu_of(s_[0][:, :], bg.t[:, 0:256], [m1, s_[1]])
                bg.w = [a]
                c = tt(hT[:, i, :], s_[0][:, :], bu.t[:, 0:256], ALU.mult, [m2, a, free])
                bu.w = [c]
                s_[1] = [c]
                res.append(c)
            pg.done(m1)
            pu.done(m2)
            step(3)
        return res, m2

    ph = ExitStack()
    sg = [[sb(f"sg{i}", [128, T], ph), []] for i in range(3)]
    hT = sb("hT", [128, 22, T], ph)
    side.append(adaln("ssm", 2))
    side.append(adaln("moe", 0))
    h = modulated("dense")
    t, m = up(io["dense_w_gu"][0], hT, h, [], 22)
    finish_side()
    bk, m = project(hT, 22, io["dense_w_down"][0], t)
    gated_add(bk, "dense", m)
    prog.barrier()
    ph.close()

    ph = ExitStack()
    W = io["ssm_w_in"][0]
    zs = sb("zs", [128, 2, 2048], ph)
    xt = sb("xt", [128, 2, 2048], ph)
    BC = sb("BC", [128, 8, T], ph)
    cv = [[sb(f"cv{i}", [128, T], ph), []] for i in range(3)]
    xs = [[sb(f"xs{i}", [128, T], ph), []] for i in range(2)]
    dcol = sb("dcol", [32, 4], ph)
    drow = sb("drow", [128, 32], ph)
    s_m = dsem("s_mamba")
    for i, n in enumerate(("ssm_dt_bias", "ssm_a_log")):
        dma(dcol[:, i:i + 1], io[n][0].rearrange("(p a) -> p a", a=1), s_m, prog.last(), eng="gpsimd")
    t_dc = dma(drow[:, :], io["ssm_d"][0].partition_broadcast(128), s_m, eng="gpsimd")
    h = modulated("ssm")
    pc = wcols(W, 5120, 32)
    b = banks.take()
    m = A(b.t[0:32, 0:256], pc, 0, 32, [h, b.w])
    pc.done(m)
    dtT = sb("dtT", [32, T], ph)
    daT = sb("daT", [32, T], ph)
    cmT = sb("cmT", [32, T], ph)
    lnexp()
    t1 = ts(dtT[:, :], b.t[0:32, 0:256], dcol[:, 0:1], ALU.add, w=[m, t_dc])
    b.w = [t1]
    t = act(daT[:, :], dtT[:, :], AF.Abs, [t1])
    t = act(daT[:, :], daT[:, :], AF.Exp, [t], scale=-1.0)
    t = act(daT[:, :], daT[:, :], AF.Ln, [t], bias=1.0)
    t_dt = stt(dtT[:, :], dtT[:, :], 0.0, daT[:, :], ALU.max, ALU.add, [t])
    t2 = act(dcol[:, 2:3], dcol[:, 1:2], AF.Exp, [t_dc])
    t = ts(daT[:, :], dtT[:, :], dcol[:, 2:3], ALU.mult, -1.0, ALU.mult, w=[t2, t_dt])
    onesr = sb("onesr", [32, T], ph)
    z = fill(onesr[:, :], 1.0)
    t_cm = scan(cmT[:, :], onesr[:, :], daT[:, :], [t, z])
    dtc = sb("dtc", [128, 2, 32], ph)
    cmc = sb("cmc", [128, 2, 32], ph)
    b = banks.take()
    for hf in range(2):
        m = tp(b.t[:, hf * 32:hf * 32 + 32], dtT[:, hf * 128:(hf + 1) * 128], [t_dt, b.w])
    for hf in range(2):
        m = tp(b.t[:, 64 + hf * 32:96 + hf * 32], cmT[:, hf * 128:(hf + 1) * 128], [t_cm])
    cp(dtc[:, :, :].rearrange("p a b -> p (a b)"), b.t[:, 0:64], [m])
    t_cols = cp(cmc[:, :, :].rearrange("p a b -> p (a b)"), b.t[:, 64:128])
    b.w = [t_cols]
    tz = []
    for c0 in range(0, 2048, 512):
        pc = wcols(W, c0, 512)
        for hf in range(2):
            b = banks.take()
            m = Bm(b.t[:, :], pc, 0, 512, hf, [h, b.w])
            b.w = [silu_of(zs[:, hf, c0:c0 + 512], b.t[:, :], [m])]
            tz.append(b.w[0])
        pc.done(m)
    t_x2, t_bc = [], []
    cw, cb = vec["conv_w"], vec["conv_b"]
    for r in range(24):
        if r % 4 == 0:
            pc = wcols(W, 2048 + r * 128, 512)
        b = banks.take()
        m = A(b.t[:, 0:256], pc, (r % 4) * 128, 128, [h, b.w])
        if r % 4 == 3:
            pc.done(m)
        c_, x_ = cv[r % 3], xs[r % 2]
        t = act(c_[0][:, :], b.t[:, 0:256], AF.Identity, [m, c_[1], vec_tok["conv_w"], vec_tok["conv_b"]], scale=cw[:, 72 + r:73 + r], bias=cb[:, r:r + 1])
        for j in (2, 1, 0):
            n = 3 - j
            t = stt(c_[0][:, n:T], b.t[:, 0:T - n], cw[:, j * 24 + r:j * 24 + r + 1], c_[0][:, n:T], ALU.mult, ALU.add, [t])
        b.w = [t]
        if r < 16:
            t = silu_of(x_[0][:, :], c_[0][:, :], [t, x_[1]])
            c_[1] = [t]
            b = banks.take()
            for hf in range(2):
                m2 = tp(b.t[:, hf * 128:(hf + 1) * 128], x_[0][:, hf * 128:(hf + 1) * 128], [t, b.w])
            x_[1] = [m2]
            b.w = [cp(xt[:, :, r * 128:(r + 1) * 128], b.t[:, 0:256].rearrange("p (h n) -> p h n", h=2), [m2], eng="scalar" if r % 2 else "vector")]
            t_x2.append(b.w[0])
        else:
            t = silu_of(BC[:, r - 16, :], c_[0][:, :], [t])
            c_[1] = [t]
            t_bc.append(t)
    lnexp()
    CB = sb("CB", [128, 4, 384], ph)
    t_cb = []
    for g in range(4):
        b = banks.take()
        mm(b.t[:, 0:256], BC[:, g, 0:128], BC[:, 4 + g, :], w=[t_bc, b.w])
        m = mm(b.t[:, 256:384], BC[:, g, 128:256], BC[:, 4 + g, 128:256])
        c = tt(CB[:, g, 0:128], b.t[:, 0:128], K["causal"][:, :], ALU.mult, [m, t_const])
        c = cp(CB[:, g, 128:256], b.t[:, 128:256])
        c = tt(CB[:, g, 256:384], b.t[:, 256:384], K["causal"][:, :], ALU.mult)
        b.w = [c]
        t_cb.append(c)
    EB = [[sb(f"eb{i}", [128, 384], ph), []] for i in range(4)]
    xd = [[sb(f"xd{i}", [128, 512], ph), []] for i in range(2)]
    ys = sb("ys", [128, 8], ph)
    t_y = []
    rowbanks = Banks(allbanks[0:4])
    ybanks = Banks(allbanks[4:8])
    for g in range(4):
        yb = [ybanks.take() for _ in range(2)]
        for r in range(8):
            hd = g * 8 + r
            e_ = EB[hd % 4]
            b = rowbanks.take()
            m = mm(b.t[:, 0:256], K["ident"][0:32, hd:hd + 1].to_broadcast([32, 128]), cmT[:, :], w=[t_cm, b.w])
            t = ts(e_[0][:, 0:256], b.t[:, 0:256], cmc[:, 0, hd:hd + 1], ALU.subtract, 0.0, ALU.min, w=[m, t_cols, e_[1]])
            t = ts(e_[0][:, 256:384], b.t[:, 128:256], cmc[:, 1, hd:hd + 1], ALU.subtract, 0.0, ALU.min)
            b.w = [t]
            t = act(e_[0][:, :], e_[0][:, :], AF.Exp, [t])
            t = stt(e_[0][:, 0:256], e_[0][:, 0:256], dtc[:, 0, hd:hd + 1], CB[:, g, 0:256], ALU.mult, ALU.mult, [t, t_cb])
            t = stt(e_[0][:, 256:384], e_[0][:, 256:384], dtc[:, 1, hd:hd + 1], CB[:, g, 256:384], ALU.mult, ALU.mult)
            c0 = hd * 64
            m0 = mm(yb[0].t[:, r * 64:(r + 1) * 64], e_[0][:, 0:128], xt[:, 0, c0:c0 + 64], w=[t, t_x2, yb[0].w])
            m1 = chain(yb[1].t[:, r * 64:(r + 1) * 64], [(e_[0][:, 128:256], xt[:, 0, c0:c0 + 64]), (e_[0][:, 256:384], xt[:, 1, c0:c0 + 64])], [yb[1].w])
            e_[1] = [m1]
        for hf in range(2):
            x_ = xd[hf]
            sl = slice(g * 512, (g + 1) * 512)
            t = tt(x_[0][:, :].rearrange("p (r d) -> p r d", d=64), xt[:, hf, sl].rearrange("p (r d) -> p r d", d=64),
                   bc(drow[:, g * 8:g * 8 + 8], 2, 64), ALU.mult, [x_[1], t_x2, t_dc], eng="gpsimd")
            t = tt(x_[0][:, :], yb[hf].t[:, :], x_[0][:, :], ALU.add, [t, m1])
            yb[hf].w = [t]
            t = tt(zs[:, hf, sl], zs[:, hf, sl], x_[0][:, :], ALU.mult, [t, tz], eng="gpsimd")
            a = act(x_[0][:, :], zs[:, hf, sl], AF.Square, [t], accum_out=ys[:, hf * 4 + g:hf * 4 + g + 1])
            x_[1] = [a]
            t_y.append(a)
    t = ts(ys[:, :], ys[:, :], 1.0 / 512, ALU.mult, EPS, ALU.add, w=t_y)
    t = act(ys[:, :], ys[:, :], AF.Ln, [t])
    t = act(ys[:, :], ys[:, :], AF.Exp, [t], scale=-0.5)
    tn = []
    for hf in range(2):
        for g in range(4):
            c = ts(zs[:, hf, g * 512:(g + 1) * 512], zs[:, hf, g * 512:(g + 1) * 512], ys[:, hf * 4 + g:hf * 4 + g + 1], ALU.mult, w=[t])
        tn.append(c)
    yT = xt[:, :, :].rearrange("p h (a t) -> p (h a) t", t=T)
    ty = transposed(zs, 16, yT, tn, vec["gate_norm"], [m1, t_y])
    bk, m = project(yT, 16, io["ssm_w_out"][0], ty)
    gated_add(bk, "ssm", m)
    prog.barrier()
    ph.close()

    ph = ExitStack()
    sg = [[sb(f"eg{i}", [128, T], ph), []] for i in range(3)]
    hT = sb("ehT", [128, 28, T], ph)
    acc = sb("eacc", [128, 2, D], ph)
    rw = sb("rw", [128, KC, NE], ph)
    s_r = dsem("s_router")
    t_rw = dma(rw[:, :, :], io["moe_router"][0].rearrange("(k p) e -> p k e", p=128), s_r, prog.last(), eng="gpsimd")
    h = modulated("moe")
    L = sb("L", [128, 2, NE], ph)
    gt = sb("egate", [128, 2, NE], ph)
    pr = sb("pr", [128, 2, 64], ph)
    e1_ = sb("e1_", [128, 2], ph)
    b = banks.take()
    for hf in range(2):
        m = chain(b.t[:, hf * 8:hf * 8 + 8], [(HT[:, k, hf * 128:(hf + 1) * 128], rw[:, k, :]) for k in range(KC)], [h, t_rw, b.w])
    t_L = cp(L[:, :, :].rearrange("p h e -> p (h e)"), b.t[:, 0:16], [m])
    b.w = [t_L]
    t_gate = []
    for hf in range(2):
        p1 = pr[:, 0, :].rearrange("p (e j) -> p e j", j=8)
        p2 = pr[:, 1, :].rearrange("p (e j) -> p e j", j=8)
        lj, le = bc(L[:, hf, :], 1, 8), bc(L[:, hf, :], 2, 8)
        t = tt(p1, lj, le, ALU.is_equal, [t_L, t_gate])
        t = tt(pr[:, 0, :], pr[:, 0, :], K["tie"][:, :], ALU.mult, [t, t_const])
        t2 = tt(p2, lj, le, ALU.is_gt, [t_L, t_gate])
        t = tt(p1, p1, p2, ALU.add, [t, t2])
        t = red(gt[:, hf, :], p1, ALU.add, [t])
        t = ts(gt[:, hf, :], gt[:, hf, :], 1.5, ALU.is_lt, w=[t])
        t3 = red(e1_[:, hf:hf + 1], L[:, hf, :], ALU.max, [t_L], negate=True)
        t3 = act(L[:, hf, :], L[:, hf, :], AF.Exp, [t3, t2], bias=e1_[:, hf:hf + 1])
        t = tt(gt[:, hf, :], gt[:, hf, :], L[:, hf, :], ALU.mult, [t, t3])
        t = red(e1_[:, hf:hf + 1], gt[:, hf, :], ALU.add, [t])
        t = recip(e1_[:, hf:hf + 1], e1_[:, hf:hf + 1], [t])
        t_gate.append(ts(gt[:, hf, :], gt[:, hf, :], e1_[:, hf:hf + 1], ALU.mult, w=[t]))
    free = []
    t_acc = [[None, None], [None, None]]
    for e in range(NE):
        t, m = up(io["moe_w_gu"][0][e], hT, h, free, 28)
        bk, m = project(hT, 28, io["moe_w_down"][0][e], t)
        free = [m[1][1]]
        for hf in range(2):
            for i in range(2):
                o = acc[:, hf, i * 512:(i + 1) * 512]
                if e == 0:
                    c = ts(o, bk[hf][i].t[:, :], gt[:, hf, 0:1], ALU.mult, w=[m[hf][i], t_gate])
                else:
                    c = stt(o, bk[hf][i].t[:, :], gt[:, hf, e:e + 1], o, ALU.mult, ALU.add, [m[hf][i], t_acc[hf][i]])
                bk[hf][i].w = [c]
                t_acc[hf][i] = c
    s1, s2, g, slot, toks = mod["moe"]
    for hf in range(2):
        t = tt(acc[:, hf, :], acc[:, hf, :], g[:, :], ALU.mult, t_acc[hf])
        t_X[hf] = tt(X[:, hf, :], X[:, hf, :], acc[:, hf, :], ALU.add, [t])
    fr = acc[:, 0, :]
    fn_ = sb("fn", [128, D], ph)
    t_fn = dma(fn_[:, :], io["final_norm"].partition_broadcast(128), dsem("s_fn"), prog.last(), eng="gpsimd")
    t2 = rms(xn)
    t_X = [tt(X[:, hf, :], xn[:, hf, :], fn_[:, :], ALU.mult, [t2[hf], t_fn]) for hf in range(2)]
    xn_free = t_X
    prog.barrier()
    ph.close()

    pfirst.close()
    for l in range(2):
        ph = ExitStack()
        Wl = io["w_in_2"][l]
        lnr = sb(f"lnr{l}", [128, 4, D], ph)
        s_l = dsem(f"s_ln{l}")
        lt = []
        for i, n in enumerate(("ln1_g_2", "ln1_b_2", "ln2_g_2", "ln2_b_2")):
            dma(lnr[:, i, :], io[n][l].partition_broadcast(128), s_l, prog.last() if i == 0 else (), eng="gpsimd")
        hcol = sb(f"hcol{l}", [64, 4], ph)
        for i, n in enumerate(("gdn_dt_bias_2", "gdn_a_log_2")):
            dma(hcol[0:4, i:i + 1], io[n][l].rearrange("(p a) -> p a", a=1), s_l, eng="gpsimd")
        gnr = sb(f"gnr{l}", [128, 128], ph)
        t_l = dma(gnr[:, :], io["gdn_norm_g_2"][l].partition_broadcast(128), s_l, eng="gpsimd")
        st = sb(f"st{l}", [128, 2, 2, 6], ph)
        mv = sb(f"mv{l}", [128, 2, 2], ph)
        rs_ = sb(f"rs_{l}", [128, 2], ph)
        pm = ExitStack()
        mix = sb(f"mix{l}", [128, 2, D], pm)
        pg = ExitStack()
        h, m = to_HT(X, t_X)
        qk = sb(f"qk{l}", [128, 12, T], pg)
        cv = [[sb(f"gcv{l}{i}", [128, T], pg), []] for i in range(3)]
        gcw = vec[f"gconv{l}"]
        tc = []
        for r in range(12):
            if r % 4 == 0:
                pc = wcols(Wl, r * 128, 512)
            b = banks.take()
            m = A(b.t[:, 0:256], pc, (r % 4) * 128, 128, [h, b.w])
            if r % 4 == 3:
                pc.done(m)
            c_ = cv[r % 3]
            t = act(c_[0][:, :], b.t[:, 0:256], AF.Copy, [m, c_[1], vec_tok[f"gconv{l}"]], scale=gcw[:, 36 + r:37 + r])
            for j in (2, 1, 0):
                n = 3 - j
                t = stt(c_[0][:, n:T], b.t[:, 0:T - n], gcw[:, j * 12 + r:j * 12 + r + 1], c_[0][:, n:T], ALU.mult, ALU.add, [t])
            b.w = [t]
            t = silu_of(qk[:, r, :], c_[0][:, :], [t])
            c_[1] = [t]
            tc.append(t)
        zsl = sb(f"zsl{l}", [128, 2, 512], pg)
        pc = wcols(Wl, 1536, 520)
        bab = banks.take()
        A(bab.t[0:4, 0:256], pc, 0, 4, [h, bab.w])
        m_ab = A(bab.t[32:36, 0:256], pc, 4, 4, [h])
        tz = []
        for hf in range(2):
            b = banks.take()
            m = Bm(b.t[:, :], pc, 8, 512, hf, [h, b.w])
            b.w = [silu_of(zsl[:, hf, :], b.t[:, :], [m])]
            tz.append(b.w[0])
        pc.done(m)
        lnexp()
        gb = sb(f"gb{l}", [64, T], pg)
        ga = sb(f"ga{l}", [64, T], pg)
        z = fill(gb[:, :], 0.0)
        t1 = ts(ga[0:4, :], bab.t[0:4, 0:256], hcol[0:4, 0:1], ALU.add, w=[m_ab, t_l])
        t2 = act(ga[32:36, :], bab.t[32:36, 0:256], AF.Exp, [m_ab, t1], scale=-1.0)
        bab.w = [t2]
        gc = sb(f"gc{l}", [4, T], pg)
        t = act(gc[:, :], ga[0:4, :], AF.Abs, [t1])
        t = act(gc[:, :], gc[:, :], AF.Exp, [t], scale=-1.0)
        t = act(gc[:, :], gc[:, :], AF.Ln, [t], bias=1.0)
        t = stt(ga[0:4, :], ga[0:4, :], 0.0, gc[:, :], ALU.max, ALU.add, [t])
        t3 = act(hcol[0:4, 2:3], hcol[0:4, 1:2], AF.Exp, [t_l])
        t = ts(ga[0:4, :], ga[0:4, :], hcol[0:4, 2:3], ALU.mult, -1.0, ALU.mult, w=[t, t3])
        t4 = scan(gb[0:4, :], K["reset128"][0:4, :], ga[0:4, :], [t, z, t_const])
        t = ts(ga[32:36, :], ga[32:36, :], 1.0, ALU.add, w=[t2])
        t5 = recip(gb[32:36, :], ga[32:36, :], [t, z])
        col = sb(f"col{l}", [128, 2, 64], pg)
        b = banks.take()
        for hf in range(2):
            m = tp(b.t[:, hf * 64:hf * 64 + 64], gb[:, hf * 128:(hf + 1) * 128], [t4, t5, b.w])
        t_col = cp(col[:, :, :].rearrange("p h c -> p (h c)"), b.t[:, 0:128], [m])
        b.w = [t_col]
        eg = sb(f"eg_{l}", [128, 8], pg)
        nbe = sb(f"nbe{l}", [128, 4], pg)
        t_eg = act(eg[:, :].rearrange("p (h a) -> p h a", h=2), col[:, :, 0:4], AF.Exp, [t_col])
        t_nbe = stt(nbe[:, :], eg[:, 4:8], -1.0, col[:, 1, 32:36], ALU.mult, ALU.mult, [t_eg])
        sq = sb(f"sq{l}", [128, 8, T], pg)
        t_qk = []
        for j in range(4):
            r = 2 * j
            t = tt(sq[:, r:r + 2, :], qk[:, r:r + 2, :], qk[:, r:r + 2, :], ALU.mult, tc)
            b = banks.take()
            for a in range(2):
                m = mm(b.t[:, a * 256:(a + 1) * 256], ones[:, :], sq[:, r + a, :], w=[t, t_ones, b.w])
            sv = sq[:, r:r + 2, :].rearrange("p a t -> p (a t)")
            t = ts(sv, b.t[:, :], EPS, ALU.add, w=[m])
            b.w = [t]
            t = act(sv, sv, AF.Ln, [t])
            t = act(sv, sv, AF.Exp, [t], scale=-0.5)
            qv = qk[:, r:r + 2, :].rearrange("p a t -> p (a t)")
            if j < 2:
                t_qk.append(stt(qv, qv, 128 ** -0.5, sv, ALU.mult, ALU.mult, [t]))
            else:
                t_qk.append(tt(qv, qv, sv, ALU.mult, [t]))
        vtm = sb(f"vtm{l}", [128, 2, 4, 128], pg)
        kd = sb(f"kd{l}", [128, 4, 128], pg)
        t_v = []
        for hf in range(2):
            b = banks.take()
            for a in range(4):
                m = tp(b.t[:, a * 128:(a + 1) * 128], qk[:, 8 + a, hf * 128:(hf + 1) * 128], [tc, b.w])
            c = tt(vtm[:, hf, :, :], b.t[:, :].rearrange("p (a d) -> p a d", d=128), bc(col[:, hf, 32:36], 2, 128), ALU.mult, [m, t_col])
            b.w = [c]
            t_v.append(c)
        DT = sb(f"DT{l}", [128, 8, 128], pg)
        ATb = sb(f"ATb{l}", [128, 8, 128], pg)
        AAb = sb(f"AAb{l}", [128, 8, 128], pg)
        t_dt, t_att, t_aa = [], [], []
        t_bt = []
        brow = sq[:, 0:4, :]
        for a in range(4):
            b = banks.take()
            m1 = mm(b.t[:, 0:256], K["ident"][0:64, a:a + 1].to_broadcast([64, 128]), gb[:, :], w=[t4, t5, t_const, b.w])
            m1 = mm(b.t[:, 256:512], K["ident"][0:64, 32 + a:33 + a].to_broadcast([64, 128]), gb[:, :])
            for c_ in range(2):
                t = ts(DT[:, c_ * 4 + a, :], b.t[:, c_ * 128:(c_ + 1) * 128], col[:, c_, a:a + 1], ALU.subtract, 0.0, ALU.min, w=[m1, t_col])
            t_bt.append(cp(brow[:, a, :], b.t[:, 256:512], [t_qk]))
            b.w = [t_bt[-1]]
            t_dt.append(t)
        t_dx = act(DT[:, :, :], DT[:, :, :], AF.Exp, t_dt)
        b = banks.take()
        for a in range(4):
            m = tp(b.t[:, a * 128:(a + 1) * 128], qk[:, 4 + a, 0:128], [t_qk, b.w])
        t_kd = tt(kd[:, :, :], b.t[:, :].rearrange("p (a d) -> p a d", d=128), bc(DT[:, 0:4, 127], 2, 128), ALU.mult, [m, t_dx])
        b.w = [t_kd]
        t_dm = tt(DT[:, :, :], DT[:, :, :], bc(K["causal"][:, :], 1, 8), ALU.mult, [t_dx, t_kd])
        for c_ in range(2):
            s_ = slice(c_ * 128, (c_ + 1) * 128)
            b, b2 = banks.take(), banks.take()
            for a in range(4):
                m = mm(b.t[:, a * 128:(a + 1) * 128], qk[:, 4 + a, s_], qk[:, a, s_], w=[t_qk, b.w])
            for a in range(4):
                m2 = mm(b2.t[:, a * 128:(a + 1) * 128], qk[:, 4 + a, s_], qk[:, 4 + a, s_], w=[b2.w])
            dv = DT[:, c_ * 4:c_ * 4 + 4, :].rearrange("p a i -> p (a i)")
            c = tt(ATb[:, c_ * 4:c_ * 4 + 4, :].rearrange("p a i -> p (a i)"), b.t[:, :], dv, ALU.mult, [m, t_dm])
            b.w = [c]
            t_att.append(c)
            av = AAb[:, c_ * 4:c_ * 4 + 4, :]
            c = tt(av.rearrange("p a i -> p (a i)"), b2.t[:, :], dv, ALU.mult, [m2, t_dm])
            b2.w = [c]
            t_aa.append(tt(av, av, brow[:, :, s_], ALU.mult, [c, t_bt]))
        Xi = sb(f"Xi{l}", [128, 8, 128], pg)
        Xt = sb(f"Xt{l}", [128, 8, 128], pg)
        Ci = sb(f"Ci{l}", [128, 8, 128], pg)
        Pi = DT
        t_X0, t_Xt, t_P = [None, None], [None, None], [None, None]
        free_C, free_P = [None, None], [None, None]
        for n in range(7):
            lm = K["levels"][:, n * 128:(n + 1) * 128]
            for c_ in range(2):
                s_ = slice(c_ * 4, c_ * 4 + 4)
                fl = lambda z_: z_[:, s_, :].rearrange("p a i -> p (a i)")
                t_c = tt(Ci[:, s_, :], AAb[:, s_, :], bc(lm, 1, 4), ALU.mult, [t_aa, free_C[c_]], eng="gpsimd")
                b = banks.take()
                for a in range(4):
                    i = c_ * 4 + a
                    m = mm(b.t[:, a * 128:(a + 1) * 128], Ci[:, i, :], K["ident"][:, :] if n == 0 else Xi[:, i, :], w=[t_c, b.w, t_X0[c_]])
                free_C[c_] = [m]
                idb = bc(K["ident"][:, :], 1, 4)
                if n == 0:
                    c = tt(Xi[:, s_, :], idb, b.t[:, :].rearrange("p (a i) -> p a i", i=128), ALU.subtract, [m])
                    b.w = [c]
                    t_X0[c_] = c
                    t_Xt[c_] = tt(Xt[:, s_, :], idb, Ci[:, s_, :], ALU.subtract, [t_c])
                    free_C[c_] = [m, t_Xt[c_]]
                    continue
                t_P[c_] = cp(fl(Pi), b.t[:, :], [m, free_P[c_], t_aa, t_att], eng="scalar")
                b.w = [t_P[c_]]
                if n < 6:
                    b = banks.take()
                    for a in range(4):
                        i = c_ * 4 + a
                        m = mm(b.t[:, a * 128:(a + 1) * 128], Xt[:, i, :], Pi[:, i, :], w=[t_P[c_], t_Xt[c_], b.w])
                    t_X0[c_] = tt(fl(Xi), fl(Xi), b.t[:, :], ALU.subtract, [m])
                    b.w = [t_X0[c_]]
                b = banks.take()
                for a in range(4):
                    i = c_ * 4 + a
                    m = mm(b.t[:, a * 128:(a + 1) * 128], Pi[:, i, :], Xt[:, i, :], w=[t_P[c_], t_Xt[c_], b.w])
                t_Xt[c_] = tt(fl(Xt), fl(Xt), b.t[:, :], ALU.subtract, [m])
                b.w = [t_Xt[c_]]
                free_P[c_] = [m]
        U = sb(f"U{l}", [128, 2, 4, 128], pg)
        S1 = sb(f"S1{l}", [128, 4, 128], pg)
        Og = sb(f"Ogd{l}", [128, 2, 4, 128], pg)
        f4 = lambda z_: z_.rearrange("p a d -> p (a d)")

        def four(fl_, fr_, w):
            b = banks.take()
            for a in range(4):
                m = mm(b.t[:, a * 128:(a + 1) * 128], fl_(a), fr_(a), w=[w, b.w])
            return b, m

        b, m = four(lambda a: Xt[:, a, :], lambda a: vtm[:, 0, a, :], [t_Xt[0], t_v])
        tu = cp(f4(U[:, 0, :, :]), b.t[:, :], [m])
        b.w = [tu]
        b, m = four(lambda a: kd[:, a, :], lambda a: U[:, 0, a, :], [tu, t_kd])
        tS = cp(f4(S1[:, :, :]), b.t[:, :], [m])
        b.w = [tS]
        b, m = four(lambda a: ATb[:, a, :], lambda a: U[:, 0, a, :], [t_att])
        to0 = cp(f4(Og[:, 0, :, :]), b.t[:, :], [m], eng="scalar")
        b.w = [to0]
        b, m = four(lambda a: qk[:, 4 + a, 128:256], lambda a: S1[:, a, :], [tS])
        for a in range(4):
            tr_ = stt(vtm[:, 1, a, :], b.t[:, a * 128:(a + 1) * 128], nbe[:, a:a + 1], vtm[:, 1, a, :], ALU.mult, ALU.add, [m, t_nbe])
        b.w = [tr_]
        bq, mq = four(lambda a: qk[:, a, 128:256], lambda a: S1[:, a, :], [])
        b, m = four(lambda a: Xt[:, 4 + a, :], lambda a: vtm[:, 1, a, :], [tr_, t_Xt[1]])
        tu = cp(f4(U[:, 1, :, :]), b.t[:, :], [m])
        b.w = [tu]
        b, m = four(lambda a: ATb[:, 4 + a, :], lambda a: U[:, 1, a, :], [tu])
        tc1 = cp(f4(Og[:, 1, :, :]), b.t[:, :], [m])
        b.w = [tc1]
        for a in range(4):
            to1 = stt(Og[:, 1, a, :], bq.t[:, a * 128:(a + 1) * 128], eg[:, 4 + a:5 + a], Og[:, 1, a, :], ALU.mult, ALU.add, [mq, tc1])
        bq.w = [to1]
        og3 = Og[:, :, :, :].rearrange("p h a v -> p (h a) v")
        sq3 = U[:, :, :, :].rearrange("p h a v -> p (h a) v")
        vs = sb(f"gvs{l}", [128, 8], pg)
        t = tt(sq3, og3, og3, ALU.mult, [to0, to1, m])
        t = red(vs[:, :], sq3, ALU.add, [t])
        t = ts(vs[:, :], vs[:, :], 1.0 / 128, ALU.mult, EPS, ALU.add, w=[t])
        t = act(vs[:, :], vs[:, :], AF.Ln, [t])
        t = act(vs[:, :], vs[:, :], AF.Exp, [t], scale=-0.5)
        t = tt(og3, og3, bc(vs[:, :], 2, 128), ALU.mult, [t])
        t = tt(og3, og3, bc(gnr[:, :], 1, 8), ALU.mult, [t, t_l])
        t_gdn = tt(mix[:, :, 0:512], Og[:, :, :, :].rearrange("p h a v -> p h (a v)"), zsl[:, :, :], ALU.mult, [t, tz])
        prog.barrier()
        pg.close()
        pg = ExitStack()
        qr = sb(f"qr{l}", [128, 8, T], pg)
        rt = [[sb(f"rt{l}{i}", [128, T], pg), []] for i in range(3)]
        vbt = sb(f"vbt{l}", [128, 2, 512], pg)
        tq = []
        for r in range(8):
            if r % 4 == 0:
                pc = wcols(Wl, 2056 + r * 128, 512)
            b = banks.take()
            m = A(b.t[:, 0:256], pc, (r % 4) * 128, 128, [h, b.w])
            if r % 4 == 3:
                pc.done(m)
            t = act(qr[:, r, :], b.t[:, 0:256], AF.Copy, [m], scale=0.125 if r < 4 else 1.0)
            b.w = [t]
            b = banks.take()
            m = mm(b.t[:, 0:256], K["perm"][:, :], qr[:, r, :], w=[t, t_const, b.w])
            r_ = rt[r % 3]
            t2 = tt(r_[0][:, :], b.t[:, 0:256], K["sin"][:, :], ALU.mult, [m, r_[1]])
            b.w = [t2]
            t = tt(qr[:, r, :], qr[:, r, :], K["cos"][:, :], ALU.mult, [t, m], eng="gpsimd")
            t = tt(qr[:, r, :], qr[:, r, :], r_[0][:, :], ALU.add, [t, t2], eng="gpsimd")
            r_[1] = [t]
            tq.append(t)
        pc = wcols(Wl, 3080, 512)
        tvb = []
        for hf in range(2):
            b = banks.take()
            m = Bm(b.t[:, :], pc, 0, 512, hf, [h, b.w])
            b.w = [cp(vbt[:, hf, :], b.t[:, :], [m])]
            tvb += b.w
        pc.done(m)
        S = sb(f"Sm{l}", [128, 8, 256], pg)
        PT = sb(f"PTm{l}", [128, 8, 2, 128], pg)
        mx = sb(f"mxm{l}", [128, 8], pg)
        sm = sb(f"smm{l}", [128, 8], pg)
        free_S, free_PT, free_sm = [], [], []
        t_mb = []
        for hf in range(2):
            nk = (hf + 1) * 128
            per = 512 // nk
            t_p = [None] * 8
            for g in range(2):
                for j0 in range(0, 4, per):
                    b = banks.take()
                    for j in range(j0, j0 + per):
                        m = mm(b.t[:, (j - j0) * nk:(j - j0 + 1) * nk], qr[g * 64:g * 64 + 64, j, hf * 128:(hf + 1) * 128], qr[g * 64:g * 64 + 64, 4 + j, 0:nk], w=[tq, b.w])
                    sv = S[:, :, :].rearrange("p (j g) k -> p g j k", g=2)[:, g, j0:j0 + per, :]
                    bv = b.t[:, 0:per * nk].rearrange("p (j k) -> p j k", k=nk)
                    c = tt(sv[:, :, nk - 128:nk], bv[:, :, nk - 128:nk], bc(K["cmask"][:, :], 1, per), ALU.add, [m, free_S, t_const])
                    if hf:
                        c = cp(sv[:, :, 0:128], bv[:, :, 0:128], [m, free_S])
                    b.w = [c]
            t = red(mx[:, :], S[:, :, 0:nk], ALU.max, [c, free_sm], negate=True)
            for hd in range(8):
                t_p[hd] = act(S[:, hd, 0:nk], S[:, hd, 0:nk], AF.Exp, [t, free_sm], bias=mx[:, hd:hd + 1], accum_out=sm[:, hd:hd + 1])
            t_s = recip(sm[:, :], sm[:, :], t_p)
            t_pt = []
            for hd in range(0, 8, 2):
                b = banks.take()
                for a in range(2):
                    for k in range(hf + 1):
                        m = tp(b.t[:, (a * (hf + 1) + k) * 128:(a * (hf + 1) + k + 1) * 128], S[:, hd + a, k * 128:(k + 1) * 128], [t_p, b.w])
                c = cp(PT[:, hd:hd + 2, 0:hf + 1, :], b.t[:, 0:2 * nk].rearrange("p (a k q) -> p a k q", a=2, q=128), [m, free_PT], eng="scalar" if hd % 4 else "vector")
                b.w = [c]
                t_pt.append(c)
            free_S = [m]
            b = banks.take()
            for hd in range(8):
                m = chain(b.t[:, hd * 64:(hd + 1) * 64], [(PT[:, hd, k, :], vbt[:, k, hd * 64:(hd + 1) * 64]) for k in range(hf + 1)], [t_pt, tvb, b.w])
            free_PT = [m]
            t = tt(mix[:, hf, 512:1024].rearrange("p (a d) -> p a d", d=64), b.t[:, :].rearrange("p (a d) -> p a d", d=64), bc(sm[:, :], 2, 64), ALU.mult, [m, t_s])
            b.w = [t]
            free_sm = [t]
            t_mb.append(t)
        mixT = qr
        tm = transposed(mix, 8, mixT, [[t_mb[0], t_gdn], [t_mb[1], t_gdn]], w=t_mb)
        bk, m = project(mixT, 8, io["w_out_2"][l], tm)

        def post_norm(bk, m, gi, name):
            tv_ = []
            for hf in range(2):
                for i in range(2):
                    s_ = slice(i * 512, (i + 1) * 512)
                    t = stt(xn[:, hf, s_], X[:, hf, s_], ALPHA, bk[hf][i].t[:, :], ALU.mult, ALU.add, [m[hf][i], t_X[hf], xn_free])
                    bk[hf][i].w = [t]
                    t = prog.add("vector", lambda e, o=st[:, hf, i, :], i_=xn[:, hf, s_]: e.bn_stats(o, i_), [t])
                t = prog.add("vector", lambda e, o=mv[:, hf, :], i_=st[:, hf, :, :].rearrange("p a b -> p (a b)"): e.bn_aggr(o, i_), [t])
                tv_.append(t)
            t = ts(rs_[:, :], mv[:, :, 1], LN_EPS, ALU.add, w=tv_)
            t = act(rs_[:, :], rs_[:, :], AF.Ln, [t])
            t = act(rs_[:, :], rs_[:, :], AF.Exp, [t], scale=-0.5)
            for hf in range(2):
                t2 = ts(xn[:, hf, :], xn[:, hf, :], mv[:, hf, 0:1], ALU.subtract, rs_[:, hf:hf + 1], ALU.mult, w=[t])
                t2 = tt(xn[:, hf, :], xn[:, hf, :], lnr[:, gi, :], ALU.mult, [t2, t_l])
                t_X[hf] = tt(X[:, hf, :], xn[:, hf, :], lnr[:, gi + 1, :], ALU.add, [t2])

        post_norm(bk, m, 0, f"a{l}")
        xn_free = list(t_X)
        prog.barrier()
        pg.close()
        pm.close()
        pf = ExitStack()
        hT = sb(f"fhT{l}", [128, 22, T], pf)
        cg = [[sb(f"cg{l}{i}", [128, T], pf), []] for i in range(3)]
        cu = [[sb(f"cu{l}{i}", [128, T], pf), []] for i in range(3)]
        h, m = to_HT(X, t_X)
        w01, w2_, wb = vec[f"fconv{l}"], vec[f"fconv2{l}"], vec[f"fconvb{l}"]
        vt = [vec_tok[f"fconv{l}"], vec_tok[f"fconv2{l}"]]

        def conv3(dst, b, m, r):
            t = act(dst[0][:, :], b.t[:, 0:256], AF.Identity, [m, dst[1], vt], scale=w2_[:, r:r + 1], bias=wb[:, r:r + 1])
            t = stt(dst[0][:, 1:T], b.t[:, 0:T - 1], w01[:, 44 + r:45 + r], dst[0][:, 1:T], ALU.mult, ALU.add, [t])
            t = stt(dst[0][:, 2:T], b.t[:, 0:T - 2], w01[:, r:r + 1], dst[0][:, 2:T], ALU.mult, ALU.add, [t])
            b.w = [t]
            return t

        th = []
        for c0 in range(0, FF, 512):
            n = min(512, FF - c0)
            p1, p2 = wcols(io["w_up_2"][l], c0, n), wcols(io["w_up_2"][l], FF + c0, n)
            for f in range(0, n, 128):
                i = (c0 + f) // 128
                b1, b2 = banks.take(), banks.take()
                m1 = A(b1.t[:, 0:256], p1, f, 128, [h, b1.w])
                m2 = A(b2.t[:, 0:256], p2, f, 128, [b2.w])
                t1 = conv3(cg[i % 3], b1, m1, i)
                t2 = conv3(cu[i % 3], b2, m2, 22 + i)
                t = silu_of(cg[i % 3][0][:, :], cg[i % 3][0][:, :], [t1])
                t = tt(hT[:, i, :], cg[i % 3][0][:, :], cu[i % 3][0][:, :], ALU.mult, [t, t2], eng="gpsimd")
                cg[i % 3][1] = cu[i % 3][1] = [t]
                th.append(t)
            p1.done(m1)
            p2.done(m2)
        lnexp()
        bk, m = project(hT, 22, io["w_down_2"][l], th)
        post_norm(bk, m, 2, f"b{l}")
        xn_free = list(t_X)
        prog.barrier()
        pf.close()
        ph.close()

    s_out = dsem("s_out")
    t_out = dma(out[0].rearrange("(h p) d -> p h d", p=128), X[:, :, :], s_out, t_X)
    sems_end = [t_out]
    prog.number(sems)
    with ctx, nc.Block() as block:
        @block.sync
        def _(e):
            prog.write("sync", e)
            for t in sems_end:
                e.wait_ge(t.sem, t.val)

        @block.tensor
        def _(e):
            prog.write("tensor", e)

        @block.vector
        def _(e):
            prog.write("vector", e)

        @block.scalar
        def _(e):
            prog.write("scalar", e)

        @block.gpsimd
        def _(e):
            prog.write("gpsimd", e)


NAMES = ['x', 'c', 'hyb_norm', 'hyb_mod_w', 'hyb_mod_b', 'hyb_w_in', 'gla_gk_up', 'gla_gk_bias', 'gla_out_norm', 'nsa_cmp_pe',
         'nsa_cmp_w1', 'nsa_cmp_w2', 'hyb_w_out', 'dense_norm', 'dense_mod_w', 'dense_mod_b', 'dense_w_gu', 'dense_w_down',
         'ssm_norm', 'ssm_mod_w', 'ssm_mod_b', 'ssm_w_in', 'ssm_conv_w', 'ssm_conv_b', 'ssm_dt_bias', 'ssm_a_log', 'ssm_d',
         'ssm_gate_norm', 'ssm_w_out', 'moe_norm', 'moe_mod_w', 'moe_mod_b', 'moe_router', 'moe_w_gu', 'moe_w_down', 'final_norm',
         'w_in_2', 'gdn_conv_w_2', 'gdn_a_log_2', 'gdn_dt_bias_2', 'gdn_norm_g_2', 'w_out_2', 'ln1_g_2', 'ln1_b_2', 'w_up_2',
         'ffn_conv_w_2', 'ffn_conv_b_2', 'w_down_2', 'ln2_g_2', 'ln2_b_2']


def kernel(**inputs):
    import concourse.bacc as bacc
    from concourse.bass_utils import run_bass_kernel_spmd

    nc = bacc.Bacc("TRN2", target_bir_lowering=False, num_devices=1)
    arrays, io, cn = {}, {}, {}
    for n in NAMES:
        a = np.ascontiguousarray(inputs[n])
        arrays["in_" + n] = a
        io[n] = nc.dram_tensor("in_" + n, a.shape, mybir.dt.float32, kind="ExternalInput").ap()
    for n, a in constants().items():
        arrays["const_" + n] = a
        cn[n] = nc.dram_tensor("const_" + n, a.shape, mybir.dt.float32, kind="ExternalInput").ap()
    out = nc.dram_tensor("out", (1, T, D), mybir.dt.float32, kind="ExternalOutput").ap()
    program(nc, io, cn, out)
    r = run_bass_kernel_spmd(nc, [arrays], core_ids=[0])
    return np.asarray(r.results[0]["out"])
```

```python
import numpy as np
import concourse.bass as bass
from concourse import mybir
from concourse.alu_op_type import AluOpType as ALU
from contextlib import ExitStack

F32 = mybir.dt.float32
AF = mybir.ActivationFunctionType
AX = mybir.AxisListType

ENGINES = ("sync", "tensor", "vector", "scalar", "gpsimd")


class Op:

    def __init__(self, eng, fn, waits, dma):
        self.eng, self.fn, self.waits, self.dma = eng, fn, waits, dma
        self.needed, self.sem, self.val = False, None, 0


class Program:

    def __init__(self):
        self.q = {e: [] for e in ENGINES}
        self.hold = {e: [] for e in ENGINES}
        self.dma_count = {}

    def add(self, eng, fn, waits=(), dma=None):
        flat = []

        def walk(w):
            if w is None:
                return
            if isinstance(w, (list, tuple)):
                for x in w:
                    walk(x)
            else:
                flat.append(w)

        walk(list(waits) if isinstance(waits, (list, tuple)) else [waits])
        flat += self.hold[eng]
        self.hold[eng] = []
        for w in flat:
            w.needed = True
        op = Op(eng, fn, flat, dma)
        if dma is not None:
            self.dma_count[dma] = self.dma_count.get(dma, 0) + 16
            op.sem, op.val = dma, self.dma_count[dma]
        self.q[eng].append(op)
        return op

    def last(self):
        own = {e: [o for o in self.q[e] if isinstance(o, Op) and o.dma is None] for e in ("tensor", "vector", "scalar", "gpsimd")}
        return [o[-1] for o in own.values() if o]

    def barrier(self):
        ends = self.last()
        for e in ("tensor", "vector", "scalar", "gpsimd"):
            self.hold[e] = self.hold[e] + ends
        return ends

    def begin_if(self, flag, tok):
        tok.needed = True
        for e in ENGINES:
            self.q[e].append(("if", flag, tok))

    def end_if(self):
        for e in ENGINES:
            self.q[e].append(("end",))

    def number(self, sems):
        self.sems = sems
        for e in ENGINES:
            n = 0
            for op in self.q[e]:
                if isinstance(op, Op) and op.dma is None and op.needed:
                    n += 1
                    op.sem, op.val = sems[e], n

    def write(self, name, eng):
        seen = {}
        ops, i = self.q[name], 0
        made = {}
        while i < len(ops):
            if isinstance(ops[i], Op):
                self.one(eng, ops[i], seen, made)
                i += 1
                continue
            _, flag, tok = ops[i]
            end = next(j for j in range(i, len(ops)) if not isinstance(ops[j], Op) and ops[j][0] == "end")
            eng.wait_ge(tok.sem, tok.val)
            go = eng.value_load(flag, min_val=0, max_val=1)
            before = dict(made)
            with eng.If(go):
                inside = dict(seen)
                for op in ops[i + 1:end]:
                    self.one(eng, op, inside, made)
            with eng.Else():
                for s, v in made.items():
                    if v > before.get(s, 0):
                        if before.get(s, 0):
                            eng.wait_ge(s, before[s])
                        eng.sem_inc(s, v - before.get(s, 0))
            i = end + 1

    def one(self, eng, op, seen, made):
        need = {}
        for w in op.waits:
            need[w.sem] = max(need.get(w.sem, 0), w.val)
        for s, v in need.items():
            if seen.get(s, 0) < v:
                eng.wait_ge(s, v)
                seen[s] = v
        ins = op.fn(eng)
        if op.dma is not None:
            ins.then_inc(op.dma, 16)
            made[op.dma] = op.val
        elif op.needed:
            ins.then_inc(op.sem, 1)
            made[op.sem] = op.val

D = 1024
T = 256
KC = 8
SLOT = 528 * 8
NSLOT = 3
NUNIT = 3
R32 = mybir.dt.float32r
EPS = 1e-6
LN_EPS = 1e-5
ALPHA = 4.0 ** 0.25
FF = 2816
FE = 3584
NE = 8
BIG = 1e30
CAP = 128


def constants():
    p = np.arange(128)
    c = {}
    c["ident"] = np.eye(128)
    c["causal"] = p[:, None] <= p[None, :]
    c["glamask"] = (p[:, None] <= p[None, :]) & (p[:, None] // 64 == p[None, :] // 64)
    lev = np.zeros((128, 7, 128))
    for n in range(7):
        b = p >> n
        lev[:, n, :] = (b[None, :] % 2 == 1) & (b[:, None] == b[None, :] - 1)
    c["levels"] = lev.reshape(128, -1)
    dist = np.zeros((128, 256))
    dist[:, :128] = 128 + p[:, None] - p[None, :]
    dist[:, 128:] = np.where(p[:, None] >= p[None, :], p[:, None] - p[None, :], BIG)
    c["dist"] = dist
    dc = np.full((128, 2, 16), BIG)
    for h in range(2):
        t = h * 128 + p
        for n in range(15):
            dc[:, h, n] = np.where(n * 16 + 31 <= t, t - (n * 16 + 15.5), BIG)
    c["distc"] = dc.reshape(128, -1)
    c["blockdiag"] = (p[:, None] // 16 == np.arange(8)[None, :])
    c["cmask"] = np.where(p[:, None] >= p[None, :], 0.0, -BIG)
    half = 8
    inv = np.float32(500000.0) ** (-np.arange(half, dtype=np.float32) / np.float32(half))
    ang = np.arange(T, dtype=np.float32)[None, :] * inv.astype(np.float32)[:, None]
    cos, sin = np.ones((128, T)), np.zeros((128, T))
    perm = np.zeros((128, 128))
    for b in (0, 64):
        cos[b:b + 8] = cos[b + 8:b + 16] = np.cos(ang.astype(np.float32))
        sin[b:b + 8] = -np.sin(ang.astype(np.float32))
        sin[b + 8:b + 16] = np.sin(ang.astype(np.float32))
        for i in range(8):
            perm[b + 8 + i, b + i] = 1
            perm[b + i, b + 8 + i] = 1
    c["cos"], c["sin"], c["perm"] = cos, sin, perm
    e = np.arange(8)
    c["tie"] = np.broadcast_to((e[None, :] < e[:, None]).reshape(1, 64), (128, 64))
    c["iota"] = np.broadcast_to(np.arange(256)[None], (128, 256))
    c["before"] = p[:, None] < p[None, :]
    c["reset64"] = np.broadcast_to((np.arange(T) % 64 != 0)[None], (128, T))
    c["reset128"] = np.broadcast_to((np.arange(T) % 128 != 0)[None], (128, T))
    return {k: np.ascontiguousarray(v, dtype=np.float32) for k, v in c.items()}



def program(nc, io, cn, out):
    prog = Program()
    ctx = ExitStack()

    def sb(name, shape, stack=ctx, dt=F32):
        return stack.enter_context(nc.sbuf_tensor(name, list(shape), dt))

    psum = [ctx.enter_context(nc.psum_tensor(f"ps{i}", [128, 512], F32)) for i in range(8)]
    sems = {e: ctx.enter_context(nc.semaphore(f"s_{e}")) for e in ENGINES}

    def dsem(name):
        return ctx.enter_context(nc.semaphore(name))

    def mm(o, lhsT, rhs, start=True, stop=True, w=(), skip=False):
        return prog.add("tensor", lambda e: e.matmul(o, lhsT, rhs, start=start, stop=stop, skip_group_check=skip), w)

    def chain(o, pairs, w=()):
        for i, (a, b) in enumerate(pairs):
            t = mm(o, a, b, i == 0, i == len(pairs) - 1, w if i == 0 else ())
        return t

    def tp(o, i, w=()):
        n = i.shape[0]
        return prog.add("tensor", lambda e: e.transpose(o, i, K["ident"][0:n, 0:n]), w)

    def act(o, i, f, w=(), **kw):
        return prog.add("scalar", lambda e: e.activation(o, i, f, **kw), w)

    def tt(o, a, b, op, w=(), eng="vector"):
        return prog.add(eng, lambda e: e.tensor_tensor(o, a, b, op), w)

    def ts(o, a, s1, op0, s2=None, op1=None, w=(), eng="vector"):
        if op1 is None:
            return prog.add(eng, lambda e: e.tensor_scalar(o, a, s1, None, op0), w)
        return prog.add(eng, lambda e: e.tensor_scalar(o, a, s1, s2, op0, op1), w)

    def stt(o, a, s, b, op0, op1, w=()):
        return prog.add("vector", lambda e: e.scalar_tensor_tensor(o, a, s, b, op0, op1), w)

    def cp(o, i, w=(), eng="vector"):
        if eng == "scalar":
            return act(o, i, AF.Copy, w)
        return prog.add(eng, lambda e: e.tensor_copy(o, i), w)

    def red(o, i, op, w=(), negate=False):
        return prog.add("vector", lambda e: e.tensor_reduce(o, i, AX.X, op, negate=negate), w)

    def recip(o, i, w=()):
        return prog.add("vector", lambda e: e.reciprocal(o, i), w)

    def scan(o, a, b, w=()):
        return prog.add("vector", lambda e: e.tensor_tensor_scan(o, a, b, 0.0, ALU.mult, ALU.add), w)

    def fill(o, v, w=(), eng="gpsimd"):
        return prog.add(eng, lambda e: e.memset(o, v), w)

    def dma(o, i, sem, w=(), eng="sync"):
        return prog.add(eng, lambda e: e.dma_start(o, i), w, dma=sem)

    def lnexp(w=()):
        return prog.add("scalar", lambda e: e.preload_act_table_set("natural_log_exp_and_others"), w)

    def bc(ap, axis, n):
        a = ap.unsqueeze(axis)
        s = list(a.shape)
        s[axis] = n
        return a.to_broadcast(s)

    class Bank:
        def __init__(self, t):
            self.t, self.w = t, []

    class Banks:
        def __init__(self, ts_):
            self.b, self.i = ts_, 0

        def take(self):
            b = self.b[self.i]
            self.i = (self.i + 1) % len(self.b)
            return b

    allbanks = [Bank(t) for t in psum]
    banks = Banks(allbanks)

    slots = sb("slots", [128, NSLOT, SLOT])
    slot_sem = [dsem(f"s_w{i}") for i in range(NSLOT)]
    slot_free = [[] for _ in range(NSLOT)]
    nload = [0]

    class Piece:
        def __init__(self, i, ap, tok):
            self.i, self.ap, self.tok = i, ap, tok

        def done(self, *toks):
            slot_free[self.i] = list(toks)

    def load(src, shape):
        i = nload[0] % NSLOT
        nload[0] += 1
        a, b = shape
        assert slot_free[i] is not None
        v = slots[:, i, 0:a * b].rearrange("p (a b) -> p a b", b=b)
        t = dma(v, src, slot_sem[i], slot_free[i])
        slot_free[i] = None
        return Piece(i, v, t)

    def wcols(w, c0, n):
        return load(w[:, c0:c0 + n].rearrange("(k p) n -> p k n", p=128), (KC, n))

    def wheads(w, c0):
        i = nload[0] % NSLOT
        nload[0] += 1
        v = slots[:, i, 0:KC * 512].rearrange("p (a b) -> p a b", b=512)
        for g in range(2):
            for k in range(KC):
                t = dma(v[:, k, :].rearrange("p (r g d) -> p g r d", g=2, d=64)[:, g, :, :],
                        w[k * 128:(k + 1) * 128, c0 + g * 256:c0 + (g + 1) * 256].rearrange("p (r d) -> p r d", d=64), slot_sem[i], slot_free[i])
        slot_free[i] = None
        return Piece(i, v, t)

    def wrows(w, r0, n):
        return load(w[r0:r0 + n * 128, :].rearrange("(f p) n -> p f n", p=128), (n, D))

    K, Ksh = {}, {}
    s_const = dsem("s_const")
    X = sb("X", [128, 2, D])
    s_x = dsem("s_x")
    t_x = dma(X[:, :, :], io["x"][0].rearrange("(h p) d -> p h d", p=128), s_x)
    rows = sb("rows", [128, 128])

    def const(n):
        K[n] = sb("k_" + n, [128, cn[n].shape[1]])
        return dma(K[n][:, :], cn[n], s_const)

    for n in ("ident", "causal", "tie", "iota", "before"):
        t_const = const(n)
    ones = sb("ones", [128, 128])
    t_ones = fill(ones[:, :], 1.0)

    vec = {}
    vec_tok = {}
    rows_free = []
    s_rows = dsem("s_rows")

    def vectors(block, parts):
        nonlocal rows_free
        n = sum(s.shape[0] for _, s in parts)
        z = fill(rows[:, :], 0.0, rows_free)
        at = 0
        first = [z]
        for _, s in parts:
            t = dma(rows[at:at + s.shape[0], :], s, s_rows, first, eng="gpsimd")
            at += s.shape[0]
        b = banks.take()
        m = tp(b.t[:, 0:128], rows[:, :], [t, t_const, b.w])
        v = sb("v_" + block, [128, n])
        c = cp(v[:, :], b.t[:, 0:n], [m])
        b.w = [c]
        rows_free = [m]
        at = 0
        for name, s in parts:
            vec[name] = v[:, at:at + s.shape[0]]
            vec_tok[name] = c
            at += s.shape[0]

    def r128(v):
        return v.rearrange("(r p) -> r p", p=128)

    vectors("a", [("c", r128(io["c"][0])), ("hyb_norm", r128(io["hyb_norm"][0])), ("dense_norm", r128(io["dense_norm"][0])),
                  ("ssm_norm", r128(io["ssm_norm"][0])), ("moe_norm", r128(io["moe_norm"][0])),
                  ("gate_norm", r128(io["ssm_gate_norm"][0])), ("conv_b", r128(io["ssm_conv_b"][0])),
                  ("gk_bias", r128(io["gla_gk_bias"][0]))])
    vectors("b", [("conv_w", io["ssm_conv_w"][0].rearrange("j (r p) -> (j r) p", p=128))])
    for l in range(2):
        vectors(f"g{l}", [(f"gconv{l}", io["gdn_conv_w_2"][l].rearrange("j (r p) -> (j r) p", p=128))])
        vectors(f"f{l}", [(f"fconv{l}", io["ffn_conv_w_2"][l][0:2].rearrange("j (r p) -> (j r) p", p=128))])
        vectors(f"h{l}", [(f"fconv2{l}", io["ffn_conv_w_2"][l][2:3].rearrange("j (r p) -> (j r) p", p=128)),
                          (f"fconvb{l}", r128(io["ffn_conv_b_2"][l]))])

    sc = sb("sc", [128, KC])
    with_e = sb("sc_e", [128, KC])
    e0 = lnexp()
    e1 = act(with_e[:, :], vec["c"], AF.Exp, [vec_tok["c"], e0], scale=-1.0)
    a1 = ts(with_e[:, :], with_e[:, :], 1.0, ALU.add, w=[e1])
    a2 = recip(with_e[:, :], with_e[:, :], [a1])
    t_sc = tt(sc[:, :], with_e[:, :], vec["c"], ALU.mult, [a2])

    xn = sb("xn", [128, 2, D])
    ssq = sb("ssq", [128, 2])
    rst = sb("rst", [128, 2])
    pfirst = ExitStack()
    macc_free = []
    s_macc = dsem("s_macc")
    mod = {}
    gates = [sb(f"gate{i}", [128, D], pfirst) for i in range(3)]
    gate_free = [[], [], []]
    side = []

    def step(n=1):
        for _ in range(n):
            while side:
                try:
                    next(side[0])
                    break
                except StopIteration:
                    side.pop(0)

    def finish_side():
        while side:
            step()

    pmacc = ExitStack()
    s12 = {n: (sb(f"s1_{n}", [128, KC], pfirst), sb(f"s2_{n}", [128, KC], pfirst)) for n in ("hyb", "dense", "ssm", "moe")}

    macc = sb("macc", [128, 3 * D], pmacc)

    def adaln(name, slot):
        nonlocal macc_free
        w_, b_ = io[name + "_mod_w"][0], io[name + "_mod_b"]
        z = fill(macc[:, :], 0.0, macc_free)
        t = dma(macc[0:1, :], b_, s_macc, [z], eng="gpsimd")
        for k in range(KC):
            pc = load(w_[k * 128:(k + 1) * 128, :].rearrange("p (a n) -> p a n", a=1), (1, 3 * D))
            t = stt(macc[:, :], pc.ap[:, 0, :], sc[:, k:k + 1], macc[:, :], ALU.mult, ALU.add, [t, pc.tok, t_sc])
            pc.done(t)
            yield
        b = banks.take()
        for i in range(16):
            m = mm(b.t[:, i:i + 1], macc[:, i * 128:(i + 1) * 128], ones[:, 0:1], w=[t, t_ones, b.w])
        s1, s2 = s12[name]
        c2 = cp(s2[:, :], b.t[:, 0:8], [m])
        c1 = stt(s1[:, :], b.t[:, 8:16], 1.0, vec[name + "_norm"], ALU.add, ALU.mult, [m, vec_tok[name + "_norm"]])
        b.w = [c1]
        toks = [c1, c2]
        g = gates[slot]
        for i in range(2):
            b = banks.take()
            m = mm(b.t[:, :], ones[:, :], macc[:, 2 * D + i * 512:2 * D + (i + 1) * 512], w=[b.w])
            b.w = [cp(g[:, i * 512:(i + 1) * 512], b.t[:, :], [m, gate_free[slot]])]
            toks += b.w
        macc_free = [m]
        mod[name] = (s1, s2, g, slot, toks)

    HT_free = []
    xn_free = []
    t_X = [t_x, t_x]

    def rms(dst):
        out_ = []
        for h in range(2):
            q = act(dst[:, h, :], X[:, h, :], AF.Square, [t_X[h], xn_free], accum_out=ssq[:, h:h + 1])
            out_.append(q)
        t = ts(ssq[:, :], ssq[:, :], 1.0 / D, ALU.mult, EPS, ALU.add, w=out_)
        t = act(rst[:, :], ssq[:, :], AF.Ln, [t])
        t = act(rst[:, :], rst[:, :], AF.Exp, [t], scale=-0.5)
        return [ts(dst[:, h, :], X[:, h, :], rst[:, h:h + 1], ALU.mult, w=[t]) for h in range(2)]

    HT = None
    HTl = None

    def new_HT(stack, name, parts=False):
        nonlocal HT, HTl
        HT = sb("HT" + name, [128, KC, T], stack, R32 if parts else F32)
        HTl = sb("HTl" + name, [128, KC, T], stack, R32) if parts else None

    def hi_lo(hi, lo, x, w, wh=()):
        t = act(hi, x, AF.Copy, [w, wh])
        return tt(lo, x, hi.bitcast(F32), ALU.subtract, [t, wh])

    def to_HT(src, toks, s1=None, s2=None, w=()):
        nonlocal HT_free
        res = []
        for k in range(KC):
            b = banks.take()
            for h in range(2):
                m = tp(b.t[:, h * 128:(h + 1) * 128], src[:, h, k * 128:(k + 1) * 128], [toks[h], b.w, t_const])
            if HTl is not None and s1 is None:
                c = hi_lo(HT[:, k, :], HTl[:, k, :], b.t[:, 0:256], [m])
            elif HTl is not None:
                x_ = HTf[k % 2]
                c = ts(x_[0][:, :], b.t[:, 0:256], s1[:, k:k + 1], ALU.mult, s2[:, k:k + 1], ALU.add, w=[m, w, x_[1]])
                b.w = [c]
                c = hi_lo(HT[:, k, :], HTl[:, k, :], x_[0][:, :], [c])
                x_[1] = [c]
                res.append(c)
                continue
            elif s1 is None:
                c = cp(HT[:, k, :], b.t[:, 0:256], [m, HT_free], eng="scalar" if k % 2 else "vector")
            elif k % 2:
                c = act(HT[:, k, :], b.t[:, 0:256], AF.Identity, [m, HT_free, w], scale=s1[:, k:k + 1], bias=s2[:, k:k + 1])
            else:
                c = ts(HT[:, k, :], b.t[:, 0:256], s1[:, k:k + 1], ALU.mult, s2[:, k:k + 1], ALU.add, w=[m, HT_free, w])
            b.w = [c]
            res.append(c)
        HT_free = []
        return res, m

    def modulated(name):
        nonlocal xn_free
        s1, s2, g, slot, toks = mod[name]
        x2 = rms(xn)
        res, m = to_HT(xn, x2, s1, s2, toks)
        xn_free = [m]
        return res

    def gated_add(bk, name, m):
        s1, s2, g, slot, toks = mod[name]
        last = None
        for h in range(2):
            for i in range(2):
                o = xn[:, h, i * 512:(i + 1) * 512]
                c = tt(o, bk[h][i].t[:, :], g[:, i * 512:(i + 1) * 512], ALU.mult, [m[h][i], toks, xn_free])
                bk[h][i].w = [c]
                last = tt(X[:, h, i * 512:(i + 1) * 512], X[:, h, i * 512:(i + 1) * 512], o, ALU.add, [c])
            t_X[h] = last
        gate_free[slot] = [last]

    UN = {}

    def new_units(stack, name):
        UN["hi"] = sb("uh" + name, [128, NUNIT, 2048], stack, R32)
        UN["lo"] = sb("ul" + name, [128, NUNIT, 2048], stack, R32)
        UN["free"] = [[] for _ in range(NUNIT)]
        UN["n"] = 0

    class Unit:

        def __init__(self, x, tok):
            self.i = UN["n"] % NUNIT
            UN["n"] += 1
            sh = list(x.shape)
            view = lambda a: a[:, self.i, :].rearrange("p (a b) -> p a b", b=sh[2])
            self.hi, self.lo = view(UN["hi"])[:, 0:sh[1], :], view(UN["lo"])[:, 0:sh[1], :]
            assert UN["free"][self.i] is not None
            self.tok = hi_lo(self.hi, self.lo, x, [tok], UN["free"][self.i])
            UN["free"][self.i] = None

        def done(self, *toks):
            UN["free"][self.i] = list(toks)

    def A3(o, u, c0, w):
        ps = []
        for k in range(KC):
            a, l = u.hi[:, k, c0:c0 + 128], u.lo[:, k, c0:c0 + 128]
            ps += [(a, HT[:, k, :]), (a, HTl[:, k, :]), (l, HT[:, k, :])]
        return chain(o, ps, [w, u.tok])

    AHEAD = NUNIT - 1
    queue = []

    def put(x, pc, last, use):
        u = Unit(x, pc.tok)
        if last:
            pc.done(u.tok)
        queue.append((u, use))
        if len(queue) > AHEAD:
            u, use = queue.pop(0)
            use(u)

    def drain():
        while queue:
            u, use = queue.pop(0)
            use(u)

    def project3(hi, lo, ntile, wmat, toks, halves, end, bk=None, begin=None):
        m = [[None] * 2 for _ in range(halves)]
        st_ = {"bk": bk}

        def use(u, g0, n, last):
            if g0 == 0 and begin:
                begin()
            if st_["bk"] is None:
                st_["bk"] = [[banks.take() for _ in range(2)] for _ in range(halves)]
            bk = st_["bk"]
            for f in range(n):
                g = g0 + f
                for h in range(halves):
                    sl = slice(h * 128, (h + 1) * 128)
                    for i in range(2):
                        c = slice(i * 512, (i + 1) * 512)
                        o = bk[h][i].t[:, :]
                        mm(o, hi[:, g, sl], u.hi[:, f, c], g == 0, False, [u.tok, toks[g]] + (bk[h][i].w if g == 0 else []))
                        mm(o, hi[:, g, sl], u.lo[:, f, c], False, False)
                    for i in range(2):
                        c = slice(i * 512, (i + 1) * 512)
                        m[h][i] = mm(bk[h][i].t[:, :], lo[:, g, sl], u.hi[:, f, c], False, g == ntile - 1)
            u.done(m[-1][1])
            if last:
                end(bk, m)

        for r in range(0, ntile, 4):
            n = min(4, ntile - r)
            pc = wrows(wmat, r * 128, n)
            for f0 in range(0, n, 2):
                last = r + f0 + 2 >= ntile
                put(pc.ap[:, f0:f0 + 2, :], pc, f0 + 2 >= n, lambda u, g0=r + f0, last=last: use(u, g0, 2, last))

    def A(o, pc, c0, n, w, rhs=None, lhs=None):
        return chain(o, [(pc.ap[:, k, c0:c0 + n], HT[:, k, :]) for k in range(KC)], [w, pc.tok])

    def Bm(o, pc, c0, n, h, w):
        return chain(o, [(HT[:, k, h * 128:(h + 1) * 128], pc.ap[:, k, c0:c0 + n]) for k in range(KC)], [w, pc.tok])

    def silu_of(o, i, w):
        return act(o, i, AF.Silu, w)

    def project(src, ntile, wmat, toks, w=()):
        bk = [[banks.take() for _ in range(2)] for _ in range(2)]
        m = [[None] * 2 for _ in range(2)]
        for r in range(0, ntile, 4):
            n = min(4, ntile - r)
            pc = wrows(wmat, r * 128, n)
            for f in range(n):
                for h in range(2):
                    for i in range(2):
                        first, lst = r + f == 0, r + f == ntile - 1
                        m[h][i] = mm(bk[h][i].t[:, :], src[:, r + f, h * 128:(h + 1) * 128],
                                     pc.ap[:, f, i * 512:(i + 1) * 512], first, lst,
                                     [pc.tok, toks[r + f]] + (bk[h][i].w if first else []))
            pc.done(m[1][1])
        return bk, m

    def transposed(src, ntile, dst, toks, scale=None, w=()):
        res = []
        for k in range(ntile):
            b = banks.take()
            for h in range(2):
                m = tp(b.t[:, h * 128:(h + 1) * 128], src[:, h, k * 128:(k + 1) * 128], [toks[h], b.w, t_const])
            if scale is None:
                c = cp(dst[:, k, :], b.t[:, 0:256], [m, w], eng="scalar" if k % 2 else "vector")
            elif k % 2:
                c = act(dst[:, k, :], b.t[:, 0:256], AF.Copy, [m, w], scale=scale[:, k:k + 1])
            else:
                c = ts(dst[:, k, :], b.t[:, 0:256], scale[:, k:k + 1], ALU.mult, w=[m, w])
            b.w = [c]
            res.append(c)
        return res

    side.append(adaln("hyb", 0))
    finish_side()
    side.append(adaln("dense", 1))
    ph = ExitStack()
    s_hc = dsem("s_hc")
    for n in ("glamask", "dist", "distc", "blockdiag", "reset64"):
        K[n] = sb("k_" + n, [128, cn[n].shape[1]], ph)
        t_hc = dma(K[n][:, :], cn[n], s_hc, eng="gpsimd")
    new_HT(ph, "0")
    h = modulated("hyb")
    W = io["hyb_w_in"][0]
    mix = sb("mix", [128, 2, D], ph)
    pn = ph
    ph = ExitStack()
    q2 = sb("q2", [128, 2, T], ph)
    k2 = sb("k2", [128, 2, T], ph)
    va = sb("va", [128, 2, 512], ph)
    rs = sb("rs", [128, 2, 512], ph)
    lrT = sb("lrT", [16, T], ph)
    gku = sb("gku", [16, T], ph)
    s_g = dsem("s_gla")
    t_gku = dma(gku[:, :], io["gla_gk_up"][0], s_g, eng="gpsimd")
    onr = sb("onr", [128, 128], ph)
    t_onr = dma(onr[:, :], io["gla_out_norm"][0].partition_broadcast(128), s_g, eng="gpsimd")
    t_gku = t_onr

    pc = wcols(W, 0, 512)
    tq, tk = [], []
    for f in range(4):
        b = banks.take()
        m = A(b.t[:, 0:256], pc, f * 128, 128, [h, b.w])
        if f < 2:
            c = act(q2[:, f, :], b.t[:, 0:256], AF.Copy, [m], scale=0.125)
            tq.append(c)
        else:
            c = cp(k2[:, f - 2, :], b.t[:, 0:256], [m])
            tk.append(c)
        b.w = [c]
    pc.done(m)
    step()
    pc = wcols(W, 512, 512)
    tv = []
    for hf in range(2):
        b = banks.take()
        m = Bm(b.t[:, :], pc, 0, 512, hf, [h, b.w])
        b.w = [cp(va[:, hf, :], b.t[:, :], [m])]
        tv += b.w
    pc.done(m)
    step()
    pc = wcols(W, 1024, 528)
    b = banks.take()
    m = A(b.t[0:16, 0:256], pc, 0, 16, [h, b.w])
    t_lr = cp(lrT[:, :], b.t[0:16, 0:256], [m])
    b.w = [t_lr]
    tr = []
    for hf in range(2):
        b = banks.take()
        m = Bm(b.t[:, :], pc, 16, 512, hf, [h, b.w])
        b.w = [silu_of(rs[:, hf, :], b.t[:, :], [m])]
        tr += b.w
    pc.done(m)
    step()

    zb = sb("zb", [128, 2, T], ph)
    za = sb("za", [128, 2, T], ph)
    cum = sb("cum", [128, 2, T], ph)
    Eq, Ek, Ee = zb, za, sb("Ee", [128, 2, T], ph)
    be = sb("be", [128, 2, 4], ph)
    dec = sb("dec", [128, 2, 4], ph)
    lnexp()
    bz = banks.take()
    tz = []
    for f in range(2):
        m = mm(bz.t[:, f * 256:(f + 1) * 256], gku[:, f * 128:(f + 1) * 128], lrT[:, :], w=[t_lr, t_gku, bz.w])
    for f in range(2):
        tz.append(ts(zb[:, f, :], bz.t[:, f * 256:(f + 1) * 256], vec["gk_bias"][:, f:f + 1], ALU.add, w=[m, vec_tok["gk_bias"]]))
    bz.w = tz
    t = act(za[:, :, :], zb[:, :, :], AF.Abs, tz)
    t = act(za[:, :, :], za[:, :, :], AF.Exp, [t], scale=-1.0)
    t = act(za[:, :, :], za[:, :, :], AF.Ln, [t], bias=1.0)
    t = stt(zb[:, :, :], zb[:, :, :], 0.0, za[:, :, :], ALU.min, ALU.subtract, [t])
    tcum = [scan(cum[:, f, :], K["reset64"][:, :], zb[:, f, :], [t, t_hc]) for f in range(2)]
    ce = cum[:, :, :].rearrange("p f (n c) -> p f n c", c=64)[:, :, :, 63]
    tbe = ts(be[:, :, :], ce, 1.0 / 16, ALU.mult, w=tcum)
    tde = act(dec[:, :, :], be[:, :, :], AF.Exp, [tbe])
    t1 = act(Eq[:, :, :], cum[:, :, :], AF.Exp, tcum, scale=1.0 / 16)
    t2 = act(Ek[:, :, :], cum[:, :, :], AF.Exp, tcum, scale=-1.0 / 16)
    for f in range(2):
        for n in range(4):
            t3 = act(Ee[:, f, n * 64:(n + 1) * 64], cum[:, f, n * 64:(n + 1) * 64], AF.Exp, [tbe], scale=-1.0 / 16, bias=be[:, f, n:n + 1])
    tqd = tt(q2[:, :, :], q2[:, :, :], Eq[:, :, :], ALU.mult, [tq, t1])
    tke = tt(Ee[:, :, :], k2[:, :, :], Ee[:, :, :], ALU.mult, [tk, t3])
    tkd = tt(k2[:, :, :], k2[:, :, :], Ek[:, :, :], ALU.mult, [tke, t2])
    ke = sb("ke", [128, 2, T], ph)
    b = banks.take()
    for hf in range(2):
        for f in range(2):
            m = tp(b.t[:, hf * 256 + f * 128:hf * 256 + (f + 1) * 128], Ee[:, f, hf * 128:(hf + 1) * 128], [tke, b.w])
    tket = cp(ke[:, :, :].rearrange("p a b -> p (a b)"), b.t[:, :], [m])
    b.w = [tket]
    St = sb("St", [128, 3, 2, 128], ph)
    ts_ = None
    tst = []
    for n in range(3):
        hf, r = n // 2, (n % 2) * 64
        b = banks.take()
        for f in range(2):
            for g in range(2):
                hd = f * 2 + g
                m = mm(b.t[g * 64:g * 64 + 64, f * 128:(f + 1) * 128], ke[r:r + 64, hf, f * 128 + g * 64:f * 128 + g * 64 + 64],
                       va[r:r + 64, hf, hd * 128:(hd + 1) * 128], w=[tket, tv, b.w])
        if n == 0:
            ts_ = cp(St[:, 0, :, :], b.t[:, 0:256].rearrange("p (f v) -> p f v", v=128), [m])
        else:
            for f in range(2):
                ts_ = stt(St[:, n, f, :], St[:, n - 1, f, :], dec[:, f, n:n + 1], b.t[:, f * 128:(f + 1) * 128], ALU.mult, ALU.add, [m, tde, ts_])
        b.w = [ts_]
        tst.append(ts_)
    AT = sb("AT", [128, 2, 4, 128], ph)
    tat = []
    for g in range(2):
        b = banks.take()
        for f in range(2):
            for hf in range(2):
                m = mm(b.t[:, (f * 2 + hf) * 128:(f * 2 + hf + 1) * 128], k2[g * 64:g * 64 + 64, f, hf * 128:(hf + 1) * 128],
                       q2[g * 64:g * 64 + 64, f, hf * 128:(hf + 1) * 128], w=[tqd, tkd, b.w])
        c = tt(AT[:, g, :, :], b.t[:, :].rearrange("p (a c) -> p a c", c=128), bc(K["glamask"][:, :], 1, 4), ALU.mult, [m, t_hc])
        b.w = [c]
        tat.append(c)
    Og = sb("Og", [128, 2, 4, 128], ph)
    to_ = []
    for hf in range(2):
        for g in range(2):
            b = banks.take()
            for f in range(2):
                hd = f * 2 + g
                o = b.t[:, f * 128:(f + 1) * 128]
                m = mm(o, AT[:, g, f * 2 + hf, :], va[:, hf, hd * 128:(hd + 1) * 128], w=[tat, tv, b.w])
                for n in (2 * hf, 2 * hf + 1):
                    if n:
                        r = (n % 2) * 64
                        m = mm(o[r:r + 64, :], q2[g * 64:g * 64 + 64, f, n * 64:(n + 1) * 64], St[g * 64:g * 64 + 64, n - 1, f, :], False, True, [tst], skip=True)
            c = cp(Og[:, hf, :, :].rearrange("p (f g) v -> p g f v", g=2)[:, g, :, :], b.t[:, 0:256].rearrange("p (f v) -> p f v", v=128), [m])
            b.w = [c]
            to_.append(c)
    og3 = Og[:, :, :, :].rearrange("p h a v -> p (h a) v")
    sq = AT[:, :, :, :].rearrange("p g a v -> p (g a) v")
    vs = sb("vs", [128, 8], ph)
    t = tt(sq, og3, og3, ALU.mult, to_)
    t = red(vs[:, :], sq, ALU.add, [t])
    t = ts(vs[:, :], vs[:, :], 1.0 / 128, ALU.mult, EPS, ALU.add, w=[t])
    t = act(vs[:, :], vs[:, :], AF.Ln, [t])
    t = act(vs[:, :], vs[:, :], AF.Exp, [t], scale=-0.5)
    t = tt(og3, og3, bc(vs[:, :], 2, 128), ALU.mult, [t])
    t = tt(og3, og3, bc(onr[:, :], 1, 8), ALU.mult, [t, t_onr])
    t_gla = tt(mix[:, :, 0:512], Og[:, :, :, :].rearrange("p h a v -> p h (a v)"), rs[:, :, :], ALU.mult, [t, tr])

    prog.barrier()
    ph.close()
    ph = pn
    qT = sb("nq", [128, 4, T], ph)
    pc = wheads(W, 1552)
    tnq = []
    for j in range(4):
        b = banks.take()
        m = A(b.t[:, 0:256], pc, j * 128, 128, [h, b.w])
        c = act(qT[:, j, :], b.t[:, 0:256], AF.Copy, [m], scale=0.125)
        b.w = [c]
        tnq.append(c)
    pc.done(m)
    step()
    KCm = [sb(f"kc{j}", [128, 3, T], ph) for j in range(2)]
    kb = [sb(f"kb{j}", [128, T], ph) for j in range(2)]
    vb = [sb(f"vb{j}", [128, 2, 128], ph) for j in range(2)]
    gt = sb("gt", [128, 2, 24], ph)
    pe_sb = sb("pe_sb", [32, 2, 64], ph)
    s_nsa = dsem("s_nsa")
    t_pe = dma(pe_sb[:, :, :], io["nsa_cmp_pe"][0].rearrange("j b d -> b j d"), s_nsa, eng="gpsimd")
    w2 = sb("w2", [128, 2, 2, 64], ph)
    for j in range(2):
        t_w2 = dma(w2[:, j, :, :], io["nsa_cmp_w2"][0][j].rearrange("(c p) d -> p c d", p=128), s_nsa, eng="gpsimd")
    t_pe = t_w2
    pc = wcols(W, 2064, 512)
    tkc = []
    for j in range(2):
        b = banks.take()
        m = A(b.t[:, 0:256], pc, j * 128, 128, [h, b.w])
        z = fill(KCm[j][:, 2, :], 0.0)
        for g in range(2):
            s_ = b.t[g * 64:g * 64 + 64, :]
            c = cp(KCm[j][0:64, g, 0:256], s_[:, 0:256], [m])
            c = cp(KCm[j][64:128, g, 0:255], s_[:, 1:256], [m])
        b.w = [c]
        b2 = banks.take()
        m2 = tp(b2.t[0:64, 0:32], pe_sb[:, j, :], [t_pe, t_w2, t_const, b2.w])
        pv = b2.t[0:64, 0:32].rearrange("p (i two) -> p two i", two=2)
        kv = KCm[j][:, 2, 0:32].rearrange("p (i two) -> p two i", two=2)
        c = cp(kv[0:64, 0, :], pv[:, 0, :], [m2, z])
        c = cp(kv[64:128, 0, :], pv[:, 1, :], [m2, z])
        b2.w = [c]
        tkc.append(c)
    b = banks.take()
    m = A(b.t[:, 0:256], pc, 256, 128, [h, b.w])
    tkb = [cp(kb[0][:, :], b.t[:, 0:256], [m])]
    b.w = [tkb[0]]
    tvb = [[], []]
    for hf in range(2):
        b = banks.take()
        m = Bm(b.t[:, 0:128], pc, 384, 128, hf, [h, b.w])
        b.w = [cp(vb[0][:, hf, :], b.t[:, 0:128], [m])]
        tvb[0] += b.w
    pc.done(m)
    step()
    pc = wcols(W, 2576, 280)
    b = banks.take()
    m = A(b.t[:, 0:256], pc, 0, 128, [h, b.w])
    tkb.append(cp(kb[1][:, :], b.t[:, 0:256], [m]))
    b.w = [tkb[1]]
    tg = []
    for hf in range(2):
        b = banks.take()
        m = Bm(b.t[:, 0:152], pc, 128, 152, hf, [h, b.w])
        c = cp(vb[1][:, hf, :], b.t[:, 0:128], [m])
        tvb[1].append(c)
        c = act(gt[:, hf, :], b.t[:, 128:152], AF.Exp, [c], scale=-1.0)
        b.w = [c]
        tg.append(c)
    pc.done(m)
    step()
    t = ts(gt[:, :, :], gt[:, :, :], 1.0, ALU.add, w=tg)
    t_gt = recip(gt[:, :, :], gt[:, :, :], [t])

    hid = sb("hid", [128, 2, 2, 2, 16], ph)
    hx = sb("hx", [128, 3, 15], ph)
    hb = sb("hb", [128, 1], ph)
    hy = sb("hy", [128, 2, 15], ph)
    hz = sb("hz", [128, 2, 15], ph)
    z = fill(hid[:, :, :, :, :].rearrange("p a b c d -> p (a b c d)"), 0.0)
    thid = []
    tfree = []
    for j in range(2):
        pc = load(io["nsa_cmp_w1"][0][j].rearrange("(i p) n -> p i n", p=128), (16, 256))
        for c_ in range(2):
            b = banks.take()
            rv = KCm[j][:, :, 0:240].rearrange("p g (n s) -> p g n s", s=16)
            pairs = []
            for i in range(16):
                r = KCm[j][:, :, 2 * i:2 * i + 225 - 1]
                ap = list(r.ap)
                r2 = bass.AP(tensor=r.tensor, offset=r.offset, ap=[ap[0], ap[1], [16, 15]])
                pairs.append((pc.ap[:, i, c_ * 128:(c_ + 1) * 128], r2))
            m = chain(b.t[:, 0:45], pairs, [pc.tok, tkc[j], tfree, b.w])
            t = cp(hb[:, :], b.t[:, 30:31], [m, tfree])
            x_ = hx[:, 0:2, :]
            t = ts(x_, b.t[:, 0:30].rearrange("p (g n) -> p g n", n=15), hb[:, 0:1], ALU.add, w=[t, tfree])
            b.w = [t]
            t2 = tt(hy[:, :, :], x_, x_, ALU.mult, [t, tfree])
            t2 = ts(hy[:, :, :], hy[:, :, :], 0.044715, ALU.mult, 1.0, ALU.add, w=[t2])
            t2 = tt(hy[:, :, :], hy[:, :, :], x_, ALU.mult, [t2])
            t2 = act(hz[:, :, :], hy[:, :, :], AF.Exp, [t2, tfree], scale=-2.0 * 0.7978845608028654)
            t2 = ts(hz[:, :, :], hz[:, :, :], 1.0, ALU.add, w=[t2])
            t2 = recip(hz[:, :, :], hz[:, :, :], [t2])
            t2 = tt(hid[:, j, c_, :, 0:15], x_, hz[:, :, :], ALU.mult, [t2, z])
            tfree = [t2]
            thid.append(t2)
        pc.done(m)
        step()
    kcT = sb("kcT", [128, 16], ph)
    b = banks.take()
    for g in range(2):
        m = chain(b.t[g * 64:g * 64 + 64, 0:16], [(w2[:, 0, c_, :], hid[:, 0, c_, g, :]) for c_ in range(2)], [thid, t_w2, b.w])
    t_kcT = cp(kcT[:, :], b.t[:, 0:16], [m])
    b.w = [t_kcT]
    vbd = sb("vbd", [128, 8, 64], ph)
    b = banks.take()
    hrep = sb("hrep", [128, 2, 8, 16], ph)
    for c_ in range(2):
        t = cp(hrep[:, c_, :, :].rearrange("p (g r) n -> p g r n", r=4), bc(hid[:, 1, c_, :, :], 2, 4), [thid])
    m = chain(b.t[:, 0:64], [(hrep[:, c_, :, :].rearrange("p a n -> p (a n)"), w2[:, 1, c_, :]) for c_ in range(2)], [t, t_w2, b.w])
    vct = sb("vct", [128, 64], ph)
    t = cp(vct[:, :], b.t[:, 0:64], [m])
    b.w = [t]
    t_vbd = tt(vbd[:, :, :], bc(vct[:, :], 1, 8), bc(K["blockdiag"][:, :], 2, 64), ALU.mult, [t, t_hc])

    nb = sb("nb", [128, 2, 512], ph)
    S = sb("S", [128, 8, 256], ph)
    PT = sb("PT", [128, 8, 2, 128], ph)
    mx = sb("mx", [128, 8], ph)
    sm = sb("sm", [128, 8], ph)
    fac = sb("fac", [128, 8], ph)
    tmp = sb("tmp", [128, 8, 64], ph)
    slope = [2.0 ** -(i + 1) for i in range(8)]
    free_S, free_PT, free_sm, free_tmp = [], [], [], []
    t_nb = [None, None]
    for hf in range(2):
        q_ = slice(hf * 128, hf * 128 + 128)
        Sc = S[:, 0:8, 0:16]
        t = free_S
        bks = []
        for g in range(2):
            b = banks.take()
            for j in range(4):
                m = mm(b.t[:, j * 16:(j + 1) * 16], qT[g * 64:g * 64 + 64, j, q_], kcT[g * 64:g * 64 + 64, :], w=[tnq, t_kcT, b.w])
            for j in range(4):
                hd = g * 4 + j
                c = stt(S[:, hd, 0:16], K["distc"][:, hf * 16:(hf + 1) * 16], -slope[hd], b.t[:, j * 16:(j + 1) * 16], ALU.mult, ALU.add, [m, t, t_hc])
            b.w = [c]
        t = red(mx[:, :], Sc, ALU.max, [c, free_sm], negate=True)
        t = ts(mx[:, :], mx[:, :], 1e20, ALU.min, w=[t])
        t = tt(Sc, Sc, bc(mx[:, :], 2, 16), ALU.add, [t])
        t = act(Sc, Sc, AF.Exp, [t])
        t2 = red(sm[:, :], Sc, ALU.add, [t])
        t2 = ts(sm[:, :], sm[:, :], 1e-20, ALU.max, w=[t2])
        t2 = recip(sm[:, :], sm[:, :], [t2])
        t_fac = tt(fac[:, :], sm[:, :], gt[:, hf, :].rearrange("p (a c) -> p c a", c=3)[:, 0, :], ALU.mult, [t2, t_gt])
        pcm = sb(f"pcm{hf}", [128, 128], ph)
        t = cp(pcm[:, :].rearrange("p (a n) -> p a n", n=16), Sc, [t])
        free_S = [t]
        b = banks.take()
        m = tp(b.t[:, 0:128], pcm[:, :], [t, b.w])
        t = cp(PT[:, 0, 0, :], b.t[:, 0:128], [m, free_PT])
        b.w = [t]
        b = banks.take()
        m = mm(b.t[:, :], PT[:, 0, 0, :], vbd[:, :, :].rearrange("p a d -> p (a d)"), w=[t, t_vbd, b.w])
        free_PT = [m]
        t = tt(nb[:, hf, :].rearrange("p (a d) -> p a d", d=64), b.t[:, :].rearrange("p (a d) -> p a d", d=64), bc(fac[:, :], 2, 64), ALU.mult, [m, t_fac])
        b.w = [t]
        t_nb[hf] = t
        free_sm = [t]
        nk = (hf + 1) * 128
        for br in range(2):
            per = 512 // nk
            t_p = [None] * 8
            for g in range(2):
                for j0 in range(0, 4, per):
                    b = banks.take()
                    for j in range(j0, j0 + per):
                        m = mm(b.t[:, (j - j0) * nk:(j - j0 + 1) * nk], qT[g * 64:g * 64 + 64, j, q_], kb[br][g * 64:g * 64 + 64, 0:nk], w=[tnq, tkb[br], b.w])
                    for j in range(j0, j0 + per):
                        hd = g * 4 + j
                        c = stt(S[:, hd, 0:nk], K["dist"][:, 256 - nk:256], -slope[hd], b.t[:, (j - j0) * nk:(j - j0 + 1) * nk], ALU.mult, ALU.add, [m, free_S, t_hc])
                    b.w = [c]
                t = red(mx[:, g * 4:g * 4 + 4], S[:, g * 4:g * 4 + 4, 0:nk], ALU.max, [c, free_sm], negate=True)
                for hd in range(g * 4, g * 4 + 4):
                    t_p[hd] = act(S[:, hd, 0:nk], S[:, hd, 0:nk], AF.Exp, [t, free_sm], bias=mx[:, hd:hd + 1], accum_out=sm[:, hd:hd + 1])
            t2 = recip(sm[:, :], sm[:, :], t_p)
            t_fac = tt(fac[:, :], sm[:, :], gt[:, hf, :].rearrange("p (a c) -> p c a", c=3)[:, br + 1, :], ALU.mult, [t2, t_gt, free_sm])
            t_pt = []
            for hd in range(0, 8, 2):
                b = banks.take()
                for a in range(2):
                    for k in range(hf + 1):
                        m = tp(b.t[:, (a * (hf + 1) + k) * 128:(a * (hf + 1) + k + 1) * 128], S[:, hd + a, k * 128:(k + 1) * 128], [t_p, b.w])
                c = cp(PT[:, hd:hd + 2, 0:hf + 1, :], b.t[:, 0:2 * nk].rearrange("p (a k q) -> p a k q", a=2, q=128), [m, free_PT], eng="scalar" if hd % 4 else "vector")
                b.w = [c]
                t_pt.append(c)
            free_S = [m]
            b = banks.take()
            for hd in range(8):
                g = hd // 4
                m = chain(b.t[:, hd * 64:(hd + 1) * 64], [(PT[:, hd, k, :], vb[br][:, k, g * 64:g * 64 + 64]) for k in range(hf + 1)], [t_pt, tvb[br], b.w])
            free_PT = [m]
            t = tt(tmp[:, :, :], b.t[:, :].rearrange("p (a d) -> p a d", d=64), bc(fac[:, :], 2, 64), ALU.mult, [m, t_fac, free_tmp])
            b.w = [t]
            free_sm = [t]
            dst = nb[:, hf, :] if br == 0 else mix[:, hf, 512:1024]
            t_nb[hf] = tt(dst.rearrange("p (a d) -> p a d", d=64), nb[:, hf, :].rearrange("p (a d) -> p a d", d=64), tmp[:, :, :], ALU.add, [t, t_nb[hf]])
            free_tmp = [t_nb[hf]]
    mixT = sb("mixT", [128, 8, T], ph)
    tm = transposed(mix, 8, mixT, [[t_nb[0], t_gla], [t_nb[1], t_gla]])
    bk, m = project(mixT, 8, io["hyb_w_out"][0], tm)
    gated_add(bk, "hyb", m)
    finish_side()
    prog.barrier()
    ph.close()

    def up3(Wg, nf, epilogue, side_steps=0):
        half = nf * 128
        for c0 in range(0, half, 512):
            n = min(512, half - c0)
            pg, pu = wcols(Wg, c0, n), wcols(Wg, half + c0, n)
            for f0 in range(0, n, 256):
                first = []

                def use_gate(u, first=first):
                    for f in range(0, 256, 128):
                        b = banks.take()
                        first.append((b, A3(b.t[:, 0:256], u, f, [b.w])))
                    u.done(first[-1][1])

                def use_up(u, first=first, i=(c0 + f0) // 128):
                    for f in range(2):
                        b = banks.take()
                        m2 = A3(b.t[:, 0:256], u, f * 128, [b.w])
                        epilogue(i + f, first[f][0], b, first[f][1], m2)
                    u.done(m2)

                put(pg.ap[:, :, f0:f0 + 256], pg, f0 + 256 >= n, use_gate)
                put(pu.ap[:, :, f0:f0 + 256], pu, f0 + 256 >= n, use_up)
            step(side_steps)

    ph = ExitStack()
    sg = [[sb(f"sg{i}", [128, T], ph), []] for i in range(2)]
    hTh, hTl = sb("hTh", [128, 22, T], ph, R32), sb("hTl", [128, 22, T], ph, R32)
    new_HT(ph, "1", True)
    new_units(ph, "1")
    side.append(adaln("ssm", 2))
    side.append(adaln("moe", 0))
    HTf = sg
    h = modulated("dense")
    prog.hold["tensor"] += h
    t = []

    def gated(i, bg, bu, m1, m2):
        s_ = sg[i % 2]
        a = silu_of(s_[0][:, :], bg.t[:, 0:256], [m1, s_[1]])
        bg.w = [a]
        c = tt(s_[0][:, :], s_[0][:, :], bu.t[:, 0:256], ALU.mult, [m2, a])
        bu.w = [c]
        s_[1] = [hi_lo(hTh[:, i, :], hTl[:, i, :], s_[0][:, :], [c])]
        t.append(s_[1][0])

    up3(io["dense_w_gu"][0], 22, gated, 3)
    finish_side()
    project3(hTh, hTl, 22, io["dense_w_down"][0], t, 2, lambda bk, m: gated_add(bk, "dense", m))
    drain()
    prog.barrier()
    ph.close()
    pmacc.close()

    ph = ExitStack()
    W = io["ssm_w_in"][0]
    zs = sb("zs", [128, 2, 2048], ph)
    xt = sb("xt", [128, 2, 2048], ph)
    BC = sb("BC", [128, 8, T], ph)
    cv = [[sb(f"cv{i}", [128, T], ph), []] for i in range(3)]
    xs = [[sb(f"xs{i}", [128, T], ph), []] for i in range(2)]
    dcol = sb("dcol", [32, 4], ph)
    drow = sb("drow", [128, 32], ph)
    s_m = dsem("s_mamba")
    for i, n in enumerate(("ssm_dt_bias", "ssm_a_log")):
        dma(dcol[:, i:i + 1], io[n][0].rearrange("(p a) -> p a", a=1), s_m, prog.last(), eng="gpsimd")
    t_dc = dma(drow[:, :], io["ssm_d"][0].partition_broadcast(128), s_m, eng="gpsimd")
    new_HT(ph, "2")
    h = modulated("ssm")
    pc = wcols(W, 5120, 32)
    b = banks.take()
    m = A(b.t[0:32, 0:256], pc, 0, 32, [h, b.w])
    pc.done(m)
    dtT = sb("dtT", [32, T], ph)
    daT = sb("daT", [32, T], ph)
    cmT = sb("cmT", [32, T], ph)
    lnexp()
    t1 = ts(dtT[:, :], b.t[0:32, 0:256], dcol[:, 0:1], ALU.add, w=[m, t_dc])
    b.w = [t1]
    t = act(daT[:, :], dtT[:, :], AF.Abs, [t1])
    t = act(daT[:, :], daT[:, :], AF.Exp, [t], scale=-1.0)
    t = act(daT[:, :], daT[:, :], AF.Ln, [t], bias=1.0)
    t_dt = stt(dtT[:, :], dtT[:, :], 0.0, daT[:, :], ALU.max, ALU.add, [t])
    t2 = act(dcol[:, 2:3], dcol[:, 1:2], AF.Exp, [t_dc])
    t = ts(daT[:, :], dtT[:, :], dcol[:, 2:3], ALU.mult, -1.0, ALU.mult, w=[t2, t_dt])
    onesr = sb("onesr", [32, T], ph)
    z = fill(onesr[:, :], 1.0)
    t_cm = scan(cmT[:, :], onesr[:, :], daT[:, :], [t, z])
    dtc = sb("dtc", [128, 2, 32], ph)
    cmc = sb("cmc", [128, 2, 32], ph)
    b = banks.take()
    for hf in range(2):
        m = tp(b.t[:, hf * 32:hf * 32 + 32], dtT[:, hf * 128:(hf + 1) * 128], [t_dt, b.w])
    for hf in range(2):
        m = tp(b.t[:, 64 + hf * 32:96 + hf * 32], cmT[:, hf * 128:(hf + 1) * 128], [t_cm])
    cp(dtc[:, :, :].rearrange("p a b -> p (a b)"), b.t[:, 0:64], [m])
    t_cols = cp(cmc[:, :, :].rearrange("p a b -> p (a b)"), b.t[:, 64:128])
    b.w = [t_cols]
    tz = []
    for c0 in range(0, 2048, 512):
        pc = wcols(W, c0, 512)
        for hf in range(2):
            b = banks.take()
            m = Bm(b.t[:, :], pc, 0, 512, hf, [h, b.w])
            b.w = [silu_of(zs[:, hf, c0:c0 + 512], b.t[:, :], [m])]
            tz.append(b.w[0])
        pc.done(m)
    t_x2, t_bc = [], []
    cw, cb = vec["conv_w"], vec["conv_b"]
    for r in range(24):
        if r % 4 == 0:
            pc = wcols(W, 2048 + r * 128, 512)
        b = banks.take()
        m = A(b.t[:, 0:256], pc, (r % 4) * 128, 128, [h, b.w])
        if r % 4 == 3:
            pc.done(m)
        c_, x_ = cv[r % 3], xs[r % 2]
        t = act(c_[0][:, :], b.t[:, 0:256], AF.Identity, [m, c_[1], vec_tok["conv_w"], vec_tok["conv_b"]], scale=cw[:, 72 + r:73 + r], bias=cb[:, r:r + 1])
        for j in (2, 1, 0):
            n = 3 - j
            t = stt(c_[0][:, n:T], b.t[:, 0:T - n], cw[:, j * 24 + r:j * 24 + r + 1], c_[0][:, n:T], ALU.mult, ALU.add, [t])
        b.w = [t]
        if r < 16:
            t = silu_of(x_[0][:, :], c_[0][:, :], [t, x_[1]])
            c_[1] = [t]
            b = banks.take()
            for hf in range(2):
                m2 = tp(b.t[:, hf * 128:(hf + 1) * 128], x_[0][:, hf * 128:(hf + 1) * 128], [t, b.w])
            x_[1] = [m2]
            b.w = [cp(xt[:, :, r * 128:(r + 1) * 128], b.t[:, 0:256].rearrange("p (h n) -> p h n", h=2), [m2], eng="scalar" if r % 2 else "vector")]
            t_x2.append(b.w[0])
        else:
            t = silu_of(BC[:, r - 16, :], c_[0][:, :], [t])
            c_[1] = [t]
            t_bc.append(t)
    lnexp()
    CB = sb("CB", [128, 4, 384], ph)
    t_cb = []
    for g in range(4):
        b = banks.take()
        mm(b.t[:, 0:256], BC[:, g, 0:128], BC[:, 4 + g, :], w=[t_bc, b.w])
        m = mm(b.t[:, 256:384], BC[:, g, 128:256], BC[:, 4 + g, 128:256])
        c = tt(CB[:, g, 0:128], b.t[:, 0:128], K["causal"][:, :], ALU.mult, [m, t_const])
        c = cp(CB[:, g, 128:256], b.t[:, 128:256])
        c = tt(CB[:, g, 256:384], b.t[:, 256:384], K["causal"][:, :], ALU.mult)
        b.w = [c]
        t_cb.append(c)
    EB = [[sb(f"eb{i}", [128, 384], ph), []] for i in range(4)]
    xd = [[sb(f"xd{i}", [128, 512], ph), []] for i in range(2)]
    ys = sb("ys", [128, 8], ph)
    t_y = []
    rowbanks = Banks(allbanks[0:4])
    ybanks = Banks(allbanks[4:8])
    for g in range(4):
        yb = [ybanks.take() for _ in range(2)]
        for r in range(8):
            hd = g * 8 + r
            e_ = EB[hd % 4]
            b = rowbanks.take()
            m = mm(b.t[:, 0:256], K["ident"][0:32, hd:hd + 1].to_broadcast([32, 128]), cmT[:, :], w=[t_cm, b.w])
            t = ts(e_[0][:, 0:256], b.t[:, 0:256], cmc[:, 0, hd:hd + 1], ALU.subtract, 0.0, ALU.min, w=[m, t_cols, e_[1]])
            t = ts(e_[0][:, 256:384], b.t[:, 128:256], cmc[:, 1, hd:hd + 1], ALU.subtract, 0.0, ALU.min)
            b.w = [t]
            t = act(e_[0][:, :], e_[0][:, :], AF.Exp, [t])
            t = stt(e_[0][:, 0:256], e_[0][:, 0:256], dtc[:, 0, hd:hd + 1], CB[:, g, 0:256], ALU.mult, ALU.mult, [t, t_cb])
            t = stt(e_[0][:, 256:384], e_[0][:, 256:384], dtc[:, 1, hd:hd + 1], CB[:, g, 256:384], ALU.mult, ALU.mult)
            c0 = hd * 64
            m0 = mm(yb[0].t[:, r * 64:(r + 1) * 64], e_[0][:, 0:128], xt[:, 0, c0:c0 + 64], w=[t, t_x2, yb[0].w])
            m1 = chain(yb[1].t[:, r * 64:(r + 1) * 64], [(e_[0][:, 128:256], xt[:, 0, c0:c0 + 64]), (e_[0][:, 256:384], xt[:, 1, c0:c0 + 64])], [yb[1].w])
            e_[1] = [m1]
        for hf in range(2):
            x_ = xd[hf]
            sl = slice(g * 512, (g + 1) * 512)
            t = tt(x_[0][:, :].rearrange("p (r d) -> p r d", d=64), xt[:, hf, sl].rearrange("p (r d) -> p r d", d=64),
                   bc(drow[:, g * 8:g * 8 + 8], 2, 64), ALU.mult, [x_[1], t_x2, t_dc], eng="gpsimd")
            t = tt(x_[0][:, :], yb[hf].t[:, :], x_[0][:, :], ALU.add, [t, m1])
            yb[hf].w = [t]
            t = tt(zs[:, hf, sl], zs[:, hf, sl], x_[0][:, :], ALU.mult, [t, tz], eng="gpsimd")
            a = act(x_[0][:, :], zs[:, hf, sl], AF.Square, [t], accum_out=ys[:, hf * 4 + g:hf * 4 + g + 1])
            x_[1] = [a]
            t_y.append(a)
    t = ts(ys[:, :], ys[:, :], 1.0 / 512, ALU.mult, EPS, ALU.add, w=t_y)
    t = act(ys[:, :], ys[:, :], AF.Ln, [t])
    t = act(ys[:, :], ys[:, :], AF.Exp, [t], scale=-0.5)
    tn = []
    for hf in range(2):
        for g in range(4):
            c = ts(zs[:, hf, g * 512:(g + 1) * 512], zs[:, hf, g * 512:(g + 1) * 512], ys[:, hf * 4 + g:hf * 4 + g + 1], ALU.mult, w=[t])
        tn.append(c)
    yT = xt[:, :, :].rearrange("p h (a t) -> p (h a) t", t=T)
    ty = transposed(zs, 16, yT, tn, vec["gate_norm"], [m1, t_y])
    bk, m = project(yT, 16, io["ssm_w_out"][0], ty)
    gated_add(bk, "ssm", m)
    prog.barrier()
    ph.close()

    ph = ExitStack()
    rw = sb("rw", [128, KC, NE], ph)
    s_r = dsem("s_router")
    t_rw = dma(rw[:, :, :], io["moe_router"][0].rearrange("(k p) e -> p k e", p=128), s_r, prog.last(), eng="gpsimd")
    new_HT(ph, "3")
    h = modulated("moe")
    L = sb("L", [128, 2, NE], ph)
    gt = sb("egate", [128, 2, NE], ph)
    sel = sb("esel", [128, 2, NE], ph)
    pos = sb("epos", [128, 2, NE], ph)
    pr = sb("pr", [128, 2, 64], ph)
    e1_ = sb("e1_", [128, 2], ph)
    b = banks.take()
    for hf in range(2):
        m = chain(b.t[:, hf * 8:hf * 8 + 8], [(HT[:, k, hf * 128:(hf + 1) * 128], rw[:, k, :]) for k in range(KC)], [h, t_rw, b.w])
    t_L = cp(L[:, :, :].rearrange("p h e -> p (h e)"), b.t[:, 0:16], [m])
    b.w = [t_L]
    t_gate, t_sel = [], []
    for hf in range(2):
        p1 = pr[:, 0, :].rearrange("p (e j) -> p e j", j=8)
        p2 = pr[:, 1, :].rearrange("p (e j) -> p e j", j=8)
        lj, le = bc(L[:, hf, :], 1, 8), bc(L[:, hf, :], 2, 8)
        t = tt(p1, lj, le, ALU.is_equal, [t_L, t_gate])
        t = tt(pr[:, 0, :], pr[:, 0, :], K["tie"][:, :], ALU.mult, [t, t_const])
        t2 = tt(p2, lj, le, ALU.is_gt, [t_L, t_gate])
        t = tt(p1, p1, p2, ALU.add, [t, t2])
        t = red(sel[:, hf, :], p1, ALU.add, [t])
        t = ts(sel[:, hf, :], sel[:, hf, :], 1.5, ALU.is_lt, w=[t])
        t_sel.append(t)
        t3 = red(e1_[:, hf:hf + 1], L[:, hf, :], ALU.max, [t_L], negate=True)
        t3 = act(L[:, hf, :], L[:, hf, :], AF.Exp, [t3, t2], bias=e1_[:, hf:hf + 1])
        t = tt(gt[:, hf, :], sel[:, hf, :], L[:, hf, :], ALU.mult, [t, t3])
        t = red(e1_[:, hf:hf + 1], gt[:, hf, :], ALU.add, [t])
        t = recip(e1_[:, hf:hf + 1], e1_[:, hf:hf + 1], [t])
        t_gate.append(ts(gt[:, hf, :], gt[:, hf, :], e1_[:, hf:hf + 1], ALU.mult, w=[t]))
    b = banks.take()
    mm(b.t[:, 0:8], K["before"][:, :], sel[:, 0, :], w=[t_sel, b.w])
    chain(b.t[:, 8:16], [(ones[:, :], sel[:, 0, :]), (K["before"][:, :], sel[:, 1, :])])
    m = chain(b.t[:, 16:24], [(ones[:, :], sel[:, 0, :]), (ones[:, :], sel[:, 1, :])])
    t_pos = cp(pos[:, :, :].rearrange("p h e -> p (h e)"), b.t[:, 0:16], [m])
    fl = sb("fl", [1, 2], ph)
    fli = sb("fli", [1, 1], ph, mybir.dt.int32)
    t = red(fl[:, 0:1], b.t[0:1, 16:24], ALU.max)
    b.w = [t]
    t = ts(fl[:, 1:2], fl[:, 0:1], CAP + 0.5, ALU.is_gt, w=[t])
    t_flag = cp(fli[:, :], fl[:, 1:2], [t])

    acc = sb("eacc", [128, 2, D], ph)
    hTh, hTl = sb("ehTh", [128, 28, 128], ph, R32), sb("ehTl", [128, 28, 128], ph, R32)
    XGh, XGl = sb("XGh", [128, KC, 128], ph, R32), sb("XGl", [128, KC, 128], ph, R32)
    XGf, Y = HT[:, 0:4, :].rearrange("p a (b s) -> p (a b) s", s=128), HT[:, 4:8, :].rearrange("p a b -> p (a b)")
    Pe, PT = sb("Pe", [128, 2, 128], ph), [sb(f"PTe{i}", [128, 2, 128], ph) for i in range(2)]
    hrow = [[sb(f"hrow{i}", [128, 512], ph), []] for i in range(2)]
    new_units(ph, "3")
    s1, s2, g, slot, toks = mod["moe"]
    free = {"hT": [], "XG": [], "Y": [m], "XGf": [m], "PT": [[], []], "Pe": []}
    t_acc = [[None, None], [None, None]]
    dbanks = allbanks[6:8]
    ubanks = Banks(allbanks[0:6])
    z = [fill(acc[:, hf, :], 0.0) for hf in range(2)]

    def gather(e, blk):
        for hf in range(2):
            t = ts(Pe[:, hf, :], K["iota"][:, blk * CAP:blk * CAP + 128], pos[:, hf, e:e + 1], ALU.is_equal, sel[:, hf, e:e + 1], ALU.mult, w=[t_pos, t_sel, free["Pe"]])
            if CAP < 128:
                t = fill(Pe[:, hf, CAP:128], 0.0, [t])
        b = ubanks.take()
        for hf in range(2):
            m = tp(b.t[:, hf * 128:(hf + 1) * 128], Pe[:, hf, :], [t, b.w])
        t_pt = cp(PT[e % 2][:, :, :].rearrange("p h t -> p (h t)"), b.t[:, 0:256], [m, free["PT"][e % 2]])
        b.w = [t_pt]
        for k0 in range(0, KC, 4):
            b = ubanks.take()
            for k in range(k0, k0 + 4):
                m = chain(b.t[:, (k - k0) * 128:(k - k0 + 1) * 128], [(xn[:, hf, k * 128:(k + 1) * 128], Pe[:, hf, :]) for hf in range(2)], [t, b.w])
            for k in range(k0, k0 + 4):
                c = ts(XGf[:, k, :], b.t[:, (k - k0) * 128:(k - k0 + 1) * 128], s1[:, k:k + 1], ALU.mult, s2[:, k:k + 1], ALU.add, w=[m, toks, free["XGf"]])
            b.w = [c]
        free["Pe"] = [m]
        t_xg = hi_lo(XGh[:, :, :], XGl[:, :, :], XGf, [c], free["XG"])
        free["XGf"] = [t_xg]
        return t_pt, t_xg

    class Late:
        h, put = None, None

    def experts(blk):
        late = Late()
        where = {0: gather(0, blk)}

        def turned(j, hr, c, t_h):
            b = ubanks.take()
            for a in range(4):
                m = tp(b.t[:, a * 128:(a + 1) * 128], hr[0][:, a * 128:(a + 1) * 128], [c, b.w])
            hr[1] = [m]
            v = lambda x: x[:, 4 * j:4 * j + 4, :].rearrange("p a s -> p (a s)")
            t = hi_lo(v(hTh), v(hTl), b.t[:, :], [m], free["hT"])
            b.w = [t]
            t_h[4 * j:4 * j + 4] = [t] * 4

        def use_up(u, e, j, p_, k0, cur):
            if k0 == 0:
                cur.append([ubanks.take(), None])
            b = cur[p_][0]
            t_xg = where[e][1]
            for k in range(4):
                first, last = k0 + k == 0, k0 + k == KC - 1
                mm(b.t[:, :], XGh[:, k0 + k, :], u.hi[:, k, :], first, False, [u.tok, t_xg, b.w])
                mm(b.t[:, :], XGh[:, k0 + k, :], u.lo[:, k, :], False, False)
                m = mm(b.t[:, :], XGl[:, k0 + k, :], u.hi[:, k, :], False, last)
            u.done(m)
            cur[p_][1] = m
            if p_ == 0 and k0 and late.h:
                turned(*late.h)
                late.h = None
            if p_ == 1 and k0:
                hr = hrow[j % 2]
                (b1, m1), (b2, m2) = cur
                a = silu_of(hr[0][:, :], b1.t[:, :], [m1, hr[1]])
                b1.w = [a]
                c = tt(hr[0][:, :], hr[0][:, :], b2.t[:, :], ALU.mult, [a, m2])
                b2.w = [c]
                late.h = (j, hr, c, t_hs[e])
                if j == 6:
                    free["XG"] = [m2]

        def use_end(e, bk, m):
            free["hT"] = [m[0][1]]
            t_y = []
            for i in range(2):
                c = cp(Y[:, i * 512:(i + 1) * 512], dbanks[i].t[:, :], [m[0][i], free["Y"]], eng="scalar" if i else "vector")
                dbanks[i].w = [c]
                t_y.append(c)
            late.put = (e, t_y)

        def put_back(e, t_y):
            for hf in range(2):
                for i in range(2):
                    b = ubanks.take()
                    m = mm(b.t[:, :], PT[e % 2][:, hf, :], Y[:, i * 512:(i + 1) * 512], w=[t_y, where[e][0], b.w])
                    o = acc[:, hf, i * 512:(i + 1) * 512]
                    c = stt(o, b.t[:, :], gt[:, hf, e:e + 1], o, ALU.mult, ALU.add, [m, t_acc[hf][i], z, t_gate])
                    b.w = [c]
                    t_acc[hf][i] = c
            free["Y"] = [m]
            free["PT"][e % 2] = [m]

        t_hs = [[None] * 28 for _ in range(NE)]
        for e in range(NE):
            Wg, Wd = io["moe_w_gu"][0][e], io["moe_w_down"][0][e]
            for j in range(7):
                cur = []
                for p_ in range(2):
                    pc = wcols(Wg, p_ * FE + j * 512, 512)
                    for k0 in range(0, KC, 4):
                        def use(u, e=e, j=j, p_=p_, k0=k0, cur=cur):
                            use_up(u, e, j, p_, k0, cur)
                            if j == 0 and p_ == 1 and k0 and late.put:
                                put_back(*late.put)
                                late.put = None
                        put(pc.ap[:, k0:k0 + 4, :], pc, k0 > 0, use)

            def begin_down(e=e):
                turned(*late.h)
                late.h = None
                if e + 1 < NE:
                    where[e + 1] = gather(e + 1, blk)

            project3(hTh, hTl, 28, Wd, t_hs[e], 1, lambda bk, m, e=e: use_end(e, bk, m), [dbanks], begin_down)
        drain()
        put_back(*late.put)

    experts(0)
    prog.begin_if(fli[0:1, 0:1], t_flag)
    experts(1)
    prog.end_if()
    for hf in range(2):
        t = tt(acc[:, hf, :], acc[:, hf, :], g[:, :], ALU.mult, t_acc[hf])
        t_X[hf] = tt(X[:, hf, :], X[:, hf, :], acc[:, hf, :], ALU.add, [t])
    fn_ = gates[1]
    t_fn = dma(fn_[:, :], io["final_norm"].partition_broadcast(128), dsem("s_fn"), prog.last(), eng="gpsimd")
    xn_free = t_X
    t2 = rms(xn)
    t_X = [tt(X[:, hf, :], xn[:, hf, :], fn_[:, :], ALU.mult, [t2[hf], t_fn]) for hf in range(2)]
    xn_free = t_X
    prog.barrier()
    ph.close()

    pfirst.close()
    for l in range(2):
        ph = ExitStack()
        Wl = io["w_in_2"][l]
        lnr = sb(f"lnr{l}", [128, 2, D], ph)
        s_l = dsem(f"s_ln{l}")
        for i, n in enumerate(("ln1_g_2", "ln1_b_2")):
            dma(lnr[:, i, :], io[n][l].partition_broadcast(128), s_l, prog.last(), eng="gpsimd")
        hcol = sb(f"hcol{l}", [64, 4], ph)
        for i, n in enumerate(("gdn_dt_bias_2", "gdn_a_log_2")):
            dma(hcol[0:4, i:i + 1], io[n][l].rearrange("(p a) -> p a", a=1), s_l, eng="gpsimd")
        gnr = sb(f"gnr{l}", [128, 128], ph)
        t_l = dma(gnr[:, :], io["gdn_norm_g_2"][l].partition_broadcast(128), s_l, eng="gpsimd")
        st = sb(f"st{l}", [128, 2, 2, 6], ph)
        mv = sb(f"mv{l}", [128, 2, 2], ph)
        rs_ = sb(f"rs_{l}", [128, 2], ph)
        s_lt = dsem(f"s_lt{l}")
        pm = ExitStack()
        for n in ("levels", "cmask", "cos", "sin", "perm", "reset128"):
            K[n] = sb(f"k_{n}{l}", [128, cn[n].shape[1]], pm)
            t_lt = dma(K[n][:, :], cn[n], s_lt, prog.last(), eng="gpsimd")
        mix = sb(f"mix{l}", [128, 2, D], pm)
        pg = ExitStack()
        new_HT(pm, f"m{l}")
        h, m = to_HT(X, t_X)
        qk = sb(f"qk{l}", [128, 12, T], pg)
        cv = [[sb(f"gcv{l}{i}", [128, T], pg), []] for i in range(3)]
        gcw = vec[f"gconv{l}"]
        tc = []
        for r in range(12):
            if r % 4 == 0:
                pc = wcols(Wl, r * 128, 512)
            b = banks.take()
            m = A(b.t[:, 0:256], pc, (r % 4) * 128, 128, [h, b.w])
            if r % 4 == 3:
                pc.done(m)
            c_ = cv[r % 3]
            t = act(c_[0][:, :], b.t[:, 0:256], AF.Copy, [m, c_[1], vec_tok[f"gconv{l}"]], scale=gcw[:, 36 + r:37 + r])
            for j in (2, 1, 0):
                n = 3 - j
                t = stt(c_[0][:, n:T], b.t[:, 0:T - n], gcw[:, j * 12 + r:j * 12 + r + 1], c_[0][:, n:T], ALU.mult, ALU.add, [t])
            b.w = [t]
            t = silu_of(qk[:, r, :], c_[0][:, :], [t])
            c_[1] = [t]
            tc.append(t)
        zsl = sb(f"zsl{l}", [128, 2, 512], pg)
        pc = wcols(Wl, 1536, 520)
        bab = banks.take()
        A(bab.t[0:4, 0:256], pc, 0, 4, [h, bab.w])
        m_ab = A(bab.t[32:36, 0:256], pc, 4, 4, [h])
        tz = []
        for hf in range(2):
            b = banks.take()
            m = Bm(b.t[:, :], pc, 8, 512, hf, [h, b.w])
            b.w = [silu_of(zsl[:, hf, :], b.t[:, :], [m])]
            tz.append(b.w[0])
        pc.done(m)
        lnexp()
        gb = sb(f"gb{l}", [64, T], pg)
        ga = sb(f"ga{l}", [64, T], pg)
        z = fill(gb[:, :], 0.0)
        t1 = ts(ga[0:4, :], bab.t[0:4, 0:256], hcol[0:4, 0:1], ALU.add, w=[m_ab, t_l])
        t2 = act(ga[32:36, :], bab.t[32:36, 0:256], AF.Exp, [m_ab, t1], scale=-1.0)
        bab.w = [t2]
        gc = sb(f"gc{l}", [4, T], pg)
        t = act(gc[:, :], ga[0:4, :], AF.Abs, [t1])
        t = act(gc[:, :], gc[:, :], AF.Exp, [t], scale=-1.0)
        t = act(gc[:, :], gc[:, :], AF.Ln, [t], bias=1.0)
        t = stt(ga[0:4, :], ga[0:4, :], 0.0, gc[:, :], ALU.max, ALU.add, [t])
        t3 = act(hcol[0:4, 2:3], hcol[0:4, 1:2], AF.Exp, [t_l])
        t = ts(ga[0:4, :], ga[0:4, :], hcol[0:4, 2:3], ALU.mult, -1.0, ALU.mult, w=[t, t3])
        t4 = scan(gb[0:4, :], K["reset128"][0:4, :], ga[0:4, :], [t, z, t_l, t_lt])
        t = ts(ga[32:36, :], ga[32:36, :], 1.0, ALU.add, w=[t2])
        t5 = recip(gb[32:36, :], ga[32:36, :], [t, z])
        col = sb(f"col{l}", [128, 2, 64], pg)
        b = banks.take()
        for hf in range(2):
            m = tp(b.t[:, hf * 64:hf * 64 + 64], gb[:, hf * 128:(hf + 1) * 128], [t4, t5, b.w])
        t_col = cp(col[:, :, :].rearrange("p h c -> p (h c)"), b.t[:, 0:128], [m])
        b.w = [t_col]
        eg = sb(f"eg_{l}", [128, 8], pg)
        nbe = sb(f"nbe{l}", [128, 4], pg)
        t_eg = act(eg[:, :].rearrange("p (h a) -> p h a", h=2), col[:, :, 0:4], AF.Exp, [t_col])
        t_nbe = stt(nbe[:, :], eg[:, 4:8], -1.0, col[:, 1, 32:36], ALU.mult, ALU.mult, [t_eg])
        sq = sb(f"sq{l}", [128, 8, T], pg)
        t_qk = []
        for j in range(4):
            r = 2 * j
            t = tt(sq[:, r:r + 2, :], qk[:, r:r + 2, :], qk[:, r:r + 2, :], ALU.mult, tc)
            b = banks.take()
            for a in range(2):
                m = mm(b.t[:, a * 256:(a + 1) * 256], ones[:, :], sq[:, r + a, :], w=[t, t_ones, b.w])
            sv = sq[:, r:r + 2, :].rearrange("p a t -> p (a t)")
            t = ts(sv, b.t[:, :], EPS, ALU.add, w=[m])
            b.w = [t]
            t = act(sv, sv, AF.Ln, [t])
            t = act(sv, sv, AF.Exp, [t], scale=-0.5)
            qv = qk[:, r:r + 2, :].rearrange("p a t -> p (a t)")
            if j < 2:
                t_qk.append(stt(qv, qv, 128 ** -0.5, sv, ALU.mult, ALU.mult, [t]))
            else:
                t_qk.append(tt(qv, qv, sv, ALU.mult, [t]))
        vtm = sb(f"vtm{l}", [128, 2, 4, 128], pg)
        kd = sb(f"kd{l}", [128, 4, 128], pg)
        t_v = []
        for hf in range(2):
            b = banks.take()
            for a in range(4):
                m = tp(b.t[:, a * 128:(a + 1) * 128], qk[:, 8 + a, hf * 128:(hf + 1) * 128], [tc, b.w])
            c = tt(vtm[:, hf, :, :], b.t[:, :].rearrange("p (a d) -> p a d", d=128), bc(col[:, hf, 32:36], 2, 128), ALU.mult, [m, t_col])
            b.w = [c]
            t_v.append(c)
        DT = sb(f"DT{l}", [128, 8, 128], pg)
        ATb = sb(f"ATb{l}", [128, 8, 128], pg)
        AAb = sb(f"AAb{l}", [128, 8, 128], pg)
        t_dt, t_att, t_aa = [], [], []
        t_bt = []
        brow = sq[:, 0:4, :]
        for a in range(4):
            b = banks.take()
            m1 = mm(b.t[:, 0:256], K["ident"][0:64, a:a + 1].to_broadcast([64, 128]), gb[:, :], w=[t4, t5, t_l, b.w])
            m1 = mm(b.t[:, 256:512], K["ident"][0:64, 32 + a:33 + a].to_broadcast([64, 128]), gb[:, :])
            for c_ in range(2):
                t = ts(DT[:, c_ * 4 + a, :], b.t[:, c_ * 128:(c_ + 1) * 128], col[:, c_, a:a + 1], ALU.subtract, 0.0, ALU.min, w=[m1, t_col])
            t_bt.append(cp(brow[:, a, :], b.t[:, 256:512], [t_qk]))
            b.w = [t_bt[-1]]
            t_dt.append(t)
        t_dx = act(DT[:, :, :], DT[:, :, :], AF.Exp, t_dt)
        b = banks.take()
        for a in range(4):
            m = tp(b.t[:, a * 128:(a + 1) * 128], qk[:, 4 + a, 0:128], [t_qk, b.w])
        t_kd = tt(kd[:, :, :], b.t[:, :].rearrange("p (a d) -> p a d", d=128), bc(DT[:, 0:4, 127], 2, 128), ALU.mult, [m, t_dx])
        b.w = [t_kd]
        t_dm = tt(DT[:, :, :], DT[:, :, :], bc(K["causal"][:, :], 1, 8), ALU.mult, [t_dx, t_kd])
        for c_ in range(2):
            s_ = slice(c_ * 128, (c_ + 1) * 128)
            b, b2 = banks.take(), banks.take()
            for a in range(4):
                m = mm(b.t[:, a * 128:(a + 1) * 128], qk[:, 4 + a, s_], qk[:, a, s_], w=[t_qk, b.w])
            for a in range(4):
                m2 = mm(b2.t[:, a * 128:(a + 1) * 128], qk[:, 4 + a, s_], qk[:, 4 + a, s_], w=[b2.w])
            dv = DT[:, c_ * 4:c_ * 4 + 4, :].rearrange("p a i -> p (a i)")
            c = tt(ATb[:, c_ * 4:c_ * 4 + 4, :].rearrange("p a i -> p (a i)"), b.t[:, :], dv, ALU.mult, [m, t_dm])
            b.w = [c]
            t_att.append(c)
            av = AAb[:, c_ * 4:c_ * 4 + 4, :]
            c = tt(av.rearrange("p a i -> p (a i)"), b2.t[:, :], dv, ALU.mult, [m2, t_dm])
            b2.w = [c]
            t_aa.append(tt(av, av, brow[:, :, s_], ALU.mult, [c, t_bt]))
        Xi = sb(f"Xi{l}", [128, 8, 128], pg)
        Xt = sb(f"Xt{l}", [128, 8, 128], pg)
        Ci = sb(f"Ci{l}", [128, 8, 128], pg)
        Pi = DT
        t_X0, t_Xt, t_P = [None, None], [None, None], [None, None]
        free_C, free_P = [None, None], [None, None]
        for n in range(7):
            lm = K["levels"][:, n * 128:(n + 1) * 128]
            for c_ in range(2):
                s_ = slice(c_ * 4, c_ * 4 + 4)
                fl = lambda z_: z_[:, s_, :].rearrange("p a i -> p (a i)")
                t_c = tt(Ci[:, s_, :], AAb[:, s_, :], bc(lm, 1, 4), ALU.mult, [t_aa, t_lt, free_C[c_]], eng="gpsimd")
                b = banks.take()
                for a in range(4):
                    i = c_ * 4 + a
                    m = mm(b.t[:, a * 128:(a + 1) * 128], Ci[:, i, :], K["ident"][:, :] if n == 0 else Xi[:, i, :], w=[t_c, b.w, t_X0[c_]])
                free_C[c_] = [m]
                idb = bc(K["ident"][:, :], 1, 4)
                if n == 0:
                    c = tt(Xi[:, s_, :], idb, b.t[:, :].rearrange("p (a i) -> p a i", i=128), ALU.subtract, [m])
                    b.w = [c]
                    t_X0[c_] = c
                    t_Xt[c_] = tt(Xt[:, s_, :], idb, Ci[:, s_, :], ALU.subtract, [t_c])
                    free_C[c_] = [m, t_Xt[c_]]
                    continue
                t_P[c_] = cp(fl(Pi), b.t[:, :], [m, free_P[c_], t_aa, t_att], eng="scalar")
                b.w = [t_P[c_]]
                if n < 6:
                    b = banks.take()
                    for a in range(4):
                        i = c_ * 4 + a
                        m = mm(b.t[:, a * 128:(a + 1) * 128], Xt[:, i, :], Pi[:, i, :], w=[t_P[c_], t_Xt[c_], b.w])
                    t_X0[c_] = tt(fl(Xi), fl(Xi), b.t[:, :], ALU.subtract, [m])
                    b.w = [t_X0[c_]]
                b = banks.take()
                for a in range(4):
                    i = c_ * 4 + a
                    m = mm(b.t[:, a * 128:(a + 1) * 128], Pi[:, i, :], Xt[:, i, :], w=[t_P[c_], t_Xt[c_], b.w])
                t_Xt[c_] = tt(fl(Xt), fl(Xt), b.t[:, :], ALU.subtract, [m])
                b.w = [t_Xt[c_]]
                free_P[c_] = [m]
        U = sb(f"U{l}", [128, 2, 4, 128], pg)
        S1 = sb(f"S1{l}", [128, 4, 128], pg)
        Og = sb(f"Ogd{l}", [128, 2, 4, 128], pg)
        f4 = lambda z_: z_.rearrange("p a d -> p (a d)")

        def four(fl_, fr_, w):
            b = banks.take()
            for a in range(4):
                m = mm(b.t[:, a * 128:(a + 1) * 128], fl_(a), fr_(a), w=[w, b.w])
            return b, m

        b, m = four(lambda a: Xt[:, a, :], lambda a: vtm[:, 0, a, :], [t_Xt[0], t_v])
        tu = cp(f4(U[:, 0, :, :]), b.t[:, :], [m])
        b.w = [tu]
        b, m = four(lambda a: kd[:, a, :], lambda a: U[:, 0, a, :], [tu, t_kd])
        tS = cp(f4(S1[:, :, :]), b.t[:, :], [m])
        b.w = [tS]
        b, m = four(lambda a: ATb[:, a, :], lambda a: U[:, 0, a, :], [t_att])
        to0 = cp(f4(Og[:, 0, :, :]), b.t[:, :], [m], eng="scalar")
        b.w = [to0]
        b, m = four(lambda a: qk[:, 4 + a, 128:256], lambda a: S1[:, a, :], [tS])
        for a in range(4):
            tr_ = stt(vtm[:, 1, a, :], b.t[:, a * 128:(a + 1) * 128], nbe[:, a:a + 1], vtm[:, 1, a, :], ALU.mult, ALU.add, [m, t_nbe])
        b.w = [tr_]
        bq, mq = four(lambda a: qk[:, a, 128:256], lambda a: S1[:, a, :], [])
        b, m = four(lambda a: Xt[:, 4 + a, :], lambda a: vtm[:, 1, a, :], [tr_, t_Xt[1]])
        tu = cp(f4(U[:, 1, :, :]), b.t[:, :], [m])
        b.w = [tu]
        b, m = four(lambda a: ATb[:, 4 + a, :], lambda a: U[:, 1, a, :], [tu])
        tc1 = cp(f4(Og[:, 1, :, :]), b.t[:, :], [m])
        b.w = [tc1]
        for a in range(4):
            to1 = stt(Og[:, 1, a, :], bq.t[:, a * 128:(a + 1) * 128], eg[:, 4 + a:5 + a], Og[:, 1, a, :], ALU.mult, ALU.add, [mq, tc1])
        bq.w = [to1]
        og3 = Og[:, :, :, :].rearrange("p h a v -> p (h a) v")
        sq3 = U[:, :, :, :].rearrange("p h a v -> p (h a) v")
        vs = sb(f"gvs{l}", [128, 8], pg)
        t = tt(sq3, og3, og3, ALU.mult, [to0, to1, m])
        t = red(vs[:, :], sq3, ALU.add, [t])
        t = ts(vs[:, :], vs[:, :], 1.0 / 128, ALU.mult, EPS, ALU.add, w=[t])
        t = act(vs[:, :], vs[:, :], AF.Ln, [t])
        t = act(vs[:, :], vs[:, :], AF.Exp, [t], scale=-0.5)
        t = tt(og3, og3, bc(vs[:, :], 2, 128), ALU.mult, [t])
        t = tt(og3, og3, bc(gnr[:, :], 1, 8), ALU.mult, [t, t_l])
        t_gdn = tt(mix[:, :, 0:512], Og[:, :, :, :].rearrange("p h a v -> p h (a v)"), zsl[:, :, :], ALU.mult, [t, tz])
        prog.barrier()
        pg.close()
        pg = ExitStack()
        qr = sb(f"qr{l}", [128, 8, T], pg)
        rt = [[sb(f"rt{l}{i}", [128, T], pg), []] for i in range(3)]
        vbt = sb(f"vbt{l}", [128, 2, 512], pg)
        tq = []
        for r in range(8):
            if r % 4 == 0:
                pc = wcols(Wl, 2056 + r * 128, 512)
            b = banks.take()
            m = A(b.t[:, 0:256], pc, (r % 4) * 128, 128, [h, b.w])
            if r % 4 == 3:
                pc.done(m)
            t = act(qr[:, r, :], b.t[:, 0:256], AF.Copy, [m], scale=0.125 if r < 4 else 1.0)
            b.w = [t]
            b = banks.take()
            m = mm(b.t[:, 0:256], K["perm"][:, :], qr[:, r, :], w=[t, t_lt, b.w])
            r_ = rt[r % 3]
            t2 = tt(r_[0][:, :], b.t[:, 0:256], K["sin"][:, :], ALU.mult, [m, r_[1], t_lt])
            b.w = [t2]
            t = tt(qr[:, r, :], qr[:, r, :], K["cos"][:, :], ALU.mult, [t, m, t_lt], eng="gpsimd")
            t = tt(qr[:, r, :], qr[:, r, :], r_[0][:, :], ALU.add, [t, t2], eng="gpsimd")
            r_[1] = [t]
            tq.append(t)
        pc = wcols(Wl, 3080, 512)
        tvb = []
        for hf in range(2):
            b = banks.take()
            m = Bm(b.t[:, :], pc, 0, 512, hf, [h, b.w])
            b.w = [cp(vbt[:, hf, :], b.t[:, :], [m])]
            tvb += b.w
        pc.done(m)
        S = sb(f"Sm{l}", [128, 8, 256], pg)
        PT = sb(f"PTm{l}", [128, 8, 2, 128], pg)
        mx = sb(f"mxm{l}", [128, 8], pg)
        sm = sb(f"smm{l}", [128, 8], pg)
        free_S, free_PT, free_sm = [], [], []
        t_mb = []
        for hf in range(2):
            nk = (hf + 1) * 128
            per = 512 // nk
            t_p = [None] * 8
            for g in range(2):
                for j0 in range(0, 4, per):
                    b = banks.take()
                    for j in range(j0, j0 + per):
                        m = mm(b.t[:, (j - j0) * nk:(j - j0 + 1) * nk], qr[g * 64:g * 64 + 64, j, hf * 128:(hf + 1) * 128], qr[g * 64:g * 64 + 64, 4 + j, 0:nk], w=[tq, b.w])
                    sv = S[:, :, :].rearrange("p (j g) k -> p g j k", g=2)[:, g, j0:j0 + per, :]
                    bv = b.t[:, 0:per * nk].rearrange("p (j k) -> p j k", k=nk)
                    c = tt(sv[:, :, nk - 128:nk], bv[:, :, nk - 128:nk], bc(K["cmask"][:, :], 1, per), ALU.add, [m, free_S, t_lt])
                    if hf:
                        c = cp(sv[:, :, 0:128], bv[:, :, 0:128], [m, free_S])
                    b.w = [c]
            t = red(mx[:, :], S[:, :, 0:nk], ALU.max, [c, free_sm], negate=True)
            for hd in range(8):
                t_p[hd] = act(S[:, hd, 0:nk], S[:, hd, 0:nk], AF.Exp, [t, free_sm], bias=mx[:, hd:hd + 1], accum_out=sm[:, hd:hd + 1])
            t_s = recip(sm[:, :], sm[:, :], t_p)
            t_pt = []
            for hd in range(0, 8, 2):
                b = banks.take()
                for a in range(2):
                    for k in range(hf + 1):
                        m = tp(b.t[:, (a * (hf + 1) + k) * 128:(a * (hf + 1) + k + 1) * 128], S[:, hd + a, k * 128:(k + 1) * 128], [t_p, b.w])
                c = cp(PT[:, hd:hd + 2, 0:hf + 1, :], b.t[:, 0:2 * nk].rearrange("p (a k q) -> p a k q", a=2, q=128), [m, free_PT], eng="scalar" if hd % 4 else "vector")
                b.w = [c]
                t_pt.append(c)
            free_S = [m]
            b = banks.take()
            for hd in range(8):
                m = chain(b.t[:, hd * 64:(hd + 1) * 64], [(PT[:, hd, k, :], vbt[:, k, hd * 64:(hd + 1) * 64]) for k in range(hf + 1)], [t_pt, tvb, b.w])
            free_PT = [m]
            t = tt(mix[:, hf, 512:1024].rearrange("p (a d) -> p a d", d=64), b.t[:, :].rearrange("p (a d) -> p a d", d=64), bc(sm[:, :], 2, 64), ALU.mult, [m, t_s])
            b.w = [t]
            free_sm = [t]
            t_mb.append(t)
        mixT = qr
        tm = transposed(mix, 8, mixT, [[t_mb[0], t_gdn], [t_mb[1], t_gdn]], w=t_mb)
        bk, m = project(mixT, 8, io["w_out_2"][l], tm)

        def post_norm(bk, m, t_ln):
            tv_ = []
            for hf in range(2):
                for i in range(2):
                    s_ = slice(i * 512, (i + 1) * 512)
                    t = stt(xn[:, hf, s_], X[:, hf, s_], ALPHA, bk[hf][i].t[:, :], ALU.mult, ALU.add, [m[hf][i], t_X[hf], xn_free])
                    bk[hf][i].w = [t]
                    t = prog.add("vector", lambda e, o=st[:, hf, i, :], i_=xn[:, hf, s_]: e.bn_stats(o, i_), [t])
                t = prog.add("vector", lambda e, o=mv[:, hf, :], i_=st[:, hf, :, :].rearrange("p a b -> p (a b)"): e.bn_aggr(o, i_), [t])
                tv_.append(t)
            t = ts(rs_[:, :], mv[:, :, 1], LN_EPS, ALU.add, w=tv_)
            t = act(rs_[:, :], rs_[:, :], AF.Ln, [t])
            t = act(rs_[:, :], rs_[:, :], AF.Exp, [t], scale=-0.5)
            for hf in range(2):
                t2 = ts(xn[:, hf, :], xn[:, hf, :], mv[:, hf, 0:1], ALU.subtract, rs_[:, hf:hf + 1], ALU.mult, w=[t])
                t2 = tt(xn[:, hf, :], xn[:, hf, :], lnr[:, 0, :], ALU.mult, [t2, t_ln])
                t_X[hf] = tt(X[:, hf, :], xn[:, hf, :], lnr[:, 1, :], ALU.add, [t2])

        post_norm(bk, m, t_l)
        xn_free = list(t_X)
        s_l2 = dsem(f"s_l2{l}")
        for i, n in enumerate(("ln2_g_2", "ln2_b_2")):
            t_l2 = dma(lnr[:, i, :], io[n][l].partition_broadcast(128), s_l2, t_X, eng="gpsimd")
        prog.barrier()
        pg.close()
        pm.close()
        pf = ExitStack()
        hTh, hTl = sb(f"fhTh{l}", [128, 22, T], pf, R32), sb(f"fhTl{l}", [128, 22, T], pf, R32)
        cg = [[sb(f"cg{l}{i}", [128, T], pf), []] for i in range(3)]
        cu = [[sb(f"cu{l}{i}", [128, T], pf), []] for i in range(3)]
        new_HT(pf, f"f{l}", True)
        new_units(pf, f"f{l}")
        h, m = to_HT(X, t_X)
        prog.hold["tensor"] += h
        w01, w2_, wb = vec[f"fconv{l}"], vec[f"fconv2{l}"], vec[f"fconvb{l}"]
        vt = [vec_tok[f"fconv{l}"], vec_tok[f"fconv2{l}"]]

        def conv3(dst, b, m, r):
            t = act(dst[0][:, :], b.t[:, 0:256], AF.Identity, [m, dst[1], vt], scale=w2_[:, r:r + 1], bias=wb[:, r:r + 1])
            t = stt(dst[0][:, 1:T], b.t[:, 0:T - 1], w01[:, 44 + r:45 + r], dst[0][:, 1:T], ALU.mult, ALU.add, [t])
            t = stt(dst[0][:, 2:T], b.t[:, 0:T - 2], w01[:, r:r + 1], dst[0][:, 2:T], ALU.mult, ALU.add, [t])
            b.w = [t]
            return t

        th = []

        def gated_conv(i, b1, b2, m1, m2):
            c1, c2 = cg[i % 3], cu[i % 3]
            t1 = conv3(c1, b1, m1, i)
            t2 = conv3(c2, b2, m2, 22 + i)
            t = silu_of(c1[0][:, :], c1[0][:, :], [t1])
            t = tt(c1[0][:, :], c1[0][:, :], c2[0][:, :], ALU.mult, [t, t2], eng="gpsimd")
            c2[1] = [t]
            c1[1] = [hi_lo(hTh[:, i, :], hTl[:, i, :], c1[0][:, :], [t])]
            th.append(c1[1][0])

        up3(io["w_up_2"][l], 22, gated_conv)
        lnexp()
        project3(hTh, hTl, 22, io["w_down_2"][l], th, 2, lambda bk, m: post_norm(bk, m, t_l2))
        drain()
        xn_free = list(t_X)
        prog.barrier()
        pf.close()
        ph.close()

    s_out = dsem("s_out")
    t_out = dma(out[0].rearrange("(h p) d -> p h d", p=128), X[:, :, :], s_out, t_X)
    sems_end = [t_out]
    prog.number(sems)
    with ctx, nc.Block() as block:
        @block.sync
        def _(e):
            prog.write("sync", e)
            for t in sems_end:
                e.wait_ge(t.sem, t.val)

        @block.tensor
        def _(e):
            prog.write("tensor", e)

        @block.vector
        def _(e):
            prog.write("vector", e)

        @block.scalar
        def _(e):
            prog.write("scalar", e)

        @block.gpsimd
        def _(e):
            prog.write("gpsimd", e)


NAMES = ['x', 'c', 'hyb_norm', 'hyb_mod_w', 'hyb_mod_b', 'hyb_w_in', 'gla_gk_up', 'gla_gk_bias', 'gla_out_norm', 'nsa_cmp_pe',
         'nsa_cmp_w1', 'nsa_cmp_w2', 'hyb_w_out', 'dense_norm', 'dense_mod_w', 'dense_mod_b', 'dense_w_gu', 'dense_w_down',
         'ssm_norm', 'ssm_mod_w', 'ssm_mod_b', 'ssm_w_in', 'ssm_conv_w', 'ssm_conv_b', 'ssm_dt_bias', 'ssm_a_log', 'ssm_d',
         'ssm_gate_norm', 'ssm_w_out', 'moe_norm', 'moe_mod_w', 'moe_mod_b', 'moe_router', 'moe_w_gu', 'moe_w_down', 'final_norm',
         'w_in_2', 'gdn_conv_w_2', 'gdn_a_log_2', 'gdn_dt_bias_2', 'gdn_norm_g_2', 'w_out_2', 'ln1_g_2', 'ln1_b_2', 'w_up_2',
         'ffn_conv_w_2', 'ffn_conv_b_2', 'w_down_2', 'ln2_g_2', 'ln2_b_2']


def kernel(**inputs):
    import concourse.bacc as bacc
    from concourse.bass_utils import run_bass_kernel_spmd

    nc = bacc.Bacc("TRN2", target_bir_lowering=False, num_devices=1)
    arrays, io, cn = {}, {}, {}
    for n in NAMES:
        a = np.ascontiguousarray(inputs[n])
        arrays["in_" + n] = a
        io[n] = nc.dram_tensor("in_" + n, a.shape, mybir.dt.float32, kind="ExternalInput").ap()
    for n, a in constants().items():
        arrays["const_" + n] = a
        cn[n] = nc.dram_tensor("const_" + n, a.shape, mybir.dt.float32, kind="ExternalInput").ap()
    out = nc.dram_tensor("out", (1, T, D), mybir.dt.float32, kind="ExternalOutput").ap()
    program(nc, io, cn, out)
    r = run_bass_kernel_spmd(nc, [arrays], core_ids=[0])
    return np.asarray(r.results[0]["out"])
```

```python
import numpy as np
import concourse.bass as bass
from concourse import mybir
from concourse.alu_op_type import AluOpType as ALU
from contextlib import ExitStack

F32 = mybir.dt.float32
AF = mybir.ActivationFunctionType
AX = mybir.AxisListType

ENGINES = ("sync", "tensor", "vector", "scalar", "gpsimd")


class Op:

    def __init__(self, eng, fn, waits, dma):
        self.eng, self.fn, self.waits, self.dma = eng, fn, waits, dma
        self.needed, self.sem, self.val = False, None, 0


class Program:

    def __init__(self):
        self.q = {e: [] for e in ENGINES}
        self.hold = {e: [] for e in ENGINES}
        self.dma_count = {}

    def add(self, eng, fn, waits=(), dma=None):
        flat = []

        def walk(w):
            if w is None:
                return
            if isinstance(w, (list, tuple)):
                for x in w:
                    walk(x)
            else:
                flat.append(w)

        walk(list(waits) if isinstance(waits, (list, tuple)) else [waits])
        flat += self.hold[eng]
        self.hold[eng] = []
        for w in flat:
            w.needed = True
        op = Op(eng, fn, flat, dma)
        if dma is not None:
            self.dma_count[dma] = self.dma_count.get(dma, 0) + 16
            op.sem, op.val = dma, self.dma_count[dma]
        self.q[eng].append(op)
        return op

    def last(self):
        own = {e: [o for o in self.q[e] if isinstance(o, Op) and o.dma is None] for e in ("tensor", "vector", "scalar", "gpsimd")}
        return [o[-1] for o in own.values() if o]

    def ends(self):
        res = self.last()
        return res

    def barrier(self, ends=None):
        ends = self.ends() if ends is None else ends
        for e in ("tensor", "vector", "scalar", "gpsimd"):
            self.hold[e] = self.hold[e] + ends
        return ends

    def begin_if(self, flag, tok):
        tok.needed = True
        for e in ENGINES:
            self.q[e].append(("if", flag, tok))

    def end_if(self):
        for e in ENGINES:
            self.q[e].append(("end",))

    def number(self, sems):
        self.sems = sems
        for e in ENGINES:
            n = 0
            for op in self.q[e]:
                if isinstance(op, Op) and op.dma is None and op.needed:
                    n += 1
                    op.sem, op.val = sems[e], n

    def write(self, name, eng):
        seen = {}
        ops, i = self.q[name], 0
        made = {}
        while i < len(ops):
            if isinstance(ops[i], Op):
                self.one(eng, ops[i], seen, made)
                i += 1
                continue
            _, flag, tok = ops[i]
            end = next(j for j in range(i, len(ops)) if not isinstance(ops[j], Op) and ops[j][0] == "end")
            eng.wait_ge(tok.sem, tok.val)
            go = eng.value_load(flag, min_val=0, max_val=1)
            before = dict(made)
            with eng.If(go):
                inside = dict(seen)
                for op in ops[i + 1:end]:
                    self.one(eng, op, inside, made)
            with eng.Else():
                for s, v in made.items():
                    if v > before.get(s, 0):
                        if before.get(s, 0):
                            eng.wait_ge(s, before[s])
                        eng.sem_inc(s, v - before.get(s, 0))
            i = end + 1

    def one(self, eng, op, seen, made):
        need = {}
        for w in op.waits:
            need[w.sem] = max(need.get(w.sem, 0), w.val)
        for s, v in need.items():
            if seen.get(s, 0) < v:
                eng.wait_ge(s, v)
                seen[s] = v
        ins = op.fn(eng)
        if op.dma is not None:
            ins.then_inc(op.dma, 16)
            made[op.dma] = op.val
        elif op.needed:
            ins.then_inc(op.sem, 1)
            made[op.sem] = op.val

D = 1024
T = 256
KC = 8
SLOT = 528 * 8
NSLOT = 3
NUNIT = 3
R32 = mybir.dt.float32r
EPS = 1e-6
LN_EPS = 1e-5
ALPHA = 4.0 ** 0.25
FF = 2816
FE = 3584
NE = 8
BIG = 1e30
CAP = 128


def constants():
    p = np.arange(128)
    c = {}
    c["ident"] = np.eye(128)
    c["causal"] = p[:, None] <= p[None, :]
    c["glamask"] = (p[:, None] <= p[None, :]) & (p[:, None] // 64 == p[None, :] // 64)
    lev = np.zeros((128, 7, 128))
    for n in range(7):
        b = p >> n
        lev[:, n, :] = (b[None, :] % 2 == 1) & (b[:, None] == b[None, :] - 1)
    c["levels"] = lev.reshape(128, -1)
    dist = np.zeros((128, 256))
    dist[:, :128] = 128 + p[:, None] - p[None, :]
    dist[:, 128:] = np.where(p[:, None] >= p[None, :], p[:, None] - p[None, :], BIG)
    c["dist"] = dist
    dc = np.full((128, 2, 16), BIG)
    for h in range(2):
        t = h * 128 + p
        for n in range(15):
            dc[:, h, n] = np.where(n * 16 + 31 <= t, t - (n * 16 + 15.5), BIG)
    c["distc"] = dc.reshape(128, -1)
    c["blockdiag"] = (p[:, None] // 16 == np.arange(8)[None, :])
    c["cmask"] = np.where(p[:, None] >= p[None, :], 0.0, -BIG)
    half = 8
    inv = np.float32(500000.0) ** (-np.arange(half, dtype=np.float32) / np.float32(half))
    ang = np.arange(T, dtype=np.float32)[None, :] * inv.astype(np.float32)[:, None]
    cos, sin = np.ones((128, T)), np.zeros((128, T))
    perm = np.zeros((128, 128))
    for b in (0, 64):
        cos[b:b + 8] = cos[b + 8:b + 16] = np.cos(ang.astype(np.float32))
        sin[b:b + 8] = -np.sin(ang.astype(np.float32))
        sin[b + 8:b + 16] = np.sin(ang.astype(np.float32))
        for i in range(8):
            perm[b + 8 + i, b + i] = 1
            perm[b + i, b + 8 + i] = 1
    c["cos"], c["sin"], c["perm"] = cos, sin, perm
    e = np.arange(8)
    c["tie"] = np.broadcast_to((e[None, :] < e[:, None]).reshape(1, 64), (128, 64))
    c["iota"] = np.broadcast_to(np.arange(256)[None], (128, 256))
    c["before"] = p[:, None] < p[None, :]
    c["reset64"] = np.broadcast_to((np.arange(T) % 64 != 0)[None], (128, T))
    c["reset128"] = np.broadcast_to((np.arange(T) % 128 != 0)[None], (128, T))
    return {k: np.ascontiguousarray(v, dtype=np.float32) for k, v in c.items()}



def program(nc, io, cn, out):
    prog = Program()
    ctx = ExitStack()

    def sb(name, shape, stack=ctx, dt=F32):
        return stack.enter_context(nc.sbuf_tensor(name, list(shape), dt))

    psum = [ctx.enter_context(nc.psum_tensor(f"ps{i}", [128, 512], F32)) for i in range(8)]
    sems = {e: ctx.enter_context(nc.semaphore(f"s_{e}")) for e in ENGINES}

    def dsem(name):
        return ctx.enter_context(nc.semaphore(name))

    def mm(o, lhsT, rhs, start=True, stop=True, w=(), skip=False):
        return prog.add("tensor", lambda e: e.matmul(o, lhsT, rhs, start=start, stop=stop, skip_group_check=skip), w)

    def chain(o, pairs, w=()):
        for i, (a, b) in enumerate(pairs):
            t = mm(o, a, b, i == 0, i == len(pairs) - 1, w if i == 0 else ())
        return t

    def tp(o, i, w=()):
        n = i.shape[0]
        return prog.add("tensor", lambda e: e.transpose(o, i, K["ident"][0:n, 0:n]), w)

    def act(o, i, f, w=(), **kw):
        return prog.add("scalar", lambda e: e.activation(o, i, f, **kw), w)

    def tt(o, a, b, op, w=(), eng="vector"):
        return prog.add(eng, lambda e: e.tensor_tensor(o, a, b, op), w)

    def ts(o, a, s1, op0, s2=None, op1=None, w=(), eng="vector"):
        if op1 is None:
            return prog.add(eng, lambda e: e.tensor_scalar(o, a, s1, None, op0), w)
        return prog.add(eng, lambda e: e.tensor_scalar(o, a, s1, s2, op0, op1), w)

    def stt(o, a, s, b, op0, op1, w=()):
        return prog.add("vector", lambda e: e.scalar_tensor_tensor(o, a, s, b, op0, op1), w)

    def cp(o, i, w=(), eng="vector"):
        if eng == "scalar":
            return act(o, i, AF.Copy, w)
        return prog.add(eng, lambda e: e.tensor_copy(o, i), w)

    def red(o, i, op, w=(), negate=False):
        return prog.add("vector", lambda e: e.tensor_reduce(o, i, AX.X, op, negate=negate), w)

    def recip(o, i, w=()):
        return prog.add("vector", lambda e: e.reciprocal(o, i), w)

    def scan(o, a, b, w=()):
        return prog.add("vector", lambda e: e.tensor_tensor_scan(o, a, b, 0.0, ALU.mult, ALU.add), w)

    def fill(o, v, w=(), eng="gpsimd"):
        return prog.add(eng, lambda e: e.memset(o, v), w)

    def dma(o, i, sem, w=(), eng="sync"):
        return prog.add(eng, lambda e: e.dma_start(o, i), w, dma=sem)

    def lnexp(w=()):
        return prog.add("scalar", lambda e: e.preload_act_table_set("natural_log_exp_and_others"), w)

    def bc(ap, axis, n):
        a = ap.unsqueeze(axis)
        s = list(a.shape)
        s[axis] = n
        return a.to_broadcast(s)

    class Bank:
        def __init__(self, t):
            self.t, self.w = t, []

    class Banks:
        def __init__(self, ts_):
            self.b, self.i = ts_, 0

        def take(self):
            b = self.b[self.i]
            self.i = (self.i + 1) % len(self.b)
            return b

    allbanks = [Bank(t) for t in psum]
    banks = Banks(allbanks)

    slots = sb("slots", [128, NSLOT, SLOT])
    slot_sem = [dsem(f"s_w{i}") for i in range(NSLOT)]
    slot_free = [[] for _ in range(NSLOT)]
    nload = [0]

    class Piece:
        def __init__(self, i, ap, tok):
            self.i, self.ap, self.tok = i, ap, tok

        def done(self, *toks):
            slot_free[self.i] = list(toks)

    def load(src, shape):
        i = nload[0] % NSLOT
        nload[0] += 1
        a, b = shape
        assert slot_free[i] is not None
        v = slots[:, i, 0:a * b].rearrange("p (a b) -> p a b", b=b)
        t = dma(v, src, slot_sem[i], slot_free[i])
        slot_free[i] = None
        return Piece(i, v, t)

    def wcols(w, c0, n):
        return load(w[:, c0:c0 + n].rearrange("(k p) n -> p k n", p=128), (KC, n))

    def wheads(w, c0):
        i = nload[0] % NSLOT
        nload[0] += 1
        v = slots[:, i, 0:KC * 512].rearrange("p (a b) -> p a b", b=512)
        for g in range(2):
            for k in range(KC):
                t = dma(v[:, k, :].rearrange("p (r g d) -> p g r d", g=2, d=64)[:, g, :, :],
                        w[k * 128:(k + 1) * 128, c0 + g * 256:c0 + (g + 1) * 256].rearrange("p (r d) -> p r d", d=64), slot_sem[i], slot_free[i])
        slot_free[i] = None
        return Piece(i, v, t)

    def wrows(w, r0, n):
        return load(w[r0:r0 + n * 128, :].rearrange("(f p) n -> p f n", p=128), (n, D))

    K, Ksh = {}, {}
    s_const = dsem("s_const")
    X = sb("X", [128, 2, D])
    xn = sb("xn", [128, 2, D])
    s_x = dsem("s_x")

    def const(n, sem):
        K[n] = sb("k_" + n, [128, cn[n].shape[1]])
        return dma(K[n][:, :], cn[n], sem)

    for n in ("causal", "tie", "iota", "before"):
        K[n] = sb("k_" + n, [128, cn[n].shape[1]])
    t_id = const("ident", dsem("s_ident"))
    ones = sb("ones", [128, 128])
    t_ones = fill(ones[:, :], 1.0)

    vec = {}
    vec_tok = {}
    vec_read = []
    nvec = [0]
    vec_later, first_later = [], []

    def later(where, gen):
        next(gen)
        where.append(gen)


    def vectors(block, parts):
        n = sum(s.shape[0] for _, s in parts)
        v = sb("v_" + block, [128, n])
        yield
        c0 = nvec[0] * 128
        nvec[0] += 1
        rows = (gates[0] if nvec[0] > 3 else xn[:, 0, :])[:, c0 % D:c0 % D + 128]
        sem = dsem("s_rows" + block)
        at = 0
        for _, s in parts:
            t = dma(rows[at:at + s.shape[0], :], s, sem, eng="scalar")
            at += s.shape[0]
        yield
        b = banks.take()
        m = tp(b.t[:, 0:n], rows[0:n, :], [t, t_id, b.w])
        c = cp(v[:, :], b.t[:, 0:n], [m])
        b.w = [c]
        vec_read.append(m)
        at = 0
        for name, s in parts:
            vec[name] = v[:, at:at + s.shape[0]]
            vec_tok[name] = c
            at += s.shape[0]

    def r128(v):
        return v.rearrange("(r p) -> r p", p=128)

    for _ in vectors("c", [("c", r128(io["c"][0]))]):
        pass

    sc = sb("sc", [128, KC])
    with_e = sb("sc_e", [128, KC])
    e0 = lnexp()
    e1 = act(with_e[:, :], vec["c"], AF.Exp, [vec_tok["c"], e0], scale=-1.0)
    a1 = ts(with_e[:, :], with_e[:, :], 1.0, ALU.add, w=[e1])
    a2 = recip(with_e[:, :], with_e[:, :], [a1])
    t_sc = tt(sc[:, :], with_e[:, :], vec["c"], ALU.mult, [a2])

    ssq = sb("ssq", [128, 2])
    rst = sb("rst", [128, 2])
    eps = sb("eps", [128, 1])
    t_eps = fill(eps[:, :], EPS)
    later(first_later, vectors("a", [("hyb_norm", r128(io["hyb_norm"][0])), ("dense_norm", r128(io["dense_norm"][0])),
                  ("ssm_norm", r128(io["ssm_norm"][0])), ("moe_norm", r128(io["moe_norm"][0])),
                  ("gate_norm", r128(io["ssm_gate_norm"][0])), ("conv_b", r128(io["ssm_conv_b"][0])),
                  ("gk_bias", r128(io["gla_gk_bias"][0]))]))
    later(first_later, vectors("m", [(n + "_mod_b", r128(io[n + "_mod_b"][0])) for n in ("hyb", "dense", "ssm", "moe")]))
    later(vec_later, vectors("b", [("conv_w", io["ssm_conv_w"][0].rearrange("j (r p) -> (j r) p", p=128))]))
    for l in range(2):
        later(vec_later, vectors(f"g{l}", [(f"gconv{l}", io["gdn_conv_w_2"][l].rearrange("j (r p) -> (j r) p", p=128))]))
        later(vec_later, vectors(f"f{l}", [(f"fconv{l}", io["ffn_conv_w_2"][l][0:2].rearrange("j (r p) -> (j r) p", p=128))]))
        later(vec_later, vectors(f"h{l}", [(f"fconv2{l}", io["ffn_conv_w_2"][l][2:3].rearrange("j (r p) -> (j r) p", p=128)),
                          (f"fconvb{l}", r128(io["ffn_conv_b_2"][l]))]))
    for gen in first_later:
        next(gen)
    pfirst = ExitStack()
    mod = {}
    gates = [sb(f"gate{i}", [128, D], pfirst) for i in range(3)]
    gate_free = [[], [], []]
    nvec[0] = 8
    for gen in vec_later:
        next(gen)
    side = []
    pace, calls = [(1, 1)], [0]

    def step():
        calls[0] += 1
        if calls[0] % pace[0][1] >= pace[0][0]:
            return
        while side:
            try:
                next(side[0])
                break
            except StopIteration:
                side.pop(0)

    def ready(name, what):
        while len(mod.get(name, {}).get(what, ())) < 2:
            step()

    pmacc = ExitStack()
    s12 = {n: (sb(f"s1_{n}", [128, KC], pfirst), sb(f"s2_{n}", [128, KC], pfirst)) for n in ("hyb", "dense", "ssm", "moe")}
    macc = sb("macc", [128, D], pmacc)
    macc_free = []
    beside = sb("beside", [128, 2, D], pmacc)
    beside_sem = [dsem(f"s_beside{i}") for i in range(3)]
    beside_free = [[], [], []]

    side_banks = banks

    def mod_part(name, part, acc, t, t_b=None):
        s1, s2 = s12[name]
        if part < 2:
            b = side_banks.take()
            for i in range(8):
                m = mm(b.t[:, i:i + 1], acc[:, i * 128:(i + 1) * 128], ones[:, 0:1], w=[t, t_ones, b.w])
            bias = vec[name + "_mod_b"][:, part * 8:part * 8 + 8]
            s_ = s1 if part else s2
            c = tt(s_[:, :], b.t[:, 0:8], bias, ALU.add, [m, vec_tok[name + "_mod_b"]])
            b.w = [c]
            if part:
                c = stt(s1[:, :], s1[:, :], 1.0, vec[name + "_norm"], ALU.add, ALU.mult, [c, vec_tok[name + "_norm"]])
            mod[name]["cols"].append(c)
            return m
        slot = mod[name]["slot"]
        for i in range(2):
            b = side_banks.take()
            m = mm(b.t[:, :], ones[:, :], acc[:, i * 512:(i + 1) * 512], w=[t, t_ones, b.w])
            g = gates[slot][:, i * 512:(i + 1) * 512]
            c = tt(g, g, b.t[:, :], ALU.add, [m, t_b])
            b.w = [c]
            mod[name]["rows"].append(c)
        return m

    def adaln(name, slot, third, parts=(0, 1, 2)):
        nonlocal macc_free
        w_ = io[name + "_mod_w"][0]
        if name not in mod:
            mod[name] = {"slot": slot, "cols": [], "rows": []}
        todo = [(p_, k) for p_ in parts for k in range(KC)]
        bufs = [beside[:, 0, :], beside[:, 1, :], gates[third][:, :]]
        beside_free[2] = gate_free[third]
        got = []

        def get():
            i = len(got) % 3
            part, k = todo[len(got)]
            got.append(dma(bufs[i], w_[k * 128:(k + 1) * 128, part * D:(part + 1) * D], beside_sem[i], beside_free[i], eng="gpsimd"))

        get()
        yield
        get()
        yield
        for n, (part, k) in enumerate(todo):
            if n + 2 < len(todo):
                get()
            yield
            i = n % 3
            if k == 0:
                t = ts(macc[:, :], bufs[i], sc[:, 0:1], ALU.mult, w=[got[n], t_sc, macc_free])
            else:
                t = stt(macc[:, :], bufs[i], sc[:, k:k + 1], macc[:, :], ALU.mult, ALU.add, [t, got[n]])
            beside_free[i] = [t]
            if k == KC - 1:
                t_b = None
                if part == 2:
                    t_b = dma(gates[slot][:, :], io[name + "_mod_b"][0, 2 * D:3 * D].partition_broadcast(128), dsem("s_b_" + name), [beside_free[2], gate_free[slot]], eng="gpsimd")
                    yield
                yield
                yield
                macc_free = [mod_part(name, part, macc, t, t_b)]
        gate_free[third] = beside_free[2]

    def adaln_first(name, slot):
        w_ = io[name + "_mod_w"][0]
        mod[name] = {"slot": slot, "cols": [], "rows": []}
        accs = [gates[1], gates[2]]
        t = [None] * 2
        src = lambda k: w_[k * 256:(k + 1) * 256, 0:2 * D].rearrange("(a p) n -> p a n", p=128)
        pcs = [load(src(k), (2, 2 * D)) for k in range(2)]
        t_x = dma(X[:, :, :], io["x"][0].rearrange("(h p) d -> p h d", p=128), s_x)
        pcs.append(load(src(2), (2, 2 * D)))
        pcs.append(Piece(None, p3[:, :, :], dma(p3[:, :, :], src(3), dsem("s_p3"))))
        for n in ("causal", "tie", "iota", "before"):
            t_c = dma(K[n][:, :], cn[n], s_const)
        for k in range(4):
            pc = pcs[k]
            for a in range(2):
                for i in range(2):
                    if k + a == 0:
                        t[i] = ts(accs[i][:, :], pc.ap[:, a, i * D:(i + 1) * D], sc[:, 0:1], ALU.mult, w=[pc.tok, t_sc])
                        continue
                    t[i] = stt(accs[i][:, :], pc.ap[:, a, i * D:(i + 1) * D], sc[:, 2 * k + a:2 * k + a + 1], accs[i][:, :], ALU.mult, ALU.add, [t[i], pc.tok, t_sc])
            if k < 3:
                pc.done(t[1])
        while first_later:
            for _ in first_later.pop(0):
                pass
        for i in range(2):
            gate_free[i + 1] = [mod_part(name, i, accs[i], t[i])]
        return t_x, t_c, t[1]

    HT_free = []
    early = ExitStack()
    p3 = sb("p3", [128, 2, 2 * D], early)
    t_x, t_const, t_early = adaln_first("hyb", 0)
    early.close()
    xn_free = list(vec_read)
    t_const = [t_const, t_id]
    t_X = [t_x, t_x]

    def rms(dst):
        out_ = []
        for h in range(2):
            t = act(dst[:, h, :], X[:, h, :], AF.Square, [t_X[h], xn_free], accum_out=ssq[:, h:h + 1])
            t = act(rst[:, h:h + 1], ssq[:, h:h + 1], AF.Ln, [t, t_eps], scale=1.0 / D, bias=eps[:, :])
            t = act(rst[:, h:h + 1], rst[:, h:h + 1], AF.Exp, [t], scale=-0.5)
            out_.append(ts(dst[:, h, :], X[:, h, :], rst[:, h:h + 1], ALU.mult, w=[t]))
        return out_

    HT = None
    HTl = None

    def new_HT(stack, name, parts=False):
        nonlocal HT, HTl
        HT = sb("HT" + name, [128, KC, T], stack, R32 if parts else F32)
        HTl = sb("HTl" + name, [128, KC, T], stack, R32) if parts else None

    def hi_lo(hi, lo, x, w, wh=()):
        t = act(hi, x, AF.Copy, [w, wh])
        return tt(lo, x, hi.bitcast(F32), ALU.subtract, [t, wh])

    def to_HT(src, toks, s1=None, s2=None, w=()):
        res, lows = [], []
        for n in range(4):
            h, k0 = n // 2, n % 2 * 4
            hs = slice(h * 128, (h + 1) * 128)
            b = banks.take()
            for k in range(4):
                m = tp(b.t[:, k * 128:(k + 1) * 128], src[:, h, (k0 + k) * 128:(k0 + k + 1) * 128], [toks[h], b.w, t_const])
            v = b.t[:, :].rearrange("p (a t) -> p a t", t=128)
            if HTl is not None and s1 is None:
                c = hi_lo(HT[:, k0:k0 + 4, hs], HTl[:, k0:k0 + 4, hs], v, [m])
                b.w = [c]
                res.append(c)
            elif HTl is not None:
                for k in (k0, k0 + 2):
                    x_ = HTf[k // 2 % 2]
                    xv = x_[0][:, :].rearrange("p (a t) -> p a t", t=128)
                    for a in range(2):
                        c = ts(xv[:, a, :], v[:, k - k0 + a, :], s1[:, k + a:k + a + 1], ALU.mult, s2[:, k + a:k + a + 1], ALU.add, w=[m, w, x_[1]])
                    b.w = [c]
                    c = act(HT[:, k:k + 2, hs], xv, AF.Copy, [c])
                    x_[1] = [c]
                    lows.append((k, xv, x_, hs, c))
                    while lows and (len(lows) > 1 or (n % 2 and k == KC - 2)):
                        k_, xv, x_, hs_, c = lows.pop(0)
                        c = tt(HTl[:, k_:k_ + 2, hs_], xv, HT[:, k_:k_ + 2, hs_].bitcast(F32), ALU.subtract, [c])
                        x_[1] = [c]
                        res.append(c)
            else:
                for k in range(4):
                    if n % 2:
                        c = act(HT[:, k0 + k, hs], v[:, k, :], AF.Identity, [m, w], scale=s1[:, k0 + k:k0 + k + 1], bias=s2[:, k0 + k:k0 + k + 1])
                    else:
                        c = ts(HT[:, k0 + k, hs], v[:, k, :], s1[:, k0 + k:k0 + k + 1], ALU.mult, s2[:, k0 + k:k0 + k + 1], ALU.add, w=[m, w])
                    res.append(c)
                b.w = res[-2:]
        return res, m

    def modulated(name, early=iter(())):
        nonlocal xn_free
        ready(name, "cols")
        x2 = normed_x.pop() if normed_x else rms(xn)
        next(early, None)
        res, m = to_HT(xn, x2, *s12[name], mod[name]["cols"])
        xn_free = [m]
        return res

    normed_x, ends_x = [], []

    def gated_add(bk, name, m):
        ready(name, "rows")
        ends_x[:] = prog.ends()
        slot, toks = mod[name]["slot"], mod[name]["rows"]
        g = gates[slot]
        last = None
        for h in range(2):
            for i in range(2):
                o = xn[:, h, i * 512:(i + 1) * 512]
                c = tt(o, bk[h][i].t[:, :], g[:, i * 512:(i + 1) * 512], ALU.mult, [m[h][i], toks, xn_free])
                bk[h][i].w = [c]
                last = tt(X[:, h, i * 512:(i + 1) * 512], X[:, h, i * 512:(i + 1) * 512], o, ALU.add, [c])
            t_X[h] = last
        gate_free[slot] = [last]
        normed_x.append(rms(xn))

    UN = {}

    def new_units(stack, name, size=2048):
        UN["hi"] = sb("uh" + name, [128, NUNIT, size], stack, R32)
        UN["lo"] = sb("ul" + name, [128, NUNIT, size], stack, R32)
        UN["size"] = size
        UN["free"] = [[] for _ in range(NUNIT)]
        UN["n"] = 0

    class Unit:

        def __init__(self, x, tok):
            self.i = UN["n"] % NUNIT
            UN["n"] += 1
            sh = list(x.shape)
            view = lambda a: a[:, self.i, 0:sh[1] * sh[2]].rearrange("p (a b) -> p a b", b=sh[2])
            self.hi, self.lo = view(UN["hi"]), view(UN["lo"])
            assert UN["free"][self.i] is not None
            self.tok = hi_lo(self.hi, self.lo, x, [tok], UN["free"][self.i])
            UN["free"][self.i] = None

        def done(self, *toks):
            UN["free"][self.i] = list(toks)

    def A3(o, u, c0, w, n=128):
        step()
        ps = []
        for k in range(KC):
            a, l = u.hi[:, k, c0:c0 + n], u.lo[:, k, c0:c0 + n]
            ps += [(a, HT[:, k, :]), (a, HTl[:, k, :]), (l, HT[:, k, :])]
        return chain(o, ps, [w, u.tok])

    AHEAD = NUNIT - 1
    queue = []

    def put(x, pc, last, use):
        u = Unit(x, pc.tok)
        if last:
            pc.done(u.tok)
        queue.append((u, use))
        if len(queue) > AHEAD:
            u, use = queue.pop(0)
            use(u)

    def drain():
        while queue:
            u, use = queue.pop(0)
            use(u)

    def columns3(wmat, c0, n, tile, bks=None):
        step_ = UN["size"] // KC
        for c in range(0, n, 512):
            end = min(512, n - c)
            pc = wcols(wmat, c0 + c, end)
            for f0 in range(0, end, step_):
                def use(u, i=(c + f0) // 128, w_=min(step_, end - f0)):
                    for f in range(0, w_, 128):
                        b = (bks or banks).take()
                        m = A3(b.t[0:min(128, w_ - f), 0:256], u, f, [b.w], min(128, w_ - f))
                        tile(i + f // 128, b, m)
                    u.done(m)

                put(pc.ap[:, :, f0:min(f0 + step_, end)], pc, f0 + step_ >= end, use)
                yield

    def rows3(pc, c0, tile, bks, end=True):
        n = UN["size"] // 512
        bk = []

        def use(u, k0):
            step()
            if k0 == 0:
                bk.extend(bks.take() for _ in range(2))
            for h in range(2):
                sl = slice(h * 128, (h + 1) * 128)
                o = bk[h].t[:, :]
                for k in range(n):
                    mm(o, HT[:, k0 + k, sl], u.hi[:, k, :], k0 + k == 0, False, [u.tok] + (bk[h].w if k0 + k == 0 else []))
                    mm(o, HTl[:, k0 + k, sl], u.hi[:, k, :], False, False)
                    m = mm(o, HT[:, k0 + k, sl], u.lo[:, k, :], False, k0 + k == KC - 1)
                if k0 + n == KC:
                    tile(h, bk[h], m)
            u.done(m)

        for k0 in range(0, KC, n):
            put(pc.ap[:, k0:k0 + n, c0:c0 + 512], pc, end and k0 + n == KC, lambda u, k0=k0: use(u, k0))
            yield

    def run(gen):
        for _ in gen:
            pass

    def weave(*gens):
        gens = list(gens)
        while gens:
            for g_ in list(gens):
                try:
                    next(g_)
                except StopIteration:
                    gens.remove(g_)

    def settle(*ends):
        ends = list(ends) or prog.last()
        flat = [x for y in ends for x in (y if isinstance(y, list) else [y])]
        for e in ("vector", "scalar", "gpsimd"):
            prog.hold[e] = prog.hold[e] + flat

    def project3(hi, lo, ntile, wmat, toks, halves, end, bk=None, begin=None, after=None, order=None):
        m = [[None] * 2 for _ in range(halves)]
        st_ = {"bk": bk}
        per = UN["size"] // D
        order = order or range(0, ntile, 4)
        count, kept = ntile // per, []

        def use(u, n, tiles, last):
            if n == 0 and begin:
                begin()
            if st_["bk"] is None:
                st_["bk"] = [[banks.take() for _ in range(2)] for _ in range(halves)]
            bk = st_["bk"]
            before_last = halves == 2 and not last and n == count - 2
            todo = [(u, n, tiles, h) for h in range(1 if before_last else halves)]
            if last and halves == 2:
                todo.insert(1, kept.pop())
            if before_last:
                kept.append((u, n, tiles, 1))
            for u_, n_, tiles_, h in todo:
                for f, g in enumerate(tiles_):
                    first, lst = n_ == 0 and f == 0, n_ == count - 1 and g == tiles_[-1]
                    if h == 0:
                        step()
                    sl = slice(h * 128, (h + 1) * 128)
                    for i in range(2):
                        c = slice(i * 512, (i + 1) * 512)
                        o = bk[h][i].t[:, :]
                        mm(o, hi[:, g, sl], u_.hi[:, f, c], first, False, [u_.tok, toks[g]] + (bk[h][i].w if first else []))
                        mm(o, hi[:, g, sl], u_.lo[:, f, c], False, False)
                    for i in range(2):
                        c = slice(i * 512, (i + 1) * 512)
                        m[h][i] = mm(bk[h][i].t[:, :], lo[:, g, sl], u_.hi[:, f, c], False, lst)
                if h == halves - 1:
                    u_.done(m[h][1])
            if after:
                after(n)
            if last:
                end(bk, m)

        n, left = 0, ntile
        for r in order:
            k = min(4, ntile - r)
            pc = wrows(wmat, r * 128, k)
            for f0 in range(0, k, per):
                left -= per
                put(pc.ap[:, f0:f0 + per, :], pc, f0 + per >= k, lambda u, n=n, g0=r + f0, last=left <= 0: use(u, n, [g0 + j for j in range(per)], last))
                n += 1

    def transposed3(src, tiles, hi, lo, toks, bks=banks):
        res = {}
        for k in tiles:
            b = bks.take()
            for h in range(2):
                m = tp(b.t[:, h * 128:(h + 1) * 128], src[:, h, k * 128:(k + 1) * 128], [toks[h], b.w, t_const])
            b.w = [hi_lo(hi[:, k, :], lo[:, k, :], b.t[:, 0:256], [m])]
            res[k] = b.w[0]
        return res

    def A(o, pc, c0, n, w, rhs=None, lhs=None):
        step()
        return chain(o, [(pc.ap[:, k, c0:c0 + n], HT[:, k, :]) for k in range(KC)], [w, pc.tok])

    def Bm(o, pc, c0, n, h, w):
        step()
        return chain(o, [(HT[:, k, h * 128:(h + 1) * 128], pc.ap[:, k, c0:c0 + n]) for k in range(KC)], [w, pc.tok])

    def silu_of(o, i, w):
        return act(o, i, AF.Silu, w)

    def project(src, ntile, wmat, toks, w=()):
        bk = [[banks.take() for _ in range(2)] for _ in range(2)]
        m = [[None] * 2 for _ in range(2)]
        for r in range(0, ntile, 4):
            n = min(4, ntile - r)
            pc = wrows(wmat, r * 128, n)
            for f in range(n):
                step()
                for h in range(2):
                    for i in range(2):
                        first, lst = r + f == 0, r + f == ntile - 1
                        m[h][i] = mm(bk[h][i].t[:, :], src[:, r + f, h * 128:(h + 1) * 128],
                                     pc.ap[:, f, i * 512:(i + 1) * 512], first, lst,
                                     [pc.tok, toks[r + f]] + (bk[h][i].w if first else []))
            pc.done(m[1][1])
        return bk, m

    def transposed(src, ntile, dst, toks, scale=None, w=()):
        res = []
        for k in range(ntile):
            b = banks.take()
            for h in range(2):
                m = tp(b.t[:, h * 128:(h + 1) * 128], src[:, h, k * 128:(k + 1) * 128], [toks[h], b.w, t_const])
            if scale is None:
                c = cp(dst[:, k, :], b.t[:, 0:256], [m, w], eng="scalar" if k % 2 else "vector")
            elif k % 2:
                c = act(dst[:, k, :], b.t[:, 0:256], AF.Copy, [m, w], scale=scale[:, k:k + 1])
            else:
                c = ts(dst[:, k, :], b.t[:, 0:256], scale[:, k:k + 1], ALU.mult, w=[m, w])
            b.w = [c]
            res.append(c)
        return res

    side.append(adaln("hyb", 0, 2, (2,)))
    side.append(adaln("dense", 1, 2))
    side.append(adaln("ssm", 2, 2))
    side.append(adaln("moe", 0, 0))
    ph = ExitStack()
    s_hc = dsem("s_hc")
    for n in ("glamask", "dist", "distc", "blockdiag", "reset64"):
        K[n] = sb("k_" + n, [128, cn[n].shape[1]], ph)
        t_hc = dma(K[n][:, :], cn[n], s_hc, t_early, eng="gpsimd")
    mix = sb("mix", [128, 2, D], ph)
    W = io["hyb_w_in"][0]
    q2 = sb("q2", [128, 2, T], ph)
    k2 = sb("k2", [128, 2, T], ph)
    va = sb("va", [128, 2, 512], ph)
    rs = sb("rs", [128, 2, 512], ph)
    lrT = sb("lrT", [16, T], ph)
    gku = sb("gku", [16, T], ph)
    s_g = dsem("s_gla")
    t_gku = dma(gku[:, :], io["gla_gk_up"][0], s_g, t_early, eng="gpsimd")
    onr = sb("onr", [128, 128], ph)
    t_onr = dma(onr[:, :], io["gla_out_norm"][0].partition_broadcast(128), s_g, eng="gpsimd")
    t_gku = t_onr
    qT = sb("nq", [128, 4, T], ph)
    KCm = [sb(f"kc{j}", [128, 2, T], ph) for j in range(2)]
    kb = [sb(f"kb{j}", [128, T], ph) for j in range(2)]
    vb = [sb(f"vb{j}", [128, 2, 128], ph) for j in range(2)]
    gt = sb("gt", [128, 2, 24], ph)
    pe_sb = sb("pe_sb", [32, 2, 64], ph)
    s_nsa = dsem("s_nsa")
    dma(pe_sb[:, :, :], io["nsa_cmp_pe"][0].rearrange("j b d -> b j d"), s_nsa, eng="gpsimd")
    w2 = sb("w2", [128, 2, 2, 64], ph)
    for j in range(2):
        t_w2 = dma(w2[:, j, :, :], io["nsa_cmp_w2"][0][j].rearrange("(c p) d -> p c d", p=128), s_nsa, eng="gpsimd")
    t_pe = t_w2
    Ee = sb("Ee", [128, 2, T], ph)
    zb = sb("zb", [128, 2, T], ph)
    za = sb("za", [128, 2, T], ph)
    cum = sb("cum", [128, 2, T], ph)
    be = sb("be", [128, 2, 4], ph)
    dec = sb("dec", [128, 2, 4], ph)
    ke = sb("ke", [128, 2, T], ph)
    St = sb("St", [128, 3, 2, 128], ph)
    AT = sb("AT", [128, 2, 4, 128], ph)
    Og = sb("Og", [128, 2, 4, 128], ph)
    vs = sb("vs", [128, 8], ph)
    pe2 = sb("pe2", [128, 2, 16], ph)
    pg = ExitStack()
    new_HT(pg, "0", True)
    new_units(pg, "0", 1024)
    vT = [[sb(f"vT{i}", [128, T], pg), []] for i in range(2)]
    HTf = vT
    HT_done = modulated("hyb")
    n_read = len(vec_read)
    for gen in vec_later:
        for _ in gen:
            pass
    gate_free[0] = vec_read[n_read:]
    prog.hold["tensor"] += HT_done
    bk1, bk2 = Banks(allbanks[0:4]), Banks(allbanks[4:7])
    side_banks = Banks(allbanks[7:8])
    tq, tk, tv, tr, tnq, tkc, tkb, tvb, tg, t_lr, t_gt = [], [], [], [], [], [], [None, None], [[], []], [], [], []
    G = {}

    def tile_qk(f, b, m):
        if f < 2:
            c = act(q2[:, f, :], b.t[:, 0:256], AF.Copy, [m], scale=0.125)
            tq.append(c)
        else:
            c = cp(k2[:, f - 2, :], b.t[:, 0:256], [m])
            tk.append(c)
        b.w = [c]

    def tile_v(hf, b, m):
        b.w = [cp(va[:, hf, :], b.t[:, :], [m], eng="scalar")]
        tv.append(b.w[0])

    def tile_r(hf, b, m):
        b.w = [silu_of(rs[:, hf, :], b.t[:, :], [m])]
        tr.append(b.w[0])

    def use_lr(u):
        b = bk1.take()
        m = A3(b.t[0:16, 0:256], u, 0, [b.w], 16)
        u.done(m)
        t_lr.append(cp(lrT[:, :], b.t[0:16, 0:256], [m]))
        b.w = [t_lr[0]]

    def tile_q(j, b, m):
        c = act(qT[:, j, :], b.t[:, 0:256], AF.Copy, [m], scale=0.125)
        b.w = [c]
        tnq.append(c)

    def tile_c(j, b, m):
        for g in range(2):
            s_ = b.t[g * 64:g * 64 + 64, :]
            c = cp(KCm[j][0:64, g, 0:256], s_[:, 0:256], [m])
            c = cp(KCm[j][64:128, g, 0:255], s_[:, 1:256], [m])
        b.w = [c]
        b2 = bk1.take()
        m2 = tp(b2.t[0:64, 0:32], pe_sb[:, j, :], [t_pe, t_w2, t_const, b2.w])
        pv = b2.t[0:64, 0:32].rearrange("p (i two) -> p two i", two=2)
        c = cp(pe2[0:64, j, :], pv[:, 0, :], [m2])
        c = cp(pe2[64:128, j, :], pv[:, 1, :], [m2])
        b2.w = [c]
        tkc.append(c)

    def down(src, n, t):
        b = bk1.take()
        for hf in range(2):
            m = tp(b.t[:, hf * n:(hf + 1) * n], src[:, hf * 128:(hf + 1) * 128], [t, b.w])
        return b, m

    waiting = []

    def turn_v(j, t):
        b, m = down(vT[j][0], 128, t)
        c = cp(vb[j][:, :, :].rearrange("p h d -> p (h d)"), b.t[:, 0:256], [m])
        b.w = [c]
        tvb[j].append(c)

    def tile_kv(j, i, b, m):
        if i == 0:
            tkb[j] = cp(kb[j][:, :], b.t[:, 0:256], [m], eng="scalar")
            b.w = [tkb[j]]
            if waiting:
                turn_v(*waiting.pop(0))
        else:
            t = cp(vT[j][0][:, :], b.t[:, 0:256], [m, vT[j][1]], eng="scalar")
            b.w = [t]
            waiting.append((j, t))

    def use_gt(u):
        b = bk1.take()
        m = A3(b.t[0:24, 0:256], u, 0, [b.w], 24)
        u.done(m)
        turn_v(*waiting.pop(0))
        t = act(vT[0][0][0:24, :], b.t[0:24, 0:256], AF.Exp, [m, tvb[0]], scale=-1.0)
        b.w = [t]
        b, m = down(vT[0][0][0:24, :], 24, t)
        gv = gt[:, :, :].rearrange("p h c -> p (h c)")
        t = ts(gv, b.t[:, 0:48], 1.0, ALU.add, w=[m])
        b.w = [t]
        t_gt.append(recip(gv, gv, [t]))

    def products():
        pc = wcols(W, 1024, 528)
        put(pc.ap[:, :, 0:16], pc, False, use_lr)
        yield
        yield from rows3(pc, 16, tile_r, bk1)
        yield from columns3(W, 0, 512, tile_qk, bk1)
        yield from rows3(wcols(W, 512, 512), 0, tile_v, bk1)
        pc = wheads(W, 1552)
        for j in range(4):
            def use(u, j=j):
                b = bk1.take()
                m = A3(b.t[:, 0:256], u, 0, [b.w])
                u.done(m)
                tile_q(j, b, m)

            put(pc.ap[:, :, j * 128:(j + 1) * 128], pc, j == 3, use)
            yield
        yield from columns3(W, 2064, 256, tile_c, bk1)
        yield from columns3(W, 2320, 256, lambda i, b, m: tile_kv(0, i, b, m), bk1)
        pc = wcols(W, 2576, 280)
        for i in range(2):
            def use(u, i=i):
                b = bk1.take()
                m = A3(b.t[:, 0:256], u, 0, [b.w])
                u.done(m)
                tile_kv(1, i, b, m)

            put(pc.ap[:, :, i * 128:(i + 1) * 128], pc, False, use)
            yield
        put(pc.ap[:, :, 256:280], pc, True, use_gt)
        while queue:
            u, use = queue.pop(0)
            use(u)
            yield

    def gla():
        Eq, Ek = zb, za
        while len(tr) < 2:
            yield
        lnexp()
        bz = bk2.take()
        tz = []
        for f in range(2):
            m = mm(bz.t[:, f * 256:(f + 1) * 256], gku[:, f * 128:(f + 1) * 128], lrT[:, :], w=[t_lr, t_gku, bz.w])
        for f in range(2):
            tz.append(ts(zb[:, f, :], bz.t[:, f * 256:(f + 1) * 256], vec["gk_bias"][:, f:f + 1], ALU.add, w=[m, vec_tok["gk_bias"]]))
        bz.w = tz
        yield
        t = act(za[:, :, :], zb[:, :, :], AF.Abs, tz)
        t = act(za[:, :, :], za[:, :, :], AF.Exp, [t], scale=-1.0)
        t = act(za[:, :, :], za[:, :, :], AF.Ln, [t], bias=1.0)
        t = stt(zb[:, :, :], zb[:, :, :], 0.0, za[:, :, :], ALU.min, ALU.subtract, [t])
        tcum = [scan(cum[:, f, :], K["reset64"][:, :], zb[:, f, :], [t, t_hc]) for f in range(2)]
        ce = cum[:, :, :].rearrange("p f (n c) -> p f n c", c=64)[:, :, :, 63]
        tbe = ts(be[:, :, :], ce, 1.0 / 16, ALU.mult, w=tcum)
        tde = act(dec[:, :, :], be[:, :, :], AF.Exp, [tbe])
        t1 = act(Eq[:, :, :], cum[:, :, :], AF.Exp, tcum, scale=1.0 / 16)
        t2 = act(Ek[:, :, :], cum[:, :, :], AF.Exp, tcum, scale=-1.0 / 16)
        for f in range(2):
            for n in range(4):
                t3 = act(Ee[:, f, n * 64:(n + 1) * 64], cum[:, f, n * 64:(n + 1) * 64], AF.Exp, [tbe], scale=-1.0 / 16, bias=be[:, f, n:n + 1])
        while len(tk) < 2:
            yield
        tqd = tt(q2[:, :, :], q2[:, :, :], Eq[:, :, :], ALU.mult, [tq, t1])
        tke = tt(Ee[:, :, :], k2[:, :, :], Ee[:, :, :], ALU.mult, [tk, t3])
        tkd = tt(k2[:, :, :], k2[:, :, :], Ek[:, :, :], ALU.mult, [tke, t2])
        b = bk2.take()
        for hf in range(2):
            for f in range(2):
                m = tp(b.t[:, hf * 256 + f * 128:hf * 256 + (f + 1) * 128], Ee[:, f, hf * 128:(hf + 1) * 128], [tke, b.w])
        tket = cp(ke[:, :, :].rearrange("p a b -> p (a b)"), b.t[:, :], [m])
        b.w = [tket]
        yield
        while len(tv) < 2:
            yield
        ts_ = None
        tst = []
        for n in range(3):
            hf, r = n // 2, (n % 2) * 64
            b = bk2.take()
            for f in range(2):
                for g in range(2):
                    hd = f * 2 + g
                    m = mm(b.t[g * 64:g * 64 + 64, f * 128:(f + 1) * 128], ke[r:r + 64, hf, f * 128 + g * 64:f * 128 + g * 64 + 64],
                           va[r:r + 64, hf, hd * 128:(hd + 1) * 128], w=[tket, tv, b.w])
            if n == 0:
                ts_ = cp(St[:, 0, :, :], b.t[:, 0:256].rearrange("p (f v) -> p f v", v=128), [m])
            else:
                for f in range(2):
                    ts_ = stt(St[:, n, f, :], St[:, n - 1, f, :], dec[:, f, n:n + 1], b.t[:, f * 128:(f + 1) * 128], ALU.mult, ALU.add, [m, tde, ts_])
            b.w = [ts_]
            step()
            yield
            tst.append(ts_)
        tat = []
        for g in range(2):
            b = bk2.take()
            for f in range(2):
                for hf in range(2):
                    m = mm(b.t[:, (f * 2 + hf) * 128:(f * 2 + hf + 1) * 128], k2[g * 64:g * 64 + 64, f, hf * 128:(hf + 1) * 128],
                           q2[g * 64:g * 64 + 64, f, hf * 128:(hf + 1) * 128], w=[tqd, tkd, b.w])
            c = tt(AT[:, g, :, :], b.t[:, :].rearrange("p (a c) -> p a c", c=128), bc(K["glamask"][:, :], 1, 4), ALU.mult, [m, t_hc])
            b.w = [c]
            yield
            step()
            tat.append(c)
        to_ = []
        for hf in range(2):
            for g in range(2):
                b = bk2.take()
                for f in range(2):
                    hd = f * 2 + g
                    o = b.t[:, f * 128:(f + 1) * 128]
                    m = mm(o, AT[:, g, f * 2 + hf, :], va[:, hf, hd * 128:(hd + 1) * 128], w=[tat, tv, b.w])
                    for n in (2 * hf, 2 * hf + 1):
                        if n:
                            r = (n % 2) * 64
                            m = mm(o[r:r + 64, :], q2[g * 64:g * 64 + 64, f, n * 64:(n + 1) * 64], St[g * 64:g * 64 + 64, n - 1, f, :], False, True, [tst], skip=True)
                c = cp(Og[:, hf, :, :].rearrange("p (f g) v -> p g f v", g=2)[:, g, :, :], b.t[:, 0:256].rearrange("p (f v) -> p f v", v=128), [m])
                b.w = [c]
                yield
                step()
                to_.append(c)
        og3 = Og[:, :, :, :].rearrange("p h a v -> p (h a) v")
        sq = AT[:, :, :, :].rearrange("p g a v -> p (g a) v")
        t = tt(sq, og3, og3, ALU.mult, to_)
        t = red(vs[:, :], sq, ALU.add, [t])
        t = ts(vs[:, :], vs[:, :], 1.0 / 128, ALU.mult, EPS, ALU.add, w=[t])
        t = act(vs[:, :], vs[:, :], AF.Ln, [t])
        t = act(vs[:, :], vs[:, :], AF.Exp, [t], scale=-0.5)
        t = tt(og3, og3, bc(vs[:, :], 2, 128), ALU.mult, [t])
        t = tt(og3, og3, bc(onr[:, :], 1, 8), ALU.mult, [t, t_onr])
        G["gla"] = tt(mix[:, :, 0:512], Og[:, :, :, :].rearrange("p h a v -> p h (a v)"), rs[:, :, :], ALU.mult, [t, tr])

    weave(products(), gla())
    t_gla = G["gla"]
    pg.close()
    settle()
    pg = ExitStack()
    nb = [z_[:, :, :, :].rearrange("p g a v -> p g (a v)") for z_ in (AT, Og)]
    hid = sb("hid", [128, 2, 2, 2, 16], pg)
    hx = sb("hx", [30, 2, 256], pg)
    xk = sb("xk", [128, 2, 16, 30], pg)
    hy = sb("hy", [30, 2, 256], pg)
    hz = sb("hz", [30, 2, 256], pg)
    kcT = sb("kcT", [128, 16], pg)
    vbd = sb("vbd", [128, 8, 64], pg)
    hrep = sb("hrep", [128, 2, 8, 16], pg)
    vct = sb("vct", [128, 64], pg)
    Sb = [sb(f"S{i}", [128, 8, 256], pg) for i in range(2)]
    PTb = [sb(f"PT{i}", [128, 8, 2, 128], pg) for i in range(2)]
    mxb = [sb(f"mx{i}", [128, 8], pg) for i in range(2)]
    smb = [sb(f"sm{i}", [128, 8], pg) for i in range(2)]
    facb = [sb(f"fac{i}", [128, 8], pg) for i in range(2)]
    small = [[sb(f"c{n}{i}", sh, pg) for n, sh in (("s", [128, 8, 16]), ("m", [128, 8]), ("u", [128, 8]), ("f", [128, 8]), ("p", [128, 128]), ("t", [128, 128]))] for i in range(2)]
    slope = [2.0 ** -(i + 1) for i in range(8)]
    bk1 = Banks(allbanks[5:7])
    bkb = [Banks(allbanks[0:3]), Banks(allbanks[3:5])]
    t_nb = [None, None]
    t_br = [[None, None], [None, None]]

    def compressed():
        z = fill(hid[:, :, :, :, :].rearrange("p a b c d -> p (a b c d)"), 0.0)
        thid, t_x = [], []
        for j in range(2):
            pc = load(io["nsa_cmp_w1"][0][j].rearrange("(i p) n -> p i n", p=128), (16, 256))
            x_ = xk[:, j, :, :].rearrange("p i (g n) -> p i g n", n=15)
            for g in range(2):
                r = KCm[j][:, g, 0:254]
                r2 = bass.AP(tensor=r.tensor, offset=r.offset, ap=[list(r.ap)[0], [2, 16], [16, 15]])
                t = tt(x_[:, :, g, :], r2, bc(pe2[:, j, :], 2, 15), ALU.add, [tkc[j]])
            b = bk1.take()
            m = chain(b.t[0:30, 0:256], [(xk[:, j, i, :], pc.ap[:, i, :]) for i in range(16)], [pc.tok, t, b.w])
            pc.done(m)
            t_x.append(cp(hx[:, j, :], b.t[0:30, 0:256], [m], eng="scalar"))
            b.w = [t_x[j]]
            step()
            yield
        x_, y_, z_ = hx[:, :, :], hy[:, :, :], hz[:, :, :]
        t2 = tt(y_, x_, x_, ALU.mult, t_x)
        t2 = ts(y_, y_, 0.044715, ALU.mult, 1.0, ALU.add, w=[t2])
        t2 = tt(y_, y_, x_, ALU.mult, [t2])
        t2 = act(z_, y_, AF.Exp, [t2], scale=-2.0 * 0.7978845608028654)
        t2 = ts(z_, z_, 1.0, ALU.add, w=[t2])
        t2 = recip(z_, z_, [t2])
        t2 = tt(x_, x_, z_, ALU.mult, [t2])
        step()
        for _ in range(3):
            yield
        for j in range(2):
            b = bk1.take()
            for c_ in range(2):
                m = tp(b.t[:, c_ * 30:(c_ + 1) * 30], hx[:, j, c_ * 128:(c_ + 1) * 128], [t2, b.w])
            t = cp(hid[:, j, :, :, 0:15], b.t[:, 0:60].rearrange("p (c g n) -> p c g n", g=2, n=15), [m, z])
            b.w = [t]
            thid.append(t)
        yield
        b = bk1.take()
        for g in range(2):
            m = chain(b.t[g * 64:g * 64 + 64, 0:16], [(w2[:, 0, c_, :], hid[:, 0, c_, g, :]) for c_ in range(2)], [thid, t_w2, b.w])
        t_kcT = cp(kcT[:, :], b.t[:, 0:16], [m])
        b.w = [t_kcT]
        yield
        b = bk1.take()
        for c_ in range(2):
            t = cp(hrep[:, c_, :, :].rearrange("p (g r) n -> p g r n", r=4), bc(hid[:, 1, c_, :, :], 2, 4), [thid])
        m = chain(b.t[:, 0:64], [(hrep[:, c_, :, :].rearrange("p a n -> p (a n)"), w2[:, 1, c_, :]) for c_ in range(2)], [t, t_w2, b.w])
        t = cp(vct[:, :], b.t[:, 0:64], [m])
        b.w = [t]
        yield
        t_vbd = tt(vbd[:, :, :], bc(vct[:, :], 1, 8), bc(K["blockdiag"][:, :], 2, 64), ALU.mult, [t, t_hc])
        G["kcT"], G["vbd"] = t_kcT, t_vbd

    def blocks(hf):
        if hf == 0:
            yield from compressed()
        while "vbd" not in G:
            yield
        Sc_, mxc, smc, facc, pcm, PTc = small[hf]
        q_ = slice(hf * 128, hf * 128 + 128)
        Sc = Sc_[:, :, :]
        t = None
        for g in range(2):
            b = bk1.take()
            for j in range(4):
                m = mm(b.t[:, j * 16:(j + 1) * 16], qT[g * 64:g * 64 + 64, j, q_], kcT[g * 64:g * 64 + 64, :], w=[tnq, G["kcT"], b.w])
            for j in range(4):
                hd = g * 4 + j
                c = stt(Sc_[:, hd, :], K["distc"][:, hf * 16:(hf + 1) * 16], -slope[hd], b.t[:, j * 16:(j + 1) * 16], ALU.mult, ALU.add, [m, t, t_hc])
            b.w = [c]
            yield
        t = red(mxc[:, :], Sc, ALU.max, [c], negate=True)
        t = ts(mxc[:, :], mxc[:, :], 1e20, ALU.min, w=[t])
        t = tt(Sc, Sc, bc(mxc[:, :], 2, 16), ALU.add, [t])
        t = act(Sc, Sc, AF.Exp, [t])
        t2 = red(smc[:, :], Sc, ALU.add, [t])
        t2 = ts(smc[:, :], smc[:, :], 1e-20, ALU.max, w=[t2])
        t2 = recip(smc[:, :], smc[:, :], [t2])
        t_fac = tt(facc[:, :], smc[:, :], gt[:, hf, :].rearrange("p (a c) -> p c a", c=3)[:, 0, :], ALU.mult, [t2, t_gt])
        t = cp(pcm[:, :].rearrange("p (a n) -> p a n", n=16), Sc, [t])
        b = bk1.take()
        m = tp(b.t[:, 0:128], pcm[:, :], [t, b.w])
        t = cp(PTc[:, :], b.t[:, 0:128], [m])
        b.w = [t]
        yield
        b = bk1.take()
        m = mm(b.t[:, :], PTc[:, :], vbd[:, :, :].rearrange("p a d -> p (a d)"), w=[t, G["vbd"], b.w])
        t = tt(nb[0][:, hf, :].rearrange("p (a d) -> p a d", d=64), b.t[:, :].rearrange("p (a d) -> p a d", d=64), bc(facc[:, :], 2, 64), ALU.mult, [m, t_fac])
        b.w = [t]
        yield
        t_nb[hf] = t

    def branch(br):
        bks, S_, PT_, mx_, sm_, fac_ = bkb[br], Sb[br], PTb[br], mxb[br], smb[br], facb[br]
        dst = nb[1] if br == 0 else mix[:, :, 512:1024]
        free_S, free_PT, free_sm = [], [], []
        for hf in range(2):
            q_ = slice(hf * 128, hf * 128 + 128)
            nk = (hf + 1) * 128
            per = 512 // nk
            t_p = [None] * 8
            for g in range(2):
                for j0 in range(0, 4, per):
                    b = bks.take()
                    for j in range(j0, j0 + per):
                        m = mm(b.t[:, (j - j0) * nk:(j - j0 + 1) * nk], qT[g * 64:g * 64 + 64, j, q_], kb[br][g * 64:g * 64 + 64, 0:nk], w=[tnq, tkb[br], b.w])
                    for j in range(j0, j0 + per):
                        hd = g * 4 + j
                        c = stt(S_[:, hd, 0:nk], K["dist"][:, 256 - nk:256], -slope[hd], b.t[:, (j - j0) * nk:(j - j0 + 1) * nk], ALU.mult, ALU.add, [m, free_S, t_hc])
                    b.w = [c]
                t = red(mx_[:, g * 4:g * 4 + 4], S_[:, g * 4:g * 4 + 4, 0:nk], ALU.max, [c, free_sm], negate=True)
                yield
                for hd in range(g * 4, g * 4 + 4):
                    t_p[hd] = act(S_[:, hd, 0:nk], S_[:, hd, 0:nk], AF.Exp, [t, free_sm], bias=mx_[:, hd:hd + 1], accum_out=sm_[:, hd:hd + 1])
            t2 = recip(sm_[:, :], sm_[:, :], t_p)
            t_fac = tt(fac_[:, :], sm_[:, :], gt[:, hf, :].rearrange("p (a c) -> p c a", c=3)[:, br + 1, :], ALU.mult, [t2, t_gt, free_sm])
            t_pt = []
            for hd in range(0, 8, 2):
                b = bks.take()
                for a in range(2):
                    for k in range(hf + 1):
                        m = tp(b.t[:, (a * (hf + 1) + k) * 128:(a * (hf + 1) + k + 1) * 128], S_[:, hd + a, k * 128:(k + 1) * 128], [t_p[hd:hd + 2], b.w])
                c = cp(PT_[:, hd:hd + 2, 0:hf + 1, :], b.t[:, 0:2 * nk].rearrange("p (a k q) -> p a k q", a=2, q=128), [m, free_PT], eng="scalar" if hd % 4 else "vector")
                b.w = [c]
                step()
                yield
                t_pt.append(c)
            free_S = [m]
            b = bks.take()
            for hd in range(8):
                g = hd // 4
                m = chain(b.t[:, hd * 64:(hd + 1) * 64], [(PT_[:, hd, k, :], vb[br][:, k, g * 64:g * 64 + 64]) for k in range(hf + 1)], [t_pt, tvb[br], b.w])
            free_PT = [m]
            t = tt(dst[:, hf, :].rearrange("p (a d) -> p a d", d=64), b.t[:, :].rearrange("p (a d) -> p a d", d=64), bc(fac_[:, :], 2, 64), ALU.mult, [m, t_fac])
            b.w = [t]
            yield
            free_sm = [t]
            t_br[br][hf] = t
        G[br] = free_PT

    weave(branch(0), branch(1), blocks(0), blocks(1))
    tm_ = []
    for hf in range(2):
        o = mix[:, hf, 512:1024]
        t = tt(nb[0][:, hf, :], nb[0][:, hf, :], nb[1][:, hf, :], ALU.add, [t_nb[hf], t_br[0][hf]], eng="gpsimd")
        tm_.append([tt(o, o, nb[0][:, hf, :], ALU.add, [t, t_br[1][hf]]), t_gla])
    side_banks = Banks(allbanks[3:4])
    tb = Banks(allbanks[0:3])
    pg.close()
    settle(t_nb, t_br[0], t_br[1])
    pg = ExitStack()
    mh, ml = sb("mixTh", [128, 8, T], pg, R32), sb("mixTl", [128, 8, T], pg, R32)
    new_units(pg, "o", 1024)
    tm = {}

    def begin():
        tm.update(transposed3(mix, range(4), mh, ml, [t_gla, t_gla], tb))

    def after(n):
        if n == 2:
            tm.update(transposed3(mix, range(4, 8), mh, ml, tm_, tb))

    project3(mh, ml, 8, io["hyb_w_out"][0], tm, 2, lambda bk, m: gated_add(bk, "hyb", m), [allbanks[4:6], allbanks[6:8]], begin, after)
    drain()
    side_banks = banks
    pace[0] = (4, 5)
    prog.barrier(ends_x)
    pg.close()
    ph.close()

    def up3(Wg, nf, epilogue):
        half = nf * 128
        for c0 in range(0, half, 512):
            n = min(512, half - c0)
            pg, pu = wcols(Wg, c0, n), wcols(Wg, half + c0, n)
            for f0 in range(0, n, 256):
                first = []

                def use_gate(u, first=first):
                    for f in range(0, 256, 128):
                        b = banks.take()
                        first.append((b, A3(b.t[:, 0:256], u, f, [b.w])))
                    u.done(first[-1][1])

                def use_up(u, first=first, i=(c0 + f0) // 128):
                    for f in range(2):
                        b = banks.take()
                        m2 = A3(b.t[:, 0:256], u, f * 128, [b.w])
                        epilogue(i + f, first[f][0], b, first[f][1], m2)
                    u.done(m2)

                put(pg.ap[:, :, f0:f0 + 256], pg, f0 + 256 >= n, use_gate)
                yield
                put(pu.ap[:, :, f0:f0 + 256], pu, f0 + 256 >= n, use_up)
                yield

    ph = ExitStack()
    sg = [[sb(f"sg{i}", [128, T], ph), []] for i in range(2)]
    hTh, hTl = sb("hTh", [128, 22, T], ph, R32), sb("hTl", [128, 22, T], ph, R32)
    new_HT(ph, "1", True)
    new_units(ph, "1")
    HTf = sg
    t = []

    def gated(i, bg, bu, m1, m2):
        s_ = sg[i % 2]
        a = silu_of(s_[0][:, :], bg.t[:, 0:256], [m1, s_[1]])
        bg.w = [a]
        c = tt(s_[0][:, :], s_[0][:, :], bu.t[:, 0:256], ALU.mult, [m2, a])
        bu.w = [c]
        late.append((i, c))
        if len(late) > 1:
            parts()

    def parts():
        i, c = late.pop(0)
        s_ = sg[i % 2]
        s_[1] = [hi_lo(hTh[:, i, :], hTl[:, i, :], s_[0][:, :], [c])]
        t.append(s_[1][0])

    late = []
    ups = up3(io["dense_w_gu"][0], 22, gated)
    prog.hold["tensor"] += modulated("dense", ups)
    run(ups)
    project3(hTh, hTl, 22, io["dense_w_down"][0], t, 2, lambda bk, m: gated_add(bk, "dense", m), None, parts)
    drain()
    pace[0] = (1, 1)
    ready("moe", "rows")
    prog.barrier(ends_x)
    ph.close()
    pmacc.close()

    ph = ExitStack()
    W = io["ssm_w_in"][0]
    new_units(ph, "2")
    zs = sb("zs", [128, 16, T], ph)
    xT = sb("xT", [128, 16, T], ph)
    dD = sb("dD", [128, 16], ph)
    dcol = sb("dcol", [32, 4], ph)
    drow = sb("drow", [128, 32], ph)
    pu = ExitStack()
    xt = sb("xt", [128, 2, 2048], pu)
    BC = sb("BC", [128, 8, T], pu)
    dtT = sb("dtT", [32, T], pu)
    daT = sb("daT", [32, T], pu)
    cmT = sb("cmT", [32, T], pu)
    dtc = sb("dtc", [128, 2, 32], pu)
    cmc = sb("cmc", [128, 2, 32], pu)
    pa = ExitStack()
    cv = [[gates[1][:, i * T:(i + 1) * T], []] for i in range(3)]
    s_m = dsem("s_mamba")
    for i, n in enumerate(("ssm_dt_bias", "ssm_a_log")):
        dma(dcol[:, i:i + 1], io[n][0].rearrange("(p a) -> p a", a=1), s_m, prog.last(), eng="gpsimd")
    t_dc = dma(drow[:, :], io["ssm_d"][0].partition_broadcast(128), s_m, eng="gpsimd")
    for a in range(2):
        t_dD = cp(dD[a * 64:(a + 1) * 64, :], drow[a * 64:(a + 1) * 64, :].rearrange("p (i two) -> p two i", two=2)[:, a, :], [t_dc])
    new_HT(pa, "2", True)
    HTf = cv
    t_cols = []

    def use_dt(u):
        b = banks.take()
        m = A3(b.t[0:32, 0:256], u, 0, [b.w], 32)
        u.done(m)
        lnexp()
        t1 = ts(dtT[:, :], b.t[0:32, 0:256], dcol[:, 0:1], ALU.add, w=[m, t_dc])
        b.w = [t1]
        t = act(daT[:, :], dtT[:, :], AF.Abs, [t1])
        t = act(daT[:, :], daT[:, :], AF.Exp, [t], scale=-1.0)
        t = act(daT[:, :], daT[:, :], AF.Ln, [t], bias=1.0)
        t_dt = stt(dtT[:, :], dtT[:, :], 0.0, daT[:, :], ALU.max, ALU.add, [t])
        t2 = act(dcol[:, 2:3], dcol[:, 1:2], AF.Exp, [t_dc])
        t = ts(daT[:, :], dtT[:, :], dcol[:, 2:3], ALU.mult, -1.0, ALU.mult, w=[t2, t_dt])
        t_cols.append(scan(cmT[:, :], ones[0:32, 0:1].to_broadcast([32, T]), daT[:, :], [t, t_ones]))

    t_x2, t_bc, tz, late = [], [], [], []
    t_xT = []
    cw, cb = vec["conv_w"], vec["conv_b"]

    def turn():
        r, t = late.pop(0)
        b = banks.take()
        for hf in range(2):
            m2 = tp(b.t[:, hf * 128:(hf + 1) * 128], xT[:, r, hf * 128:(hf + 1) * 128], [t, b.w])
        b.w = [cp(xt[:, :, r * 128:(r + 1) * 128], b.t[:, 0:256].rearrange("p (h n) -> p h n", h=2), [m2], eng="scalar")]
        t_x2.append(b.w[0])
        t_xT.append(m2)

    def tile_x(r, b, m):
        c_ = cv[r % 3]
        t = act(c_[0][:, :], b.t[:, 0:256], AF.Identity, [m, c_[1], vec_tok["conv_w"], vec_tok["conv_b"]], scale=cw[:, 72 + r:73 + r], bias=cb[:, r:r + 1])
        for j in (2, 1, 0):
            n = 3 - j
            t = stt(c_[0][:, n:T], b.t[:, 0:T - n], cw[:, j * 24 + r:j * 24 + r + 1], c_[0][:, n:T], ALU.mult, ALU.add, [t])
        b.w = [t]
        made.append((r, t))
        if len(made) > 1:
            active()
        if len(late) > 4:
            turn()

    def active():
        r, t = made.pop(0)
        c_ = cv[r % 3]
        if r < 16:
            t = silu_of(xT[:, r, :], c_[0][:, :], [t])
            late.append((r, t))
        else:
            t = silu_of(BC[:, r - 16, :], c_[0][:, :], [t])
            t_bc.append(t)
        c_[1] = [t]

    def tile_z(i, b, m):
        b.w = [silu_of(zs[:, i, :], b.t[:, 0:256], [m])]
        tz.append(b.w[0])
        if made:
            active()
        if late:
            turn()

    made = []
    def products():
        pc = wcols(W, 5120, 32)
        put(pc.ap, pc, True, use_dt)
        gen = columns3(W, 2048, 3072, tile_x)
        next(gen)
        yield
        yield from gen

    ups = products()
    prog.hold["tensor"] += modulated("ssm", ups)
    run(ups)
    run(columns3(W, 0, 2048, tile_z))
    drain()
    pa.close()
    pb = ExitStack()
    b = banks.take()
    for hf in range(2):
        m = tp(b.t[:, hf * 32:hf * 32 + 32], dtT[:, hf * 128:(hf + 1) * 128], [t_cols, b.w])
    for hf in range(2):
        m = tp(b.t[:, 64 + hf * 32:96 + hf * 32], cmT[:, hf * 128:(hf + 1) * 128])
    cp(dtc[:, :, :].rearrange("p a b -> p (a b)"), b.t[:, 0:64], [m])
    t_col = cp(cmc[:, :, :].rearrange("p a b -> p (a b)"), b.t[:, 64:128])
    b.w = [t_col]
    lnexp()
    CB = sb("CB", [128, 4, 384], pb)
    t_cb = []
    for g in range(4):
        b = banks.take()
        mm(b.t[:, 0:256], BC[:, g, 0:128], BC[:, 4 + g, :], w=[t_bc, b.w])
        m = mm(b.t[:, 256:384], BC[:, g, 128:256], BC[:, 4 + g, 128:256])
        c = tt(CB[:, g, 0:128], b.t[:, 0:128], K["causal"][:, :], ALU.mult, [m, t_const])
        c = cp(CB[:, g, 128:256], b.t[:, 128:256])
        c = tt(CB[:, g, 256:384], b.t[:, 256:384], K["causal"][:, :], ALU.mult)
        b.w = [c]
        t_cb.append(c)
    EB = [[sb(f"eb{i}", [128, 384], pb), []] for i in range(4)]
    sq = [[sb(f"msq{i}", [128, T], pb), []] for i in range(2)]
    rs = xn[:, 0, :].rearrange("p (g t) -> p g t", t=T)
    rowbanks = Banks(allbanks[0:3])
    ybanks = Banks(allbanks[3:6])
    stbanks = Banks(allbanks[6:8])
    t_e, t_z, t_rs = {}, [None] * 16, [None] * 4
    pend, state = [], {}

    def decays(hd):
        g, e_ = hd // 8, EB[hd % 4]
        b = rowbanks.take()
        m = mm(b.t[:, 0:256], K["ident"][0:32, hd:hd + 1].to_broadcast([32, 128]), cmT[:, :], w=[t_cols, b.w])
        t = ts(e_[0][:, 0:256], b.t[:, 0:256], cmc[:, 0, hd:hd + 1], ALU.subtract, 0.0, ALU.min, w=[m, t_col, e_[1]])
        t = ts(e_[0][:, 256:384], b.t[:, 128:256], cmc[:, 1, hd:hd + 1], ALU.subtract, 0.0, ALU.min)
        b.w = [t]
        t = act(e_[0][:, :], e_[0][:, :], AF.Exp, [t])
        stt(e_[0][:, 0:256], e_[0][:, 0:256], dtc[:, 0, hd:hd + 1], CB[:, g, 0:256], ALU.mult, ALU.mult, [t, t_cb])
        t_e[hd] = stt(e_[0][:, 256:384], e_[0][:, 256:384], dtc[:, 1, hd:hd + 1], CB[:, g, 256:384], ALU.mult, ALU.mult)

    def squares(i, a):
        g = i // 4
        if i % 4 == 0:
            state["st"] = stbanks.take()
        b = state["st"]
        m = mm(b.t[:, 0:256], ones[:, :], sq[i % 2][0][:, :], i % 4 == 0, i % 4 == 3, [a, b.w])
        sq[i % 2][1] = [m]
        if i % 4 == 3:
            t = ts(rs[:, g, :], b.t[:, 0:256], 1.0 / 512, ALU.mult, EPS, ALU.add, w=[m, xn_free])
            b.w = [t]
            t = act(rs[:, g, :], rs[:, g, :], AF.Ln, [t])
            t_rs[g] = act(rs[:, g, :], rs[:, g, :], AF.Exp, [t], scale=-0.5)

    def normed(g):
        for i in range(4 * g, 4 * g + 4):
            t_z[i] = stt(zs[:, i, :], zs[:, i, :], vec["gate_norm"][:, i:i + 1], rs[:, g, :], ALU.mult, ALU.mult, [t_rs[g], t_z[i]])

    def outputs(hd):
        i, p0, e_ = hd // 2, (hd % 2) * 64, EB[hd % 4]
        if p0 == 0:
            state["y"] = ybanks.take()
        b = state["y"]
        c0 = hd * 64
        mm(b.t[p0:p0 + 64, 0:256], xt[:, 0, c0:c0 + 64], e_[0][:, 0:256], True, False, [t_e[hd], t_x2, b.w], skip=True)
        m = mm(b.t[p0:p0 + 64, 128:256], xt[:, 1, c0:c0 + 64], e_[0][:, 256:384], False, True, skip=True)
        e_[1] = [m]
        if p0:
            t = stt(xT[:, i, :], xT[:, i, :], dD[:, i:i + 1], b.t[:, 0:256], ALU.mult, ALU.add, [m, t_dD, t_xT])
            b.w = [t]
            t = tt(zs[:, i, :], zs[:, i, :], xT[:, i, :], ALU.mult, [t, tz], eng="gpsimd")
            s_ = sq[i % 2]
            a = act(s_[0][:, :], zs[:, i, :], AF.Square, [t, s_[1]])
            t_z[i] = a
            if pend:
                squares(*pend.pop())
            pend.append((i, a))
            if i > 4 and i % 4 == 2:
                normed(i // 4 - 1)
        return m

    for hd in range(34):
        if hd < 32:
            decays(hd)
        if hd >= 2:
            m = outputs(hd - 2)
    squares(*pend.pop())
    pb.close()
    pu.close()
    yh, yl = sb("yTh", [128, 16, T], ph, R32), sb("yTl", [128, 16, T], ph, R32)
    prog.hold["scalar"] += [m] + sq[0][1] + sq[1][1]
    ty = []
    normed(3)
    for g in range(4):
        v = lambda x: x[:, 4 * g:4 * g + 4, :].rearrange("p a t -> p (a t)")
        ty += [hi_lo(v(yh), v(yl), v(zs), t_z[4 * g:4 * g + 4])] * 4
    project3(yh, yl, 16, io["ssm_w_out"][0], ty, 2, lambda bk, m: gated_add(bk, "ssm", m))
    drain()
    prog.barrier(ends_x)
    ph.close()

    ph = ExitStack()
    rw = sb("rw", [128, KC, NE], ph)
    s_r = dsem("s_router")
    t_rw = dma(rw[:, :, :], io["moe_router"][0].rearrange("(k p) e -> p k e", p=128), s_r, ends_x, eng="gpsimd")
    new_HT(ph, "3")
    L = sb("L", [128, 2, NE], ph)
    gt = sb("egate", [128, 2, NE], ph)
    sel = sb("esel", [128, 2, NE], ph)
    pos = sb("epos", [128, 2, NE], ph)
    pr = sb("pr", [128, 2, 2, 64], ph)
    e1_ = sb("e1_", [128, 2], ph)
    fl = sb("fl", [1, 2], ph)
    fli = sb("fli", [1, 1], ph, mybir.dt.int32)
    with ExitStack() as early:
        raw = sb("first", [128, KC, 512], early)
    hTh, hTl = sb("ehTh", [128, 28, 128], ph, R32), sb("ehTl", [128, 28, 128], ph, R32)
    XGh, XGl = sb("XGh", [128, KC, 128], ph, R32), sb("XGl", [128, KC, 128], ph, R32)
    XGf, Y = HT[:, 0:4, :].rearrange("p a (b s) -> p (a b) s", s=128), HT[:, 4:8, :].rearrange("p a b -> p (a b)")
    Pe, PT = sb("Pe", [128, 2, 128], ph), [sb(f"PTe{i}", [128, 2, 128], ph) for i in range(2)]
    hrow = [[sb(f"hrow{i}", [128, 512], ph), []] for i in range(2)]
    new_units(ph, "3")
    moe_start = list(ends_x)
    h = modulated("moe")
    (s1, s2), toks, g = s12["moe"], mod["moe"]["cols"], gates[mod["moe"]["slot"]]
    free = {"hT": [], "XG": [], "Y": [], "XGf": [], "PT": [[], []], "Pe": []}
    t_acc = [[t_X[hf]] * 2 for hf in range(2)]
    dbanks = allbanks[6:8]
    ubanks = Banks(allbanks[0:6])
    route = {}
    fn_ = gates[1]
    t_fn = dma(fn_[:, :], io["final_norm"].partition_broadcast(128), dsem("s_fn"), moe_start, eng="gpsimd")

    def routed():
        b = banks.take()
        for hf in range(2):
            m = chain(b.t[:, hf * 8:hf * 8 + 8], [(HT[:, k, hf * 128:(hf + 1) * 128], rw[:, k, :]) for k in range(KC)], [h, t_rw, b.w])
        free["Y"], free["XGf"] = [m], [m]
        t_L = cp(L[:, :, :].rearrange("p h e -> p (h e)"), b.t[:, 0:16], [m])
        b.w = [t_L]
        e3 = lambda x: x.rearrange("p h (e j) -> p (h e) j", j=8)
        p1, p2 = pr[:, 0, :, :], pr[:, 1, :, :]
        for hf in range(2):
            lj, le = bc(L[:, hf, :], 1, 8), bc(L[:, hf, :], 2, 8)
            t = tt(p1[:, hf, :].rearrange("p (e j) -> p e j", j=8), lj, le, ALU.is_equal, [t_L])
            t2 = tt(p2[:, hf, :].rearrange("p (e j) -> p e j", j=8), lj, le, ALU.is_gt, [t_L])
        t3 = red(e1_[:, :], L[:, :, :], ALU.max, [t_L])
        t = tt(p1, p1, bc(K["tie"][:, :], 1, 2), ALU.mult, [t, t_const])
        t3 = tt(L[:, :, :], L[:, :, :], bc(e1_[:, :], 2, 8), ALU.subtract, [t3, t2])
        t = tt(p1, p1, p2, ALU.add, [t, t2])
        t3 = act(L[:, :, :], L[:, :, :], AF.Exp, [t3])
        t = red(sel[:, :, :].rearrange("p h e -> p (h e)"), e3(p1), ALU.add, [t])
        t_sel = ts(sel[:, :, :], sel[:, :, :], 1.5, ALU.is_lt, w=[t])
        b = banks.take()
        mm(b.t[:, 0:8], K["before"][:, :], sel[:, 0, :], w=[t_sel, b.w])
        chain(b.t[:, 8:16], [(ones[:, :], sel[:, 0, :]), (K["before"][:, :], sel[:, 1, :])])
        m = chain(b.t[:, 16:24], [(ones[:, :], sel[:, 0, :]), (ones[:, :], sel[:, 1, :])])
        t_pos = cp(pos[:, :, :].rearrange("p h e -> p (h e)"), b.t[:, 0:16], [m])
        route.update(sel=t_sel, pos=t_pos)
        yield
        t = red(fl[:, 0:1], b.t[0:1, 16:24], ALU.max, [m])
        b.w = [t]
        t = ts(fl[:, 1:2], fl[:, 0:1], CAP + 0.5, ALU.is_gt, w=[t])
        route["flag"] = cp(fli[:, :], fl[:, 1:2], [t])
        t = tt(gt[:, :, :], sel[:, :, :], L[:, :, :], ALU.mult, [t_sel, t3])
        t = red(e1_[:, :], gt[:, :, :], ALU.add, [t])
        t = recip(e1_[:, :], e1_[:, :], [t])
        route["gate"] = tt(gt[:, :, :], gt[:, :, :], bc(e1_[:, :], 2, 8), ALU.mult, [t])

    def gather(e, blk, where):
        for hf in range(2):
            t = ts(Pe[:, hf, :], K["iota"][:, blk * CAP:blk * CAP + 128], pos[:, hf, e:e + 1], ALU.is_equal, sel[:, hf, e:e + 1], ALU.mult, w=[route["pos"], route["sel"], free["Pe"]])
            if CAP < 128:
                t = fill(Pe[:, hf, CAP:128], 0.0, [t])
        yield
        b = ubanks.take()
        for hf in range(2):
            m = tp(b.t[:, hf * 128:(hf + 1) * 128], Pe[:, hf, :], [t, b.w])
        yield
        t_pt = cp(PT[e % 2][:, :, :].rearrange("p h t -> p (h t)"), b.t[:, 0:256], [m, free["PT"][e % 2]])
        b.w = [t_pt]
        done = []
        for k0 in range(0, KC, 4):
            b = ubanks.take()
            for k in range(k0, k0 + 4):
                m = chain(b.t[:, (k - k0) * 128:(k - k0 + 1) * 128], [(xn[:, hf, k * 128:(k + 1) * 128], Pe[:, hf, :]) for hf in range(2)], [t, b.w])
            yield
            for k in range(k0, k0 + 4):
                c = ts(XGf[:, k, :], b.t[:, (k - k0) * 128:(k - k0 + 1) * 128], s1[:, k:k + 1], ALU.mult, s2[:, k:k + 1], ALU.add, w=[m, toks, free["XGf"]])
            b.w = [c]
            done.append(c)
        free["Pe"] = [m]
        yield
        t_xg = [hi_lo(XGh[:, k0:k0 + 4, :], XGl[:, k0:k0 + 4, :], XGf[:, k0:k0 + 4, :], [c], free["XG"]) for k0, c in zip((0, 4), done)]
        free["XGf"] = t_xg
        where[e] = t_pt, t_xg

    class Late:
        h, put = None, None

    class First(Piece):
        def done(self, *toks):
            free["hT"] = list(toks)

    def experts(blk):
        late = Late()
        where = {}
        made = 0

        def turned(j, hr, c, t_h):
            b = ubanks.take()
            for a in range(4):
                m = tp(b.t[:, a * 128:(a + 1) * 128], hr[0][:, a * 128:(a + 1) * 128], [c, b.w])
            hr[1] = [m]
            v = lambda x: x[:, 4 * j:4 * j + 4, :].rearrange("p a s -> p (a s)")
            t = hi_lo(v(hTh), v(hTl), b.t[:, :], [m], free["hT"])
            b.w = [t]
            t_h[4 * j:4 * j + 4] = [t] * 4

        def use_up(u, e, j, p_, k0, cur):
            if k0 == 0:
                cur.append([ubanks.take(), None])
            b = cur[p_][0]
            t_xg = where[e][1][k0 // 4]
            for k in range(4):
                first, last = k0 + k == 0, k0 + k == KC - 1
                mm(b.t[:, :], XGh[:, k0 + k, :], u.hi[:, k, :], first, False, [u.tok, t_xg, b.w])
                mm(b.t[:, :], XGh[:, k0 + k, :], u.lo[:, k, :], False, False)
                m = mm(b.t[:, :], XGl[:, k0 + k, :], u.hi[:, k, :], False, last)
            u.done(m)
            cur[p_][1] = m
            if p_ == 0 and k0 and late.h:
                turned(*late.h)
                late.h = None
            if p_ == 1 and k0:
                hr = hrow[j % 2]
                (b1, m1), (b2, m2) = cur
                a = silu_of(hr[0][:, :], b1.t[:, :], [m1, hr[1]])
                b1.w = [a]
                c = tt(hr[0][:, :], hr[0][:, :], b2.t[:, :], ALU.mult, [a, m2])
                b2.w = [c]
                late.h = (j, hr, c, t_hs[e])
                if j == 6:
                    free["XG"] = [m2]

        def use_end(e, bk, m):
            free["hT"] = [m[0][1]]
            t_y = []
            for i in range(2):
                c = tt(Y[:, i * 512:(i + 1) * 512], dbanks[i].t[:, :], g[:, i * 512:(i + 1) * 512], ALU.mult, [m[0][i], mod["moe"]["rows"], free["Y"]])
                dbanks[i].w = [c]
                t_y.append(c)
            late.put = (e, t_y)

        def put_back(e, t_y):
            for hf in range(2):
                for i in range(2):
                    b = ubanks.take()
                    m = mm(b.t[:, :], PT[e % 2][:, hf, :], Y[:, i * 512:(i + 1) * 512], w=[t_y, where[e][0], b.w])
                    o = X[:, hf, i * 512:(i + 1) * 512]
                    c = stt(o, b.t[:, :], gt[:, hf, e:e + 1], o, ALU.mult, ALU.add, [m, t_acc[hf][i], route["gate"]])
                    b.w = [c]
                    t_acc[hf][i] = c
            free["Y"] = [m]
            free["PT"][e % 2] = [m]

        t_hs = [[None] * 28 for _ in range(NE)]
        for e in range(NE):
            Wg, Wd = io["moe_w_gu"][0][e], io["moe_w_down"][0][e]
            for j in range(7):
                cur = []
                for p_ in range(2):
                    if (blk, e, j, p_) == (0, 0, 1, 1):
                        src = Wg[:, FE + 512:FE + 1024].rearrange("(k p) n -> p k n", p=128)
                        pc = First(None, raw[:, :, :], dma(raw[:, :, :], src, dsem("s_eh"), moe_start))
                    else:
                        pc = wcols(Wg, p_ * FE + j * 512, 512)
                    for k0 in range(0, KC, 4):
                        def use(u, e=e, j=j, p_=p_, k0=k0, cur=cur):
                            use_up(u, e, j, p_, k0, cur)
                            if j == 0 and p_ == 1 and k0 and late.put:
                                put_back(*late.put)
                                late.put = None
                        put(pc.ap[:, k0:k0 + 4, :], pc, k0 > 0, use)
                        made += 1
                        if made == AHEAD:
                            yield
                            run(gather(0, blk, where))
                            yield

            coming = gather(e + 1, blk, where) if e + 1 < NE else iter(())

            def after(n, coming=coming):
                if n == 0:
                    turned(*late.h)
                    late.h = None
                else:
                    next(coming, None)

            project3(hTh, hTl, 28, Wd, t_hs[e], 1, lambda bk, m, e=e: use_end(e, bk, m), [dbanks], None, after)
        drain()
        put_back(*late.put)

    work, routes = experts(0), routed()
    next(work)
    next(routes)
    next(work)
    run(routes)
    run(work)
    prog.begin_if(fli[0:1, 0:1], route["flag"])
    run(experts(1))
    prog.end_if()
    t_X[:] = t_acc
    xn_free = t_X
    t2 = rms(xn)
    t_X = [tt(X[:, hf, :], xn[:, hf, :], fn_[:, :], ALU.mult, [t2[hf], t_fn]) for hf in range(2)]
    xn_free = t_X
    prog.barrier()
    ph.close()

    pfirst.close()
    lnr = sb("lnr", [128, 2, D])
    st = sb("st", [128, 2, 2, 6])
    mv = sb("mv", [128, 2, 2])
    rs_ = sb("rs_", [128, 2])
    ln_eps = sb("lneps", [128, 1])
    t_ln_eps = fill(ln_eps[:, :], LN_EPS, prog.last())
    for l in range(2):
        ph = ExitStack()
        Wl = io["w_in_2"][l]
        s_l = dsem(f"s_ln{l}")
        for i, n in enumerate(("ln1_g_2", "ln1_b_2")):
            dma(lnr[:, i, :], io[n][l].partition_broadcast(128), s_l, prog.last(), eng="gpsimd")
        hcol = sb(f"hcol{l}", [64, 4], ph)
        for i, n in enumerate(("gdn_dt_bias_2", "gdn_a_log_2")):
            dma(hcol[0:4, i:i + 1], io[n][l].rearrange("(p a) -> p a", a=1), s_l, eng="gpsimd")
        gnr = sb(f"gnr{l}", [128, 128], ph)
        t_l = dma(gnr[:, :], io["gdn_norm_g_2"][l].partition_broadcast(128), s_l, eng="gpsimd")
        s_lt = dsem(f"s_lt{l}")
        pm = ExitStack()
        for n in ("levels", "cmask", "cos", "sin", "perm", "reset128"):
            K[n] = sb(f"k_{n}{l}", [128, cn[n].shape[1]], pm)
            t_lt = dma(K[n][:, :], cn[n], s_lt, prog.last(), eng="gpsimd")
        mix = sb(f"mix{l}", [128, 2, D], pm)
        qk = sb(f"qk{l}", [128, 12, T], pm)
        zsl = sb(f"zsl{l}", [128, 2, 512], pm)
        qr = sb(f"qr{l}", [128, 8, T], pm)
        vbt = sb(f"vbt{l}", [128, 2, 512], pm)
        gb = sb(f"gb{l}", [64, T], pm)
        ga = sb(f"ga{l}", [64, T], pm)
        gc = sb(f"gc{l}", [4, T], pm)
        col = sb(f"col{l}", [128, 2, 64], pm)
        eg = sb(f"eg_{l}", [128, 8], pm)
        nbe = sb(f"nbe{l}", [128, 4], pm)
        sq = sb(f"sq{l}", [128, 8, T], pm)
        vtm = sb(f"vtm{l}", [128, 2, 4, 128], pm)
        kd = sb(f"kd{l}", [128, 4, 128], pm)
        DT = sb(f"DT{l}", [128, 8, 128], pm)
        ATb = sb(f"ATb{l}", [128, 8, 128], pm)
        AAb = sb(f"AAb{l}", [128, 8, 128], pm)
        pg = ExitStack()
        cv = [[sb(f"gcv{l}{i}", [128, T], pg), []] for i in range(3)]
        rt = [[sb(f"rt{l}{i}", [128, T], pg), []] for i in range(3)]
        new_HT(pg, f"m{l}", True)
        new_units(pg, f"m{l}", 1024)
        bk1, bk2 = Banks(allbanks[0:4]), Banks(allbanks[4:8])
        gcw = vec[f"gconv{l}"]
        tc, made, tz, tq, tvb, t_ab_ = [], [], [], [], [], []

        def active():
            r, t = made.pop(0)
            cv[r % 3][1] = [silu_of(qk[:, r, :], cv[r % 3][0][:, :], [t])]
            tc.append(cv[r % 3][1][0])

        def tile_conv(r, b, m):
            c_ = cv[r % 3]
            t = act(c_[0][:, :], b.t[:, 0:256], AF.Copy, [m, c_[1], vec_tok[f"gconv{l}"]], scale=gcw[:, 36 + r:37 + r])
            for j in (2, 1, 0):
                n = 3 - j
                t = stt(c_[0][:, n:T], b.t[:, 0:T - n], gcw[:, j * 12 + r:j * 12 + r + 1], c_[0][:, n:T], ALU.mult, ALU.add, [t])
            b.w = [t]
            made.append((r, t))
            if r:
                active()

        def tile_z(hf, b, m):
            if made:
                active()
            b.w = [silu_of(zsl[:, hf, :], b.t[:, :], [m])]
            tz.append(b.w[0])

        def tile_v(hf, b, m):
            b.w = [cp(vbt[:, hf, :], b.t[:, :], [m], eng="scalar")]
            tvb.append(b.w[0])

        def turned(r, t):
            b = bk1.take()
            m = mm(b.t[:, 0:256], K["perm"][:, :], qr[:, r, :], w=[t, t_lt, b.w])
            r_ = rt[r % 3]
            t2 = tt(r_[0][:, :], b.t[:, 0:256], K["sin"][:, :], ALU.mult, [m, r_[1], t_lt])
            b.w = [t2]
            t = tt(qr[:, r, :], qr[:, r, :], K["cos"][:, :], ALU.mult, [t, m, t_lt], eng="gpsimd")
            t = tt(qr[:, r, :], qr[:, r, :], r_[0][:, :], ALU.add, [t, t2], eng="gpsimd")
            r_[1] = [t]
            tq.append(t)

        def tile_qk(r, b, m):
            t = act(qr[:, r, :], b.t[:, 0:256], AF.Copy, [m], scale=0.125 if r < 4 else 1.0)
            b.w = [t]
            made.append((r, t))
            if r:
                turned(*made.pop(0))

        def use_ab(u):
            bab = bk2.take()
            A3(bab.t[0:4, 0:256], u, 0, [bab.w], 4)
            m_ab = A3(bab.t[0:4, 256:512], u, 4, [], 4)
            u.done(m_ab)
            t_ab_.append((bab, m_ab))

        ups = columns3(Wl, 0, 1536, tile_conv, bk1)
        next(ups)
        next(ups)
        h, m = to_HT(X, t_X)
        prog.hold["tensor"] += h
        run(ups)
        pc_z = wcols(Wl, 1536, 520)
        run(rows3(pc_z, 8, tile_z, bk1, False))
        put(pc_z.ap[:, :, 0:8], pc_z, True, use_ab)

        def products():
            yield from columns3(Wl, 2056, 1024, tile_qk, bk1)
            yield from rows3(wcols(Wl, 3080, 512), 0, tile_v, bk1)
            while queue:
                u, use = queue.pop(0)
                use(u)
                yield
            turned(*made.pop(0))

        def prepared():
            while not t_ab_:
                yield
            bab, m_ab = t_ab_[0]
            lnexp()
            z = fill(gb[:, :], 0.0)
            t1 = ts(ga[0:4, :], bab.t[0:4, 0:256], hcol[0:4, 0:1], ALU.add, w=[m_ab, t_l])
            t2 = act(ga[32:36, :], bab.t[0:4, 256:512], AF.Exp, [m_ab, t1], scale=-1.0)
            bab.w = [t2]
            yield
            t = act(gc[:, :], ga[0:4, :], AF.Abs, [t1])
            t = act(gc[:, :], gc[:, :], AF.Exp, [t], scale=-1.0)
            t = act(gc[:, :], gc[:, :], AF.Ln, [t], bias=1.0)
            t = stt(ga[0:4, :], ga[0:4, :], 0.0, gc[:, :], ALU.max, ALU.add, [t])
            t3 = act(hcol[0:4, 2:3], hcol[0:4, 1:2], AF.Exp, [t_l])
            t = ts(ga[0:4, :], ga[0:4, :], hcol[0:4, 2:3], ALU.mult, -1.0, ALU.mult, w=[t, t3])
            t4 = scan(gb[0:4, :], K["reset128"][0:4, :], ga[0:4, :], [t, z, t_l, t_lt])
            t = ts(ga[32:36, :], ga[32:36, :], 1.0, ALU.add, w=[t2])
            t5 = recip(gb[32:36, :], ga[32:36, :], [t, z])
            t_ab = [t4, t5]
            yield
            b = bk2.take()
            for hf in range(2):
                m = tp(b.t[:, hf * 64:hf * 64 + 64], gb[:, hf * 128:(hf + 1) * 128], [t_ab, b.w])
            t_col = cp(col[:, :, :].rearrange("p h c -> p (h c)"), b.t[:, 0:128], [m])
            b.w = [t_col]
            t_eg = act(eg[:, :].rearrange("p (h a) -> p h a", h=2), col[:, :, 0:4], AF.Exp, [t_col])
            t_nbe = stt(nbe[:, :], eg[:, 4:8], -1.0, col[:, 1, 32:36], ALU.mult, ALU.mult, [t_eg])
            yield
            t_qk = []
            for j in range(4):
                r = 2 * j
                t = tt(sq[:, r:r + 2, :], qk[:, r:r + 2, :], qk[:, r:r + 2, :], ALU.mult, tc)
                b = bk2.take()
                for a in range(2):
                    m = mm(b.t[:, a * 256:(a + 1) * 256], ones[:, :], sq[:, r + a, :], w=[t, t_ones, b.w])
                sv = sq[:, r:r + 2, :].rearrange("p a t -> p (a t)")
                t = ts(sv, b.t[:, :], EPS, ALU.add, w=[m])
                b.w = [t]
                t = act(sv, sv, AF.Ln, [t])
                t = act(sv, sv, AF.Exp, [t], scale=-0.5)
                yield
                qv = qk[:, r:r + 2, :].rearrange("p a t -> p (a t)")
                if j < 2:
                    t_qk.append(stt(qv, qv, 128 ** -0.5, sv, ALU.mult, ALU.mult, [t]))
                else:
                    t_qk.append(tt(qv, qv, sv, ALU.mult, [t]))
            t_v = []
            for hf in range(2):
                b = bk2.take()
                for a in range(4):
                    m = tp(b.t[:, a * 128:(a + 1) * 128], qk[:, 8 + a, hf * 128:(hf + 1) * 128], [tc, b.w])
                c = tt(vtm[:, hf, :, :], b.t[:, :].rearrange("p (a d) -> p a d", d=128), bc(col[:, hf, 32:36], 2, 128), ALU.mult, [m, t_col])
                b.w = [c]
                t_v.append(c)
                yield
            t_dt, t_att, t_aa = [], [], []
            t_bt = []
            brow = sq[:, 0:4, :]
            for a in range(4):
                b = bk2.take()
                m1 = mm(b.t[:, 0:256], K["ident"][0:64, a:a + 1].to_broadcast([64, 128]), gb[:, :], w=[t_ab, t_l, b.w])
                m1 = mm(b.t[:, 256:512], K["ident"][0:64, 32 + a:33 + a].to_broadcast([64, 128]), gb[:, :])
                for c_ in range(2):
                    t = ts(DT[:, c_ * 4 + a, :], b.t[:, c_ * 128:(c_ + 1) * 128], col[:, c_, a:a + 1], ALU.subtract, 0.0, ALU.min, w=[m1, t_col])
                t_bt.append(cp(brow[:, a, :], b.t[:, 256:512], [t_qk]))
                b.w = [t_bt[-1]]
                t_dt.append(t)
                yield
            t_dx = act(DT[:, :, :], DT[:, :, :], AF.Exp, t_dt)
            b = bk2.take()
            for a in range(4):
                m = tp(b.t[:, a * 128:(a + 1) * 128], qk[:, 4 + a, 0:128], [t_qk, b.w])
            t_kd = tt(kd[:, :, :], b.t[:, :].rearrange("p (a d) -> p a d", d=128), bc(DT[:, 0:4, 127], 2, 128), ALU.mult, [m, t_dx])
            b.w = [t_kd]
            yield
            t_dm = tt(DT[:, :, :], DT[:, :, :], bc(K["causal"][:, :], 1, 8), ALU.mult, [t_dx, t_kd])
            for c_ in range(2):
                s_ = slice(c_ * 128, (c_ + 1) * 128)
                b, b2 = bk2.take(), bk2.take()
                for a in range(4):
                    m = mm(b.t[:, a * 128:(a + 1) * 128], qk[:, 4 + a, s_], qk[:, a, s_], w=[t_qk, b.w])
                for a in range(4):
                    m2 = mm(b2.t[:, a * 128:(a + 1) * 128], qk[:, 4 + a, s_], qk[:, 4 + a, s_], w=[b2.w])
                dv = DT[:, c_ * 4:c_ * 4 + 4, :].rearrange("p a i -> p (a i)")
                c = tt(ATb[:, c_ * 4:c_ * 4 + 4, :].rearrange("p a i -> p (a i)"), b.t[:, :], dv, ALU.mult, [m, t_dm])
                b.w = [c]
                t_att.append(c)
                av = AAb[:, c_ * 4:c_ * 4 + 4, :]
                c = tt(av.rearrange("p a i -> p (a i)"), b2.t[:, :], dv, ALU.mult, [m2, t_dm])
                b2.w = [c]
                t_aa.append(tt(av, av, brow[:, :, s_], ALU.mult, [c, t_bt]))
                yield
            G.update(t_nbe=t_nbe, t_qk=t_qk, t_v=t_v, t_kd=t_kd, t_att=t_att, t_aa=t_aa)

        G = {}
        weave(products(), prepared())
        pg.close()
        settle()
        po = ExitStack()
        U = sb(f"U{l}", [128, 2, 4, 128], po)
        S1 = sb(f"S1{l}", [128, 4, 128], po)
        Og = sb(f"Ogd{l}", [128, 2, 4, 128], po)
        vs = sb(f"gvs{l}", [128, 8], po)
        pg = ExitStack()
        Xi = sb(f"Xi{l}", [128, 8, 128], pg)
        Xt = sb(f"Xt{l}", [128, 8, 128], pg)
        Ci = sb(f"Ci{l}", [128, 8, 128], pg)
        S = sb(f"Sm{l}", [128, 8, 256], pg)
        PT = sb(f"PTm{l}", [128, 8, 2, 128], pg)
        mx = sb(f"mxm{l}", [128, 8], pg)
        sm = sb(f"smm{l}", [128, 8], pg)
        bk1, bk2 = Banks(allbanks[0:5]), Banks(allbanks[5:8])

        def solved():
            t_nbe, t_qk, t_v, t_kd, t_att, t_aa = (G[k] for k in ("t_nbe", "t_qk", "t_v", "t_kd", "t_att", "t_aa"))
            Pi = DT
            t_X0, t_Xt, t_P = [None, None], [None, None], [None, None]
            free_C, free_P = [None, None], [None, None]
            idb = bc(K["ident"][:, :], 1, 4)
            for n in range(7):
                lm = K["levels"][:, n * 128:(n + 1) * 128]
                for c_ in range(2):
                    s_ = slice(c_ * 4, c_ * 4 + 4)
                    fl = lambda z_: z_[:, s_, :].rearrange("p a i -> p (a i)")
                    t_c = tt(Ci[:, s_, :], AAb[:, s_, :], bc(lm, 1, 4), ALU.mult, [t_aa, t_lt, free_C[c_]], eng="gpsimd")
                    b = bk1.take()
                    for a in range(4):
                        i = c_ * 4 + a
                        m = mm(b.t[:, a * 128:(a + 1) * 128], Ci[:, i, :], K["ident"][:, :] if n == 0 else Xi[:, i, :], w=[t_c, b.w, t_X0[c_]])
                    free_C[c_] = [m]
                    if n == 0:
                        c = tt(Xi[:, s_, :], idb, b.t[:, :].rearrange("p (a i) -> p a i", i=128), ALU.subtract, [m])
                        b.w = [c]
                        t_X0[c_] = c
                        t_Xt[c_] = tt(Xt[:, s_, :], idb, Ci[:, s_, :], ALU.subtract, [t_c])
                        free_C[c_] = [m, t_Xt[c_]]
                    else:
                        t_P[c_] = cp(fl(Pi), b.t[:, :], [m, free_P[c_], t_aa, t_att], eng="scalar")
                        b.w = [t_P[c_]]
                yield
                for c_ in range(2):
                    if n == 0:
                        continue
                    s_ = slice(c_ * 4, c_ * 4 + 4)
                    fl = lambda z_: z_[:, s_, :].rearrange("p a i -> p (a i)")
                    if n < 6:
                        b = bk1.take()
                        for a in range(4):
                            i = c_ * 4 + a
                            m = mm(b.t[:, a * 128:(a + 1) * 128], Xt[:, i, :], Pi[:, i, :], w=[t_P[c_], t_Xt[c_], b.w])
                        t_X0[c_] = tt(fl(Xi), fl(Xi), b.t[:, :], ALU.subtract, [m])
                        b.w = [t_X0[c_]]
                    b = bk1.take()
                    for a in range(4):
                        i = c_ * 4 + a
                        m = mm(b.t[:, a * 128:(a + 1) * 128], Pi[:, i, :], Xt[:, i, :], w=[t_P[c_], t_Xt[c_], b.w])
                    t_Xt[c_] = tt(fl(Xt), fl(Xt), b.t[:, :], ALU.subtract, [m])
                    b.w = [t_Xt[c_]]
                    free_P[c_] = [m]
                yield
            f4 = lambda z_: z_.rearrange("p a d -> p (a d)")

            def four(fl_, fr_, w):
                b = bk1.take()
                for a in range(4):
                    m = mm(b.t[:, a * 128:(a + 1) * 128], fl_(a), fr_(a), w=[w, b.w])
                return b, m

            b, m = four(lambda a: Xt[:, a, :], lambda a: vtm[:, 0, a, :], [t_Xt[0], t_v])
            tu = cp(f4(U[:, 0, :, :]), b.t[:, :], [m])
            b.w = [tu]
            yield
            b, m = four(lambda a: kd[:, a, :], lambda a: U[:, 0, a, :], [tu, t_kd])
            tS = cp(f4(S1[:, :, :]), b.t[:, :], [m])
            b.w = [tS]
            yield
            b, m = four(lambda a: ATb[:, a, :], lambda a: U[:, 0, a, :], [t_att])
            to0 = cp(f4(Og[:, 0, :, :]), b.t[:, :], [m], eng="scalar")
            b.w = [to0]
            yield
            b, m = four(lambda a: qk[:, 4 + a, 128:256], lambda a: S1[:, a, :], [tS])
            for a in range(4):
                tr_ = stt(vtm[:, 1, a, :], b.t[:, a * 128:(a + 1) * 128], nbe[:, a:a + 1], vtm[:, 1, a, :], ALU.mult, ALU.add, [m, t_nbe])
            b.w = [tr_]
            yield
            bq, mq = four(lambda a: qk[:, a, 128:256], lambda a: S1[:, a, :], [])
            b, m = four(lambda a: Xt[:, 4 + a, :], lambda a: vtm[:, 1, a, :], [tr_, t_Xt[1]])
            G["Xt"] = m
            tu = cp(f4(U[:, 1, :, :]), b.t[:, :], [m])
            b.w = [tu]
            yield
            b, m = four(lambda a: ATb[:, 4 + a, :], lambda a: U[:, 1, a, :], [tu])
            tc1 = cp(f4(Og[:, 1, :, :]), b.t[:, :], [m])
            b.w = [tc1]
            yield
            for a in range(4):
                to1 = stt(Og[:, 1, a, :], bq.t[:, a * 128:(a + 1) * 128], eg[:, 4 + a:5 + a], Og[:, 1, a, :], ALU.mult, ALU.add, [mq, tc1])
            bq.w = [to1]
            yield
            G["og"] = [to0, to1, m]

        def normed():
            og3 = Og[:, :, :, :].rearrange("p h a v -> p (h a) v")
            sq3 = U[:, :, :, :].rearrange("p h a v -> p (h a) v")
            t = tt(sq3, og3, og3, ALU.mult, G["og"])
            t = red(vs[:, :], sq3, ALU.add, [t])
            t = ts(vs[:, :], vs[:, :], 1.0 / 128, ALU.mult, EPS, ALU.add, w=[t])
            t = act(vs[:, :], vs[:, :], AF.Ln, [t])
            t = act(vs[:, :], vs[:, :], AF.Exp, [t], scale=-0.5)
            t = tt(og3, og3, bc(vs[:, :], 2, 128), ALU.mult, [t])
            t = tt(og3, og3, bc(gnr[:, :], 1, 8), ALU.mult, [t, t_l])
            G["out"] = tt(mix[:, :, 0:512], Og[:, :, :, :].rearrange("p h a v -> p h (a v)"), zsl[:, :, :], ALU.mult, [t, tz])

        def attended():
            free_S, free_PT, free_sm = [], [], []
            for hf in range(2):
                nk = (hf + 1) * 128
                per = 512 // nk
                t_p = [None] * 8
                for g in range(2):
                    for j0 in range(0, 4, per):
                        b = bk2.take()
                        for j in range(j0, j0 + per):
                            m = mm(b.t[:, (j - j0) * nk:(j - j0 + 1) * nk], qr[g * 64:g * 64 + 64, j, hf * 128:(hf + 1) * 128], qr[g * 64:g * 64 + 64, 4 + j, 0:nk], w=[tq, b.w])
                        sv = S[:, :, :].rearrange("p (j g) k -> p g j k", g=2)[:, g, j0:j0 + per, :]
                        bv = b.t[:, 0:per * nk].rearrange("p (j k) -> p j k", k=nk)
                        c = tt(sv[:, :, nk - 128:nk], bv[:, :, nk - 128:nk], bc(K["cmask"][:, :], 1, per), ALU.add, [m, free_S, t_lt])
                        if hf:
                            c = cp(sv[:, :, 0:128], bv[:, :, 0:128], [m, free_S])
                        b.w = [c]
                        yield
                t = red(mx[:, :], S[:, :, 0:nk], ALU.max, [c, free_sm], negate=True)
                for hd in range(8):
                    t_p[hd] = act(S[:, hd, 0:nk], S[:, hd, 0:nk], AF.Exp, [t, free_sm], bias=mx[:, hd:hd + 1], accum_out=sm[:, hd:hd + 1])
                t_s = recip(sm[:, :], sm[:, :], t_p)
                t_pt = []
                for hd in range(0, 8, 2):
                    b = bk2.take()
                    for a in range(2):
                        for k in range(hf + 1):
                            m = tp(b.t[:, (a * (hf + 1) + k) * 128:(a * (hf + 1) + k + 1) * 128], S[:, hd + a, k * 128:(k + 1) * 128], [t_p[hd:hd + 2], b.w])
                    c = cp(PT[:, hd:hd + 2, 0:hf + 1, :], b.t[:, 0:2 * nk].rearrange("p (a k q) -> p a k q", a=2, q=128), [m, free_PT], eng="scalar" if hd % 4 else "vector")
                    b.w = [c]
                    yield
                    t_pt.append(c)
                free_S = [m]
                b = bk2.take()
                for hd in range(8):
                    m = chain(b.t[:, hd * 64:(hd + 1) * 64], [(PT[:, hd, k, :], vbt[:, k, hd * 64:(hd + 1) * 64]) for k in range(hf + 1)], [t_pt, tvb, b.w])
                free_PT = [m]
                t = tt(mix[:, hf, 512:1024].rearrange("p (a d) -> p a d", d=64), b.t[:, :].rearrange("p (a d) -> p a d", d=64), bc(sm[:, :], 2, 64), ALU.mult, [m, t_s])
                b.w = [t]
                yield
                free_sm = [t]
                t_mb.append(t)

        t_mb = []
        weave(solved(), attended())
        def post_norm(bk, m, t_ln):
            ends_x[:] = prog.ends()
            lnexp()
            for hf in range(2):
                for i in range(2):
                    s_ = slice(i * 512, (i + 1) * 512)
                    t = stt(xn[:, hf, s_], X[:, hf, s_], ALPHA, bk[hf][i].t[:, :], ALU.mult, ALU.add, [m[hf][i], t_X[hf], xn_free])
                    bk[hf][i].w = [t]
                    t = prog.add("vector", lambda e, o=st[:, hf, i, :], i_=xn[:, hf, s_]: e.bn_stats(o, i_), [t])
                t = prog.add("vector", lambda e, o=mv[:, hf, :], i_=st[:, hf, :, :].rearrange("p a b -> p (a b)"): e.bn_aggr(o, i_), [t])
                t1 = act(rs_[:, hf:hf + 1], mv[:, hf, 1:2], AF.Ln, [t, t_ln_eps], bias=ln_eps[:, :])
                t1 = act(rs_[:, hf:hf + 1], rs_[:, hf:hf + 1], AF.Exp, [t1], scale=-0.5)
                t = stt(xn[:, hf, :], xn[:, hf, :], mv[:, hf, 0:1], lnr[:, 0, :], ALU.subtract, ALU.mult, [t, t_ln])
                t_X[hf] = stt(X[:, hf, :], xn[:, hf, :], rs_[:, hf:hf + 1], lnr[:, 1, :], ALU.mult, ALU.add, [t, t1])

        pg.close()
        settle(t_mb, G["Xt"])
        pg = ExitStack()
        mh, ml = sb(f"mixTh{l}", [128, 8, T], pg, R32), sb(f"mixTl{l}", [128, 8, T], pg, R32)
        new_units(pg, f"o{l}", 1024)
        tm = {}

        def begin():
            tm.update(transposed3(mix, range(4, 8), mh, ml, t_mb))
            normed()

        def after(n):
            if n == 2:
                tm.update(transposed3(mix, range(4), mh, ml, [G["out"]] * 2))

        project3(mh, ml, 8, io["w_out_2"][l], tm, 2, lambda bk, m: post_norm(bk, m, t_l), None, begin, after, (4, 0))
        drain()
        xn_free = list(t_X)
        s_l2 = dsem(f"s_l2{l}")
        for i, n in enumerate(("ln2_g_2", "ln2_b_2")):
            t_l2 = dma(lnr[:, i, :], io[n][l].partition_broadcast(128), s_l2, t_X, eng="gpsimd")
        prog.barrier(ends_x)
        pg.close()
        po.close()
        pm.close()
        pf = ExitStack()
        hTh, hTl = sb(f"fhTh{l}", [128, 22, T], pf, R32), sb(f"fhTl{l}", [128, 22, T], pf, R32)
        cg = [[sb(f"cg{l}{i}", [128, T], pf), []] for i in range(3)]
        cu = [[sb(f"cu{l}{i}", [128, T], pf), []] for i in range(3)]
        new_HT(pf, f"f{l}", True)
        new_units(pf, f"f{l}")
        w01, w2_, wb = vec[f"fconv{l}"], vec[f"fconv2{l}"], vec[f"fconvb{l}"]
        vt = [vec_tok[f"fconv{l}"], vec_tok[f"fconv2{l}"]]

        def conv3(dst, b, m, r):
            t = act(dst[0][:, :], b.t[:, 0:256], AF.Identity, [m, dst[1], vt], scale=w2_[:, r:r + 1], bias=wb[:, r:r + 1])
            t = stt(dst[0][:, 1:T], b.t[:, 0:T - 1], w01[:, 44 + r:45 + r], dst[0][:, 1:T], ALU.mult, ALU.add, [t])
            t = stt(dst[0][:, 2:T], b.t[:, 0:T - 2], w01[:, r:r + 1], dst[0][:, 2:T], ALU.mult, ALU.add, [t])
            b.w = [t]
            return t

        th = []

        def gated_conv(i, b1, b2, m1, m2):
            c1, c2 = cg[i % 3], cu[i % 3]
            t1 = conv3(c1, b1, m1, i)
            t2 = conv3(c2, b2, m2, 22 + i)
            late.append((i, t1, t2))
            more()

        def more(end=False):
            if late2:
                i, t = late2.pop(0)
                c1 = cg[i % 3]
                c1[1] = [hi_lo(hTh[:, i, :], hTl[:, i, :], c1[0][:, :], [t])]
                th.append(c1[1][0])
            if len(late) > 1 or (end and late):
                i, t1, t2 = late.pop(0)
                c1, c2 = cg[i % 3], cu[i % 3]
                t = silu_of(c1[0][:, :], c1[0][:, :], [t1])
                t = tt(c1[0][:, :], c1[0][:, :], c2[0][:, :], ALU.mult, [t, t2], eng="gpsimd")
                c2[1] = [t]
                late2.append((i, t))

        def rest():
            while late or late2:
                more(True)

        late, late2 = [], []
        ups = up3(io["w_up_2"][l], 22, gated_conv)
        next(ups)
        h, m = to_HT(X, t_X)
        prog.hold["tensor"] += h
        run(ups)
        project3(hTh, hTl, 22, io["w_down_2"][l], th, 2, lambda bk, m: post_norm(bk, m, t_l2), None, rest)
        drain()
        xn_free = list(t_X)
        prog.barrier(ends_x)
        pf.close()
        ph.close()

    s_out = dsem("s_out")
    t_out = dma(out[0].rearrange("(h p) d -> p h d", p=128), X[:, :, :], s_out, t_X)
    sems_end = [t_out]
    prog.number(sems)
    with ctx, nc.Block() as block:
        @block.sync
        def _(e):
            prog.write("sync", e)
            for t in sems_end:
                e.wait_ge(t.sem, t.val)

        @block.tensor
        def _(e):
            prog.write("tensor", e)

        @block.vector
        def _(e):
            prog.write("vector", e)

        @block.scalar
        def _(e):
            prog.write("scalar", e)

        @block.gpsimd
        def _(e):
            prog.write("gpsimd", e)


NAMES = ['x', 'c', 'hyb_norm', 'hyb_mod_w', 'hyb_mod_b', 'hyb_w_in', 'gla_gk_up', 'gla_gk_bias', 'gla_out_norm', 'nsa_cmp_pe',
         'nsa_cmp_w1', 'nsa_cmp_w2', 'hyb_w_out', 'dense_norm', 'dense_mod_w', 'dense_mod_b', 'dense_w_gu', 'dense_w_down',
         'ssm_norm', 'ssm_mod_w', 'ssm_mod_b', 'ssm_w_in', 'ssm_conv_w', 'ssm_conv_b', 'ssm_dt_bias', 'ssm_a_log', 'ssm_d',
         'ssm_gate_norm', 'ssm_w_out', 'moe_norm', 'moe_mod_w', 'moe_mod_b', 'moe_router', 'moe_w_gu', 'moe_w_down', 'final_norm',
         'w_in_2', 'gdn_conv_w_2', 'gdn_a_log_2', 'gdn_dt_bias_2', 'gdn_norm_g_2', 'w_out_2', 'ln1_g_2', 'ln1_b_2', 'w_up_2',
         'ffn_conv_w_2', 'ffn_conv_b_2', 'w_down_2', 'ln2_g_2', 'ln2_b_2']


def kernel(**inputs):
    import concourse.bacc as bacc
    from concourse.bass_utils import run_bass_kernel_spmd

    nc = bacc.Bacc("TRN2", target_bir_lowering=False, num_devices=1)
    arrays, io, cn = {}, {}, {}
    for n in NAMES:
        a = np.ascontiguousarray(inputs[n])
        arrays["in_" + n] = a
        io[n] = nc.dram_tensor("in_" + n, a.shape, mybir.dt.float32, kind="ExternalInput").ap()
    for n, a in constants().items():
        arrays["const_" + n] = a
        cn[n] = nc.dram_tensor("const_" + n, a.shape, mybir.dt.float32, kind="ExternalInput").ap()
    out = nc.dram_tensor("out", (1, T, D), mybir.dt.float32, kind="ExternalOutput").ap()
    program(nc, io, cn, out)
    r = run_bass_kernel_spmd(nc, [arrays], core_ids=[0])
    return np.asarray(r.results[0]["out"])
```
